# Optimizing a Trainium2 kernel written in Bass

```python
import math
import jax
import jax.numpy as jnp
from jax import lax
import numpy as np

D_MODEL = 1024
BATCH = 1
SEQ = 512
DEPTH = 1

CTX_LEN = 256
GRID_W = 64
ROPE_BASE = 10000.0
NORM_EPS = 1e-6

DA_HEADS = 4
DA_QK_DIM = 64
DA_V_DIM = 2 * DA_QK_DIM
DA_WIDTH = DA_HEADS * DA_V_DIM
Q_BLOCK = 128

GLA_HEADS = 4
GLA_K_DIM = 64
GLA_V_DIM = 128
GLA_WIDTH = GLA_HEADS * GLA_V_DIM
GLA_GATE_RANK = 16
GLA_GATE_TAU = 16.0
GLA_CHUNK = 64

MIX_WIDTH = DA_WIDTH + GLA_WIDTH
IN_PROJ_SIZES = (DA_HEADS * 2 * DA_QK_DIM, DA_HEADS * 2 * DA_QK_DIM, DA_WIDTH,
                 GLA_HEADS * GLA_K_DIM, GLA_HEADS * GLA_K_DIM, GLA_WIDTH, GLA_WIDTH,
                 GLA_GATE_RANK, GLA_GATE_RANK)
IN_PROJ_DIM = sum(IN_PROJ_SIZES)

N_GROUPS = 4
EXPERTS_PER_GROUP = 8
N_EXPERTS = N_GROUPS * EXPERTS_PER_GROUP
TOP_K = 2
EXPERT_HIDDEN = 512
DISPATCH_BLOCK = 128


def rms_norm(x, gain):
    xf = x.astype(jnp.float32)
    y = xf * lax.rsqrt(jnp.mean(xf * xf, axis=-1, keepdims=True) + NORM_EPS)
    return (y * gain.astype(jnp.float32)).astype(x.dtype)

def modulate(h, shift, scale):
    return h * (1 + scale) + shift

def split_in_proj(p):
    parts, start = [], 0
    for size in IN_PROJ_SIZES:
        parts.append(p[..., start:start + size])
        start += size
    return parts

def axial_rope_tables(rows, rot_dim):
    n_freq = rot_dim // 4
    r, col = jnp.meshgrid(jnp.arange(rows, dtype=jnp.float32),
                          jnp.arange(GRID_W, dtype=jnp.float32), indexing="ij")
    pos = jnp.stack([r.reshape(-1), col.reshape(-1)], axis=-1)
    inv_freq = jnp.power(ROPE_BASE, -jnp.arange(n_freq, dtype=jnp.float32) / n_freq)
    ang = pos[:, :, None] * inv_freq
    return jnp.cos(ang), jnp.sin(ang)

def apply_axial_rope(x, cos, sin):
    n_freq = cos.shape[-1]
    xr = x.reshape(x.shape[:-1] + (2, 2, n_freq))
    x1, x2 = xr[..., 0, :], xr[..., 1, :]
    cs, sn = cos.astype(x.dtype), sin.astype(x.dtype)
    out = jnp.stack([x1 * cs - x2 * sn, x2 * cs + x1 * sn], axis=-2)
    return out.reshape(x.shape)

def diff_attend(q, k, v, lam):
    s = jnp.einsum("bqhmd,bkhmd->bhmqk", q, k).astype(jnp.float32) * (DA_QK_DIM ** -0.5)
    p = jax.nn.softmax(s, axis=-1)
    a = p[:, :, 0] - lam * p[:, :, 1]
    return jnp.einsum("bhqk,bkhe->bqhe", a.astype(v.dtype), v)

def gla_chunked(q, k, v, log_a, s0):
    B, T, H, dk = q.shape
    dv = v.shape[-1]
    n_chunks = T // GLA_CHUNK

    def chunks(t):
        return jnp.moveaxis(t.reshape(B, n_chunks, GLA_CHUNK, H, t.shape[-1]), 1, 0)

    mask = jnp.tril(jnp.ones((GLA_CHUNK, GLA_CHUNK), dtype=bool))

    def step(state, inp):
        qi, ki, vi, gi = inp
        b = jnp.cumsum(gi.astype(jnp.float32), axis=1)
        b_last = b[:, -1]
        q_dec = qi * jnp.exp(b)
        k_inv = ki * jnp.exp(-b)
        scores = jnp.einsum("bihk,bjhk->bhij", q_dec, k_inv)
        scores = jnp.where(mask, scores, 0.0)
        o = (jnp.einsum("bhij,bjhv->bihv", scores, vi)
             + jnp.einsum("bihk,bhkv->bihv", q_dec, state))
        k_to_end = ki * jnp.exp(b_last[:, None] - b)
        new_state = (state * jnp.exp(b_last)[..., None]
                     + jnp.einsum("bjhk,bjhv->bhkv", k_to_end, vi))
        return new_state, o

    s_final, o = lax.scan(step, s0, (chunks(q), chunks(k), chunks(v), chunks(log_a)))
    o = jnp.moveaxis(o, 0, 1).reshape(B, T, H, dv)
    return o, s_final

def log_gate(lowrank, w2, b):
    return jax.nn.log_sigmoid((lowrank @ w2 + b).astype(jnp.float32)) / GLA_GATE_TAU

def token_mixer(h_lat, h_ctx, cos, sin, lambda_init, w_in, da_lambda, da_subln_g,
                gla_gate_w2, gla_gate_b, gla_norm_g, w_out, with_ctx_out):
    B, S, _ = h_lat.shape
    L = h_ctx.shape[1]
    dt = h_lat.dtype
    dq_l, dk_l, dv_l, gq_l, gk_l, gv_l, gr_l, lrf_l, lrb_l = split_in_proj(h_lat @ w_in)
    dq_c, dk_c, dv_c, gq_c, gk_c, gv_c, gr_c, lrf_c, lrb_c = split_in_proj(h_ctx @ w_in)

    cos_b, sin_b = cos[:, None, None], sin[:, None, None]
    q_l = apply_axial_rope(dq_l.reshape(B, S, DA_HEADS, 2, DA_QK_DIM), cos_b, sin_b)
    k_l = apply_axial_rope(dk_l.reshape(B, S, DA_HEADS, 2, DA_QK_DIM), cos_b, sin_b)
    v_l = dv_l.reshape(B, S, DA_HEADS, DA_V_DIM)
    k_c = dk_c.reshape(B, L, DA_HEADS, 2, DA_QK_DIM)
    v_c = dv_c.reshape(B, L, DA_HEADS, DA_V_DIM)
    lam_p = da_lambda.astype(jnp.float32)
    lam = (jnp.exp(jnp.sum(lam_p[0] * lam_p[1])) - jnp.exp(jnp.sum(lam_p[2] * lam_p[3]))
           + lambda_init)
    k_all = jnp.concatenate([k_c, k_l], axis=1)
    v_all = jnp.concatenate([v_c, v_l], axis=1)
    qb = jnp.moveaxis(q_l.reshape(B, S // Q_BLOCK, Q_BLOCK, DA_HEADS, 2, DA_QK_DIM), 1, 0)
    a_l = lax.map(lambda qi: diff_attend(qi, k_all, v_all, lam), qb)
    a_l = jnp.moveaxis(a_l, 0, 1).reshape(B, S, DA_HEADS, DA_V_DIM)
    a_l = rms_norm(a_l, da_subln_g) * (1.0 - lambda_init)

    def gla_inputs(gq, gk, gv, lrf, lrb, n):
        q = gq.reshape(B, n, GLA_HEADS, GLA_K_DIM) * (GLA_K_DIM ** -0.5)
        k = gk.reshape(B, n, GLA_HEADS, GLA_K_DIM)
        v = gv.reshape(B, n, GLA_HEADS, GLA_V_DIM)
        g_f = log_gate(lrf, gla_gate_w2[0], gla_gate_b[0]).reshape(B, n, GLA_HEADS, GLA_K_DIM)
        g_b = log_gate(lrb, gla_gate_w2[1], gla_gate_b[1]).reshape(B, n, GLA_HEADS, GLA_K_DIM)
        return q, k, v, g_f, g_b

    gql, gkl, gvl, gfl, gbl = gla_inputs(gq_l, gk_l, gv_l, lrf_l, lrb_l, S)
    gqc, gkc, gvc, gfc, gbc = gla_inputs(gq_c, gk_c, gv_c, lrf_c, lrb_c, L)
    flip = lambda t: jnp.flip(t, axis=1)
    s0 = jnp.zeros((B, GLA_HEADS, GLA_K_DIM, GLA_V_DIM), jnp.float32)
    o_cf, s_cf = gla_chunked(gqc, gkc, gvc, gfc, s0)
    o_cb, s_cb = gla_chunked(flip(gqc), flip(gkc), flip(gvc), flip(gbc), s0)
    o_lf, _ = gla_chunked(gql, gkl, gvl, gfl, s_cf)
    o_lb, _ = gla_chunked(flip(gql), flip(gkl), flip(gvl), flip(gbl), s_cb)
    o_l = (o_lf + flip(o_lb)).astype(dt)
    g_l = rms_norm(o_l, gla_norm_g) * jax.nn.silu(gr_l.reshape(B, S, GLA_HEADS, GLA_V_DIM))

    y_lat = jnp.concatenate([a_l.reshape(B, S, DA_WIDTH), g_l.reshape(B, S, GLA_WIDTH)], -1) @ w_out
    if not with_ctx_out:
        return y_lat, None

    q_c = dq_c.reshape(B, L, DA_HEADS, 2, DA_QK_DIM)
    a_c = rms_norm(diff_attend(q_c, k_c, v_c, lam), da_subln_g) * (1.0 - lambda_init)
    o_c = (o_cf + flip(o_cb)).astype(dt)
    g_c = rms_norm(o_c, gla_norm_g) * jax.nn.silu(gr_c.reshape(B, L, GLA_HEADS, GLA_V_DIM))
    y_ctx = jnp.concatenate([a_c.reshape(B, L, DA_WIDTH), g_c.reshape(B, L, GLA_WIDTH)], -1) @ w_out
    return y_lat, y_ctx

def hier_moe(h, w_rg, b_rg, w_re, b_re, w_gate, w_up, w_down):
    T, D = h.shape
    hf = h.astype(jnp.float32)
    g_logits = hf @ w_rg.astype(jnp.float32) + b_rg.astype(jnp.float32)
    g_prob = jax.nn.softmax(g_logits, axis=-1)
    g_sel = jnp.argmax(g_logits, axis=-1)
    g_w = jnp.take_along_axis(g_prob, g_sel[:, None], axis=-1)
    e_logits = (hf @ w_re.astype(jnp.float32) + b_re.astype(jnp.float32)).reshape(
        T, N_GROUPS, EXPERTS_PER_GROUP)
    e_in_group = jnp.take_along_axis(e_logits, g_sel[:, None, None], axis=1)[:, 0]
    top_v, top_i = lax.top_k(e_in_group, TOP_K)
    weights = jax.nn.softmax(top_v, axis=-1) * g_w
    expert_id = (g_sel[:, None] * EXPERTS_PER_GROUP + top_i).astype(jnp.int32)

    tk = T * TOP_K
    n_blocks = -(-(tk + N_EXPERTS * (DISPATCH_BLOCK - 1)) // DISPATCH_BLOCK)
    n_rows = n_blocks * DISPATCH_BLOCK
    flat_e = expert_id.reshape(-1)
    flat_t = jnp.repeat(jnp.arange(T, dtype=jnp.int32), TOP_K)
    flat_w = weights.reshape(-1)
    order = jnp.argsort(flat_e)
    e_sorted = flat_e[order]
    counts = jnp.bincount(flat_e, length=N_EXPERTS)
    starts = jnp.cumsum(counts) - counts
    padded = ((counts + DISPATCH_BLOCK - 1) // DISPATCH_BLOCK) * DISPATCH_BLOCK
    pad_ends = jnp.cumsum(padded)
    pad_starts = pad_ends - padded
    dest = pad_starts[e_sorted] + (jnp.arange(tk) - starts[e_sorted])
    row_tok = jnp.full((n_rows,), T, jnp.int32).at[dest].set(flat_t[order])
    row_w = jnp.zeros((n_rows,), jnp.float32).at[dest].set(flat_w[order])
    block_start = jnp.arange(n_blocks, dtype=jnp.int32) * DISPATCH_BLOCK
    block_e = jnp.minimum(jnp.searchsorted(pad_ends, block_start, side="right"), N_EXPERTS - 1)
    h_pad = jnp.concatenate([h, jnp.zeros((1, D), h.dtype)], axis=0)
    xb = h_pad[row_tok].reshape(n_blocks, DISPATCH_BLOCK, D)

    def expert_block(args):
        xi, e = args
        return (jax.nn.silu(xi @ w_gate[e]) * (xi @ w_up[e])) @ w_down[e]

    yb = lax.map(expert_block, (xb, block_e)).reshape(n_rows, D)
    y = jax.ops.segment_sum(yb * row_w[:, None].astype(yb.dtype), row_tok, num_segments=T + 1)
    return y[:T]

def first_inputs(seed: int = 0) -> dict:
    key = jax.random.key(seed)
    ks = jax.random.split(key, 24)
    f32 = jnp.float32
    D = D_MODEL
    nrm = lambda k, shape, s: jax.random.normal(k, shape, f32) * s
    gain = lambda k, shape: 1.0 + 0.02 * jax.random.normal(k, shape, f32)
    return {
        "x": nrm(ks[0], (BATCH, SEQ, D), 1.0),
        "c": nrm(ks[1], (BATCH, D), 1.0),
        "ctx": nrm(ks[2], (BATCH, CTX_LEN, D), 1.0),
        "c_ctx": nrm(ks[3], (D,), 1.0),
        "w_ada": nrm(ks[4], (DEPTH, D, 6 * D), 0.5 * D ** -0.5),
        "b_ada": nrm(ks[5], (DEPTH, 6 * D), 0.02),
        "norm_mix_g": gain(ks[6], (DEPTH, D)),
        "norm_ffn_g": gain(ks[7], (DEPTH, D)),
        "w_in": nrm(ks[8], (DEPTH, D, IN_PROJ_DIM), D ** -0.5),
        "da_lambda": nrm(ks[9], (DEPTH, 4, DA_QK_DIM), 0.1),
        "da_subln_g": gain(ks[10], (DEPTH, DA_V_DIM)),
        "gla_gate_w2": nrm(ks[11], (DEPTH, 2, GLA_GATE_RANK, GLA_HEADS * GLA_K_DIM), GLA_GATE_RANK ** -0.5),
        "gla_gate_b": nrm(ks[12], (DEPTH, 2, GLA_HEADS * GLA_K_DIM), 0.1),
        "gla_norm_g": gain(ks[13], (DEPTH, GLA_V_DIM)),
        "w_out": nrm(ks[14], (DEPTH, MIX_WIDTH, D), MIX_WIDTH ** -0.5),
        "router_group_w": nrm(ks[15], (DEPTH, D, N_GROUPS), D ** -0.5),
        "router_group_b": nrm(ks[16], (DEPTH, N_GROUPS), 0.01),
        "router_expert_w": nrm(ks[17], (DEPTH, D, N_EXPERTS), D ** -0.5),
        "router_expert_b": nrm(ks[18], (DEPTH, N_EXPERTS), 0.01),
        "expert_w_gate": nrm(ks[19], (DEPTH, N_EXPERTS, D, EXPERT_HIDDEN), D ** -0.5),
        "expert_w_up": nrm(ks[20], (DEPTH, N_EXPERTS, D, EXPERT_HIDDEN), D ** -0.5),
        "expert_w_down": nrm(ks[21], (DEPTH, N_EXPERTS, EXPERT_HIDDEN, D), EXPERT_HIDDEN ** -0.5),
        "final_norm_g": gain(ks[22], (D,)),
    }

def first_block(x, c, ctx, c_ctx, w_ada, b_ada, norm_mix_g, norm_ffn_g, w_in, da_lambda,
              da_subln_g, gla_gate_w2, gla_gate_b, gla_norm_g, w_out, router_group_w,
              router_group_b, router_expert_w, router_expert_b, expert_w_gate, expert_w_up,
              expert_w_down, final_norm_g):
    B, S, D = x.shape
    L = ctx.shape[1]
    rows = S // GRID_W
    cos, sin = axial_rope_tables(rows, DA_QK_DIM)
    for layer in range(DEPTH):
        last = layer == DEPTH - 1
        lambda_init = 0.8 - 0.6 * math.exp(-0.3 * layer)
        mod_lat = (jax.nn.silu(c) @ w_ada[layer] + b_ada[layer])[:, None, :]
        mod_ctx = jax.nn.silu(c_ctx) @ w_ada[layer] + b_ada[layer]
        sh1, sc1, gt1, sh2, sc2, gt2 = jnp.split(mod_lat, 6, axis=-1)
        csh1, csc1, cgt1, csh2, csc2, cgt2 = jnp.split(mod_ctx, 6, axis=-1)

        h_lat = modulate(rms_norm(x, norm_mix_g[layer]), sh1, sc1)
        h_ctx = modulate(rms_norm(ctx, norm_mix_g[layer]), csh1, csc1)
        y_lat, y_ctx = token_mixer(h_lat, h_ctx, cos, sin, lambda_init, w_in[layer],
                                   da_lambda[layer], da_subln_g[layer], gla_gate_w2[layer],
                                   gla_gate_b[layer], gla_norm_g[layer], w_out[layer],
                                   with_ctx_out=not last)
        x = x + gt1 * y_lat

        moe_args = (router_group_w[layer], router_group_b[layer], router_expert_w[layer],
                    router_expert_b[layer], expert_w_gate[layer], expert_w_up[layer],
                    expert_w_down[layer])
        h2 = modulate(rms_norm(x, norm_ffn_g[layer]), sh2, sc2)
        x = x + gt2 * hier_moe(h2.reshape(B * S, D), *moe_args).reshape(B, S, D)
        if not last:
            ctx = ctx + cgt1 * y_ctx
            hc2 = modulate(rms_norm(ctx, norm_ffn_g[layer]), csh2, csc2)
            ctx = ctx + cgt2 * hier_moe(hc2.reshape(B * L, D), *moe_args).reshape(B, L, D)
    return rms_norm(x, final_norm_g)


DEPTH_2 = 2

D_FF = 2816
FFN_RES_SCALE = 0.5

A_HEADS = 8
A_HEAD_DIM = 64
A_PATTERNS = ((128, 1), (512, 4), (2048, 16))
A_BLOCK = 128

B_HEADS = 4
B_HEAD_DIM = 128
B_CONV = 4
B_CHUNK = 64

C_D_INNER = 2 * D_MODEL
C_HEAD_DIM = 64
C_HEADS = C_D_INNER // C_HEAD_DIM
C_GROUPS = 4
C_STATE = 128
C_CONV = 4
C_CHUNK = 64

A_WIDTH = A_HEADS * A_HEAD_DIM
B_WIDTH = B_HEADS * B_HEAD_DIM
EVEN_IN = 3 * A_WIDTH + 4 * B_WIDTH + 2 * B_HEADS
C_XBC = C_D_INNER + 2 * C_GROUPS * C_STATE
ODD_IN = C_D_INNER + C_XBC + C_HEADS
N_EVEN = (DEPTH_2 + 1) // 2
N_ODD = DEPTH_2 // 2


def rmsnorm(x, w):
    xf = x.astype(jnp.float32)
    y = xf * lax.rsqrt(jnp.mean(xf * xf, axis=-1, keepdims=True) + NORM_EPS)
    return (y * w.astype(jnp.float32)).astype(x.dtype)

def l2norm(x):
    return x * lax.rsqrt(jnp.sum(x * x, axis=-1, keepdims=True) + NORM_EPS)

def swiglu(x, w_gate, w_up, w_down):
    return (jax.nn.silu(x @ w_gate) * (x @ w_up)) @ w_down

def causal_dwconv(x, w):
    k_len, ch = w.shape
    return lax.conv_general_dilated(x, w[:, None, :].astype(x.dtype), window_strides=(1,),
                                    padding=((k_len - 1, 0),), dimension_numbers=('NWC', 'WIO', 'NWC'),
                                    feature_group_count=ch)

def dilated_window_attention(q, k, v):
    bsz, seq, heads, dh = q.shape
    scale = dh ** -0.5
    nums, maxes, dens = [], [], []
    for window, dil in A_PATTERNS:
        span = window // dil
        length = seq // dil
        blk = math.gcd(length, A_BLOCK)
        nb = length // blk

        def by_residue(t):
            return t.reshape(bsz, length, dil, heads, dh).transpose(0, 2, 1, 3, 4)

        pad = ((0, 0), (0, 0), (span, 0), (0, 0), (0, 0))
        kp = jnp.pad(by_residue(k), pad)
        vp = jnp.pad(by_residue(v), pad)
        idx = jnp.arange(nb)[:, None] * blk + jnp.arange(blk + span)[None, :]
        kb = kp[:, :, idx]
        vb = vp[:, :, idx]
        qb = by_residue(q).reshape(bsz, dil, nb, blk, heads, dh)
        s = jnp.einsum('brnqhd,brnkhd->brnhqk', qb, kb) * scale
        dist = jnp.arange(blk)[:, None] + span - jnp.arange(blk + span)[None, :]
        valid = ((dist >= 0) & (dist <= span))[None] & (idx >= span)[:, None, :]
        s = jnp.where(valid[:, None], s, -jnp.inf)
        m = jnp.max(s, axis=-1, keepdims=True)
        p = jnp.exp(s - m)
        den = jnp.sum(p, axis=-1)
        num = jnp.einsum('brnhqk,brnkhd->brnqhd', p, vb)

        def back(t):
            t = t.reshape(bsz, dil, length, *t.shape[4:])
            return jnp.moveaxis(t, 1, 2).reshape(bsz, seq, *t.shape[3:])

        nums.append(back(num))
        maxes.append(back(jnp.swapaxes(m[..., 0], -1, -2)))
        dens.append(back(jnp.swapaxes(den, -1, -2)))
    mx = jnp.max(jnp.stack(maxes), axis=0)
    wts = [jnp.exp(mi - mx) for mi in maxes]
    num = sum(n * w[..., None] for n, w in zip(nums, wts))
    den = sum(d * w for d, w in zip(dens, wts))
    return num / den[..., None]

def gated_delta_rule(q, k, v, g, beta):
    bsz, seq, heads, dk = q.shape
    dv = v.shape[-1]
    nc = seq // B_CHUNK

    def chunks(t):
        t = t.reshape(bsz, nc, B_CHUNK, heads, *t.shape[3:])
        return jnp.swapaxes(t, 2, 3)

    qc, kc, vc = chunks(q * dk ** -0.5), chunks(k), chunks(v)
    gc = jnp.cumsum(chunks(g), axis=-1)
    bc = chunks(beta)[..., None]
    tri = jnp.tril(jnp.ones((B_CHUNK, B_CHUNK), bool))
    strict = jnp.tril(jnp.ones((B_CHUNK, B_CHUNK), bool), -1)
    decay = jnp.exp(jnp.where(tri, gc[..., :, None] - gc[..., None, :], -jnp.inf))
    k_beta = kc * bc
    a_mat = jnp.where(strict, jnp.einsum('bnhid,bnhjd->bnhij', k_beta, kc) * decay, 0.0)
    t_mat = a_mat + jnp.eye(B_CHUNK, dtype=a_mat.dtype)
    u = lax.linalg.triangular_solve(t_mat, vc * bc, left_side=True, lower=True, unit_diagonal=True)
    w = lax.linalg.triangular_solve(t_mat, k_beta * jnp.exp(gc)[..., None], left_side=True, lower=True,
                                    unit_diagonal=True)
    qk = jnp.where(tri, jnp.einsum('bnhid,bnhjd->bnhij', qc, kc) * decay, 0.0)
    q_dec = qc * jnp.exp(gc)[..., None]
    g_last = gc[..., -1]
    k_dec = kc * jnp.exp(g_last[..., None] - gc)[..., None]

    def step(state, inp):
        u_i, w_i, q_i, qk_i, k_i, gl_i = inp
        v_new = u_i - jnp.einsum('bhck,bhkv->bhcv', w_i, state)
        o_i = jnp.einsum('bhck,bhkv->bhcv', q_i, state) + jnp.einsum('bhij,bhjv->bhiv', qk_i, v_new)
        state = state * jnp.exp(gl_i)[..., None, None] + jnp.einsum('bhck,bhcv->bhkv', k_i, v_new)
        return state, o_i

    xs = tuple(jnp.moveaxis(t, 1, 0) for t in (u, w, q_dec, qk, k_dec, g_last))
    state0 = jnp.zeros((bsz, heads, dk, dv), q.dtype)
    _, o = lax.scan(step, state0, xs)
    return jnp.transpose(o, (1, 0, 3, 2, 4)).reshape(bsz, seq, heads, dv)

def ssd_chunked_scan(x, a, b_in, c_in):
    bsz, seq, heads, p = x.shape
    groups, n = b_in.shape[2:]
    rep = heads // groups
    nc = seq // C_CHUNK
    xc = x.reshape(bsz, nc, C_CHUNK, groups, rep, p)
    acum = jnp.cumsum(a.reshape(bsz, nc, C_CHUNK, groups, rep), axis=2)
    bc = b_in.reshape(bsz, nc, C_CHUNK, groups, n)
    cc = c_in.reshape(bsz, nc, C_CHUNK, groups, n)
    tri = jnp.tril(jnp.ones((C_CHUNK, C_CHUNK), bool))[:, :, None, None]
    seg = jnp.exp(jnp.where(tri, acum[:, :, :, None] - acum[:, :, None, :], -jnp.inf))
    cb = jnp.einsum('bnlgd,bnsgd->bnlsg', cc, bc)
    y_diag = jnp.einsum('bnlsgr,bnsgrp->bnlgrp', cb[..., None] * seg, xc)

    def step(state, inp):
        x_i, a_i, b_i, c_i = inp
        y_off = jnp.einsum('blgd,bgrpd,blgr->blgrp', c_i, state, jnp.exp(a_i))
        a_last = a_i[:, -1]
        state = state * jnp.exp(a_last)[..., None, None] + jnp.einsum(
            'bsgd,bsgr,bsgrp->bgrpd', b_i, jnp.exp(a_last[:, None] - a_i), x_i)
        return state, y_off

    xs = tuple(jnp.moveaxis(t, 1, 0) for t in (xc, acum, bc, cc))
    state0 = jnp.zeros((bsz, groups, rep, p, n), x.dtype)
    _, y_off = lax.scan(step, state0, xs)
    return (y_diag + jnp.moveaxis(y_off, 0, 1)).reshape(bsz, seq, heads, p)

def even_mixer(u, w_in, conv_w, a_log, dt_bias, head_norm_w, w_out):
    bsz, seq, _ = u.shape
    proj = (u @ w_in).astype(jnp.float32)
    cuts = [int(c) for c in np.cumsum([A_WIDTH, A_WIDTH, A_WIDTH, 3 * B_WIDTH, B_WIDTH, B_HEADS])]
    qa, ka, va, qkv_b, z, beta_raw, a_raw = jnp.split(proj, cuts, axis=-1)
    qa, ka, va = (t.reshape(bsz, seq, A_HEADS, A_HEAD_DIM) for t in (qa, ka, va))
    o_a = dilated_window_attention(qa, ka, va)
    qkv_b = jax.nn.silu(causal_dwconv(qkv_b, conv_w))
    qb, kb, vb = (t.reshape(bsz, seq, B_HEADS, B_HEAD_DIM) for t in jnp.split(qkv_b, 3, axis=-1))
    beta = jax.nn.sigmoid(beta_raw)
    g = -jnp.exp(a_log) * jax.nn.softplus(a_raw + dt_bias)
    o_b = gated_delta_rule(l2norm(qb), l2norm(kb), vb, g, beta)
    o_b = rmsnorm(o_b, head_norm_w) * jax.nn.silu(z.reshape(bsz, seq, B_HEADS, B_HEAD_DIM))
    o = jnp.concatenate([o_a.reshape(bsz, seq, A_WIDTH), o_b.reshape(bsz, seq, B_WIDTH)], axis=-1)
    return (o @ w_out).astype(u.dtype)

def odd_mixer(u, w_in, conv_w, conv_b, dt_bias, a_log, d_skip, out_norm_w, w_out):
    bsz, seq, _ = u.shape
    proj = (u @ w_in).astype(jnp.float32)
    z, xbc, dt = jnp.split(proj, [C_D_INNER, C_D_INNER + C_XBC], axis=-1)
    xbc = jax.nn.silu(causal_dwconv(xbc, conv_w) + conv_b)
    xs, b_in, c_in = jnp.split(xbc, [C_D_INNER, C_D_INNER + C_GROUPS * C_STATE], axis=-1)
    xs = xs.reshape(bsz, seq, C_HEADS, C_HEAD_DIM)
    b_in = b_in.reshape(bsz, seq, C_GROUPS, C_STATE)
    c_in = c_in.reshape(bsz, seq, C_GROUPS, C_STATE)
    dt = jax.nn.softplus(dt + dt_bias)
    a = -jnp.exp(a_log) * dt
    y = ssd_chunked_scan(xs * dt[..., None], a, b_in, c_in) + d_skip[:, None] * xs
    y = y.reshape(bsz, seq, C_D_INNER) * jax.nn.silu(z)
    y = rmsnorm(y.reshape(bsz, seq, C_GROUPS, C_D_INNER // C_GROUPS), out_norm_w.reshape(C_GROUPS, -1))
    return (y.reshape(bsz, seq, C_D_INNER) @ w_out).astype(u.dtype)

def _dt_bias(key, shape):
    dt = jnp.exp(jax.random.uniform(key, shape, jnp.float32, math.log(1e-3), math.log(1e-1)))
    return dt + jnp.log(-jnp.expm1(-dt))

def second_inputs(seed: int = 0) -> dict:
    key = jax.random.key(seed)
    ks = iter(jax.random.split(key, 24))

    def nrm(shape, scale):
        return scale * jax.random.normal(next(ks), shape, jnp.float32)

    x = nrm((BATCH, SEQ, D_MODEL), 1.0)
    norm_w = 1.0 + nrm((DEPTH_2, 6, D_MODEL), 0.05)
    ffn_w_gate = nrm((DEPTH_2, 2, D_MODEL, D_FF), D_MODEL ** -0.5)
    ffn_w_up = nrm((DEPTH_2, 2, D_MODEL, D_FF), D_MODEL ** -0.5)
    ffn_w_down = nrm((DEPTH_2, 2, D_FF, D_MODEL), D_FF ** -0.5)
    even_w_in = nrm((N_EVEN, D_MODEL, EVEN_IN), D_MODEL ** -0.5)
    even_conv_w = nrm((N_EVEN, B_CONV, 3 * B_WIDTH), B_CONV ** -0.5)
    even_a_log = jnp.log(jax.random.uniform(next(ks), (N_EVEN, B_HEADS), jnp.float32, 1.0, 16.0))
    even_dt_bias = _dt_bias(next(ks), (N_EVEN, B_HEADS))
    even_head_norm_w = 1.0 + nrm((N_EVEN, B_HEAD_DIM), 0.05)
    even_w_out = nrm((N_EVEN, A_WIDTH + B_WIDTH, D_MODEL), (A_WIDTH + B_WIDTH) ** -0.5)
    odd_w_in = nrm((N_ODD, D_MODEL, ODD_IN), D_MODEL ** -0.5)
    odd_conv_w = nrm((N_ODD, C_CONV, C_XBC), C_CONV ** -0.5)
    odd_conv_b = nrm((N_ODD, C_XBC), 0.02)
    odd_dt_bias = _dt_bias(next(ks), (N_ODD, C_HEADS))
    odd_a_log = jnp.log(jax.random.uniform(next(ks), (N_ODD, C_HEADS), jnp.float32, 1.0, 16.0))
    odd_d_skip = 1.0 + nrm((N_ODD, C_HEADS), 0.05)
    odd_out_norm_w = 1.0 + nrm((N_ODD, C_D_INNER), 0.05)
    odd_w_out = nrm((N_ODD, C_D_INNER, D_MODEL), C_D_INNER ** -0.5)
    return {'x': x, 'norm_w': norm_w, 'ffn_w_gate': ffn_w_gate, 'ffn_w_up': ffn_w_up,
            'ffn_w_down': ffn_w_down, 'even_w_in': even_w_in, 'even_conv_w': even_conv_w,
            'even_a_log': even_a_log, 'even_dt_bias': even_dt_bias, 'even_head_norm_w': even_head_norm_w,
            'even_w_out': even_w_out, 'odd_w_in': odd_w_in, 'odd_conv_w': odd_conv_w,
            'odd_conv_b': odd_conv_b, 'odd_dt_bias': odd_dt_bias, 'odd_a_log': odd_a_log,
            'odd_d_skip': odd_d_skip, 'odd_out_norm_w': odd_out_norm_w, 'odd_w_out': odd_w_out}

def second_block(x, norm_w, ffn_w_gate, ffn_w_up, ffn_w_down, even_w_in, even_conv_w, even_a_log,
              even_dt_bias, even_head_norm_w, even_w_out, odd_w_in, odd_conv_w, odd_conv_b, odd_dt_bias,
              odd_a_log, odd_d_skip, odd_out_norm_w, odd_w_out):
    h = x
    for layer in range(DEPTH_2):
        nw = norm_w[layer]
        i = layer // 2
        f = swiglu(rmsnorm(h, nw[0]), ffn_w_gate[layer, 0], ffn_w_up[layer, 0], ffn_w_down[layer, 0])
        h = h + FFN_RES_SCALE * rmsnorm(f, nw[1])
        u = rmsnorm(h, nw[2])
        if layer % 2 == 0:
            m = even_mixer(u, even_w_in[i], even_conv_w[i], even_a_log[i], even_dt_bias[i],
                           even_head_norm_w[i], even_w_out[i])
        else:
            m = odd_mixer(u, odd_w_in[i], odd_conv_w[i], odd_conv_b[i], odd_dt_bias[i], odd_a_log[i],
                          odd_d_skip[i], odd_out_norm_w[i], odd_w_out[i])
        h = h + rmsnorm(m, nw[3])
        f = swiglu(rmsnorm(h, nw[4]), ffn_w_gate[layer, 1], ffn_w_up[layer, 1], ffn_w_down[layer, 1])
        h = h + FFN_RES_SCALE * rmsnorm(f, nw[5])
    return h


def setup_inputs(seed=0):
    out = dict(first_inputs(seed))
    for name, value in second_inputs(seed + 1).items():
        if name != "x":
            out[name + "_2"] = value
    return out


def reference(
    x, c, ctx, c_ctx, w_ada, b_ada, norm_mix_g, norm_ffn_g, w_in, da_lambda, da_subln_g,
    gla_gate_w2, gla_gate_b, gla_norm_g, w_out, router_group_w, router_group_b, router_expert_w,
    router_expert_b, expert_w_gate, expert_w_up, expert_w_down, final_norm_g, norm_w_2,
    ffn_w_gate_2, ffn_w_up_2, ffn_w_down_2, even_w_in_2, even_conv_w_2, even_a_log_2,
    even_dt_bias_2, even_head_norm_w_2, even_w_out_2, odd_w_in_2, odd_conv_w_2, odd_conv_b_2,
    odd_dt_bias_2, odd_a_log_2, odd_d_skip_2, odd_out_norm_w_2, odd_w_out_2,
):
    x = first_block(
        x, c, ctx, c_ctx, w_ada, b_ada, norm_mix_g, norm_ffn_g, w_in, da_lambda, da_subln_g,
        gla_gate_w2, gla_gate_b, gla_norm_g, w_out, router_group_w, router_group_b,
        router_expert_w, router_expert_b, expert_w_gate, expert_w_up, expert_w_down,
        final_norm_g,
    )
    return second_block(
        x, norm_w_2, ffn_w_gate_2, ffn_w_up_2, ffn_w_down_2, even_w_in_2, even_conv_w_2,
        even_a_log_2, even_dt_bias_2, even_head_norm_w_2, even_w_out_2, odd_w_in_2,
        odd_conv_w_2, odd_conv_b_2, odd_dt_bias_2, odd_a_log_2, odd_d_skip_2, odd_out_norm_w_2,
        odd_w_out_2,
    )


_drawn_inputs = setup_inputs


def setup_inputs(seed=0):
    import zlib

    import numpy as np

    out = dict(_drawn_inputs(seed))
    spreads = {}
    factors = {'norm_mix_g': 3.892,
     'da_lambda': 6.947,
     'da_subln_g': 36.155,
     'gla_gate_b': 3.247,
     'gla_norm_g': 8.0,
     'router_group_b': 44.168,
     'router_expert_b': 29.824,
     'odd_conv_b_2': 3.826,
     'odd_d_skip_2': 9.578,
     'norm_ffn_g': 8.0}
    for name, (base, spread) in spreads.items():
        noise = np.random.default_rng([zlib.crc32(name.encode()), seed]).standard_normal(out[name].shape)
        drawn = base * np.exp(spread * noise) if base else spread * noise
        out[name] = jnp.asarray(drawn.astype(out[name].dtype))
    for name, factor in factors.items():
        out[name] = (out[name] * factor).astype(out[name].dtype)
    return out
```

```python
from contextlib import ExitStack

import numpy as np

import concourse.bass as bass
from concourse import mybir
from concourse.alu_op_type import AluOpType as ALU

F32 = mybir.dt.float32
F32R = mybir.dt.float32r
I32 = mybir.dt.int32
U32 = mybir.dt.uint32
ACT = mybir.ActivationFunctionType
AX = mybir.AxisListType
P = 128
BANK = 512
EPS = 1e-6

D = 1024
KD = D // P
SEQ = 512
CTX = 256
NT = SEQ // P
NC = CTX // P
ALL = NT + NC
CHUNK = 64
NEG = -1e30


class Stage(ExitStack):

    def __init__(self, nc, name):
        super().__init__()
        self.nc, self.name, self.sems = nc, name, []

    def sb(self, name, shape, dt=F32):
        return self.enter_context(self.nc.sbuf_tensor(f"{self.name}_{name}", shape, dt))

    def sem(self, name):
        sem = self.enter_context(self.nc.semaphore(f"{self.name}_{name}"))
        self.sems.append(sem.num)
        return sem

    def block(self):
        return self.enter_context(self.nc.Block())

    def __exit__(self, *error):
        done = super().__exit__(*error)
        low = high = None
        for n in sorted(self.sems) + [None]:
            if n is not None and high is not None and n == high + 1:
                high = n
                continue
            if low is not None:
                self.nc.gpsimd.sem_clear(range(low, high + 1))
            low = high = n
        return done


def in_order(eng, sem):
    count = [0]

    def link(ins):
        count[0] += 1
        ins.then_inc(sem, 1)
        eng.wait_ge(sem, count[0])

    return link


def constants():
    p = np.arange(P)[:, None]
    f = np.arange(P)[None, :]
    same = (p // CHUNK) == (f // CHUNK)
    parts = {
        "ident": p == f,
        "tri_fwd": same & (p <= f),
        "tri_bwd": same & (p >= f),
        "before": p < f,
        "ones": np.ones((P, P)),
        "same_chunk": same,
        "strict": same & (p < f),
    }
    for n in range(1, 7):
        s = 2**n
        parts[f"merge{n}"] = (p // s == f // s) & (p % s < s // 2) & (f % s >= s // 2)
    parts["add_incl"] = np.where(same & (p <= f), 0.0, NEG)
    blocks = []
    for back in (3, 2, 1, 0):
        dist = p - f + P * back
        times = ((dist >= 0) & (dist <= 128)).astype(int)
        for dil in (4, 16):
            times = times + ((dist >= 0) & (dist % dil == 0) & (dist <= 128 * dil))
        blocks.append(np.where(times > 0, np.log(np.maximum(times, 1)), NEG))
    parts["windows"] = np.concatenate(blocks, axis=1)
    tok = np.arange(SEQ)
    pos = np.stack([tok // 64, tok % 64], axis=-1).astype(np.float32)
    inv = np.power(np.float32(10000.0), -np.arange(16, dtype=np.float32) / np.float32(16))
    ang = (pos[:, :, None] * inv).astype(np.float32).reshape(SEQ, 32)
    rope = np.concatenate([np.cos(ang), np.sin(ang)], axis=1)
    parts["rope"] = rope.reshape(NT, P, 64).transpose(1, 0, 2).reshape(P, NT * 64)
    parts["iota"] = np.broadcast_to(np.arange(64.0)[None, :], (P, 64))
    at, cols, data = {}, 0, []
    for name, a in parts.items():
        a = np.ascontiguousarray(a, dtype=np.float32)
        at[name] = (cols, a.shape[1])
        cols += a.shape[1]
        data.append(a)
    return np.concatenate(data, axis=1), at


CONST_DATA, CONST_AT = constants()


class Core:

    def __init__(self, nc, args, es):
        self.nc, self.a = nc, args
        self.table = es.enter_context(nc.sbuf_tensor("const_table", [P, CONST_DATA.shape[1]], F32))
        self.x = es.enter_context(nc.sbuf_tensor("x_tokens", [P, NT, D], F32))
        self.ps = es.enter_context(nc.psum_tensor("psum_banks", [P, 8, BANK], F32))
        self.scattered = es.enter_context(nc.semaphore("rows_scattered"))
        self.gathered = es.enter_context(nc.semaphore("rows_gathered"))

    def c(self, name):
        at, n = CONST_AT[name]
        return self.table[:, at:at + n]

    def scratch(self, name, shape, dt=F32):
        return self.nc.dram_tensor(name, shape, dt, kind="Internal").ap()


def load_all(k, name, loads):
    with Stage(k.nc, name) as s:
        loaded = s.sem("loaded")
        block = s.block()

        @block.sync
        def _(sp):
            for dst, src in loads:
                sp.dma_start(dst, src, allow_slow_non_contiguous=True).then_inc(loaded, 16)
            sp.wait_ge(loaded, 16 * len(loads))


def columns(row, n=KD):
    return row.rearrange("(k p) -> p k", p=P)


def modulation(k, mod_rows):
    nc, a = k.nc, k.a
    n_chunks = 6 * D // BANK
    with Stage(nc, "mod") as s:
        cond = s.sb("cond", [P, KD, 2])
        act = s.sb("act", [P, KD, 2])
        bias = s.sb("bias", [2, 6 * D])
        row = s.sb("row", [2, 6 * D])
        w = s.sb("w", [P, 3, KD, BANK])
        cond_in, w_in = s.sem("cond_in"), [s.sem(f"w_in{j}") for j in range(3)]
        act_ok, mm, bank_free, out = s.sem("act"), s.sem("mm"), s.sem("bank_free"), s.sem("out")
        block = s.block()
        wv = a["w_ada"][0].rearrange("(k p) n -> p k n", p=P)

        @block.sync
        def _(sp):
            sp.dma_start(cond[:, :, 0], columns(a["c"][0]), allow_slow_non_contiguous=True).then_inc(cond_in, 16)
            sp.dma_start(cond[:, :, 1], columns(a["c_ctx"]), allow_slow_non_contiguous=True).then_inc(cond_in, 16)
            for r in range(2):
                sp.dma_start(bias[r:r + 1, :], a["b_ada"]).then_inc(cond_in, 16)
            for n in range(3):
                sp.dma_start(w[:, n], wv[:, :, n * BANK:(n + 1) * BANK]).then_inc(w_in[n], 16)
            with sp.Fori(1, n_chunks // 3) as i:
                for j in range(3):
                    sp.wait_ge(mm, i * 3 + (j - 2))
                    sp.dma_start(w[:, j], wv[:, :, bass.ds((i * 3 + j) * BANK, BANK)]).then_inc(w_in[j], 16)
            sp.wait_ge(bank_free, 2 + n_chunks)
            sp.dma_start(mod_rows, row[:]).then_inc(out, 16)
            sp.wait_ge(out, 16)

        @block.scalar
        def _(eng):
            eng.wait_ge(cond_in, 64)
            nc.scalar.activation(act[:], cond[:], ACT.Silu).then_inc(act_ok, 1)

        @block.tensor
        def _(pe):
            pe.wait_ge(act_ok, 1)
            with pe.Fori(0, n_chunks // 3) as i:
                for j in range(3):
                    pe.wait_ge(w_in[j], (i + 1) * 16)
                    pe.wait_ge(bank_free, i * 3 + j + 1)
                    b = k.ps[0:2, j, :]
                    for t in range(KD):
                        last = nc.tensor.matmul(b, act[:, t, :], w[:, j, t, :], start=t == 0, stop=t == KD - 1)
                    last.then_inc(mm, 1)

        @block.vector
        def _(v):
            v.wait_ge(cond_in, 64)
            v.sem_inc(bank_free, 2)
            with v.Fori(0, n_chunks // 3) as i:
                for j in range(3):
                    v.wait_ge(mm, i * 3 + j + 1)
                    cols = bass.ds((i * 3 + j) * BANK, BANK)
                    nc.vector.tensor_tensor(row[:, cols], k.ps[0:2, j, :], bias[:, cols], ALU.add).then_inc(bank_free, 1)


def norm_rows(k, name, groups, width, eps=EPS):
    nc = k.nc
    n = len(groups)
    with Stage(nc, name) as s:
        junk = s.sb("junk", [P, 2, width])
        ss = s.sb("ss", [P, n])
        rs = s.sb("rs", [P, n])
        squares, root, chain = s.sem("squares"), s.sem("root"), s.sem("chain")
        block = s.block()

        @block.scalar
        def _(eng):
            for g, (src, _) in enumerate(groups):
                if g > 1:
                    eng.wait_ge(squares, g - 1)
                nc.scalar.activation(junk[:, g % 2, :], src, ACT.Square, accum_out=ss[:, g:g + 1]).then_inc(squares, 1)
            eng.wait_ge(chain, 1)
            nc.scalar.activation(rs[:], ss[:], ACT.Sqrt).then_inc(root, 1)
            eng.wait_ge(chain, 2)
            for g in range(1, n, 2):
                nc.scalar.activation(groups[g][1], groups[g][0], ACT.Copy, scale=rs[:, g:g + 1])

        @block.vector
        def _(v):
            link = in_order(v, chain)
            v.wait_ge(squares, n)
            link(nc.vector.tensor_scalar(ss[:], ss[:], 1.0 / width, eps, ALU.mult, ALU.add))
            v.wait_ge(root, 1)
            link(nc.vector.reciprocal(rs[:], rs[:]))
            for g in range(0, n, 2):
                nc.vector.tensor_scalar(groups[g][1], groups[g][0], rs[:, g:g + 1], None, ALU.mult)


class Split:

    def __init__(self, high, low):
        self.high, self.low = high, low

    def __getitem__(self, at):
        return Split(self.high[at], self.low[at])


def split_sb(stack, nc, name, shape):
    return Split(*(stack.enter_context(nc.sbuf_tensor(f"{name}_{part}", shape, F32R)) for part in ("high", "low")))


def product(nc, out, lhs, rhs, start, stop):
    nc.tensor.matmul(out, lhs.high, rhs.high, start=start, stop=False, skip_group_check=True)
    nc.tensor.matmul(out, lhs.high, rhs.low, start=False, stop=False, skip_group_check=True)
    return nc.tensor.matmul(out, lhs.low, rhs.high, start=False, stop=stop, skip_group_check=True)


def turn(k, name, jobs, tiles):
    nc = k.nc
    cols = tiles * P
    split = isinstance(jobs[0][1], Split)
    with Stage(nc, name) as s:
        turned, out_v, out_s = s.sem("turned"), s.sem("out_v"), s.sem("out_s")
        whole_ok = s.sem("whole_ok")
        whole = s.sb("whole", [P, 2, cols]) if split and jobs[0][3] is not None else None
        block = s.block()

        @block.tensor
        def _(pe):
            for i, (sources, _, _, _) in enumerate(jobs):
                if i >= 8:
                    if split:
                        pe.wait_ge(out_v, i - 7)
                    else:
                        pe.wait_ge(out_s if i % 2 else out_v, (i - 8) // 2 + 1)
                for t in range(tiles):
                    src = sources[t]
                    last = nc.tensor.transpose(k.ps[:, i % 8, t * P:(t + 1) * P], src, k.c("ident"))
                last.then_inc(turned, 1)

        @block.vector
        def _(v):
            for i in range(0, len(jobs), 1 if split else 2):
                _, dst, gain, shift = jobs[i]
                bank = k.ps[:, i % 8, 0:cols]
                if split:
                    v.wait_ge(out_s, i + 1)
                    high = dst.high.bitcast(F32)
                    if shift is not None:
                        nc.vector.tensor_scalar(whole[:, i % 2, :], bank, gain, shift, ALU.mult, ALU.add).then_inc(whole_ok, 1)
                        v.wait_ge(whole_ok, i + 1)
                        nc.vector.tensor_tensor(dst.low, whole[:, i % 2, :], high, ALU.subtract).then_inc(out_v, 1)
                    elif gain is not None:
                        nc.vector.scalar_tensor_tensor(out=dst.low, in0=bank, scalar=gain, in1=high, op0=ALU.mult,
                                                       op1=ALU.subtract).then_inc(out_v, 1)
                    else:
                        nc.vector.tensor_tensor(dst.low, bank, high, ALU.subtract).then_inc(out_v, 1)
                    continue
                v.wait_ge(turned, i + 1)
                if gain is None:
                    nc.vector.tensor_copy(dst, bank).then_inc(out_v, 1)
                elif shift is None:
                    nc.vector.tensor_scalar(dst, bank, gain, None, ALU.mult).then_inc(out_v, 1)
                else:
                    nc.vector.tensor_scalar(dst, bank, gain, shift, ALU.mult, ALU.add).then_inc(out_v, 1)

        @block.scalar
        def _(eng):
            for i in range(0 if split else 1, len(jobs), 1 if split else 2):
                _, dst, gain, shift = jobs[i]
                eng.wait_ge(turned, i + 1)
                nc.scalar.activation(dst.high if split else dst, k.ps[:, i % 8, 0:cols], ACT.Identity,
                                     bias=0.0 if shift is None else shift,
                                     scale=1.0 if gain is None else gain).then_inc(out_s, 1)


def project_tokens(k, name, x_t, tiles, w_dram, first, chunks, dst, k_tiles=KD):
    nc = k.nc
    wv = w_dram.rearrange("(k p) n -> p k n", p=P)
    half = tiles // 2
    slots = 2 if chunks % 2 == 0 else 1
    with Stage(nc, name) as s:
        w = s.sb("w", [P, slots, k_tiles, BANK])
        w_in = [s.sem(f"w_in{j}") for j in range(slots)]
        mm, free_v, free_s = s.sem("mm"), s.sem("bank_free_v"), s.sem("bank_free_s")
        block = s.block()

        @block.sync
        def _(sp):
            for j in range(slots):
                sp.dma_start(w[:, j], wv[:, :, first + j * BANK:first + (j + 1) * BANK]).then_inc(w_in[j], 16)
            if chunks > slots:
                with sp.Fori(1, chunks // slots) as i:
                    for j in range(slots):
                        sp.wait_ge(mm, (i * slots + (j - slots + 1)) * tiles)
                        sp.dma_start(w[:, j], wv[:, :, bass.ds((i * slots + j) * BANK + first, BANK)]).then_inc(w_in[j], 16)

        @block.tensor
        def _(pe):
            with pe.Fori(0, chunks // slots) as i:
                for j in range(slots):
                    pe.wait_ge(w_in[j], (i + 1) * 16)
                    for t in range(tiles):
                        pe.wait_ge(free_s if t % 2 else free_v, (i * slots + j) * half + (t // 2 + 1))
                        for q in range(k_tiles):
                            last = nc.tensor.matmul(k.ps[:, t, :], x_t[:, q, t * P:(t + 1) * P], w[:, j, q, :],
                                                    start=q == 0, stop=q == k_tiles - 1)
                        last.then_inc(mm, 1)

        def copies(eng, free, odd):
            eng.sem_inc(free, half)
            with eng.Fori(0, chunks // slots) as i:
                for j in range(slots):
                    for t in range(odd, tiles, 2):
                        eng.wait_ge(mm, (i * slots + j) * tiles + (t + 1))
                        to = dst[:, t, bass.ds((i * slots + j) * BANK, BANK)]
                        if odd:
                            nc.scalar.activation(to, k.ps[:, t, :], ACT.Copy).then_inc(free, 1)
                        else:
                            nc.vector.tensor_copy(to, k.ps[:, t, :]).then_inc(free, 1)

        @block.vector
        def _(v):
            copies(v, free_v, 0)

        @block.scalar
        def _(eng):
            copies(eng, free_s, 1)


def project_features(k, name, x_t, spans, w_dram, first, chunks, dst):
    nc = k.nc
    wv = w_dram.rearrange("(k p) n -> p k n", p=P)
    per = BANK // P
    units = [(m, at, n) for m in range(per) for at, n in spans]
    U = len(units)
    assert U <= 8 and U % 2 == 0
    with Stage(nc, name) as s:
        slots = 2 if chunks % 2 == 0 else 1
        w = s.sb("w", [P, slots, KD, BANK])
        w_in = [s.sem(f"w_in{j}") for j in range(slots)]
        mm, free_v, free_s = s.sem("mm"), s.sem("bank_free_v"), s.sem("bank_free_s")
        block = s.block()

        @block.sync
        def _(sp):
            for j in range(slots):
                sp.dma_start(w[:, j], wv[:, :, first + j * BANK:first + (j + 1) * BANK]).then_inc(w_in[j], 16)
            if chunks > slots:
                with sp.Fori(1, chunks // slots) as i:
                    for j in range(slots):
                        sp.wait_ge(mm, (i * slots + (j - slots + 1)) * U)
                        sp.dma_start(w[:, j], wv[:, :, bass.ds((i * slots + j) * BANK + first, BANK)]).then_inc(w_in[j], 16)

        @block.tensor
        def _(pe):
            with pe.Fori(0, chunks // slots) as i:
                for j in range(slots):
                    pe.wait_ge(w_in[j], (i + 1) * 16)
                    for u, (m, at, n) in enumerate(units):
                        pe.wait_ge(free_s if u % 2 else free_v, (i * slots + j) * (U // 2) + (u // 2 + 1))
                        for q in range(KD):
                            last = nc.tensor.matmul(k.ps[:, u, 0:n], w[:, j, q, m * P:(m + 1) * P], x_t[:, q, at:at + n],
                                                    start=q == 0, stop=q == KD - 1)
                        last.then_inc(mm, 1)

        def copies(eng, free, odd):
            eng.sem_inc(free, U // 2)
            with eng.Fori(0, chunks // slots) as i:
                for j in range(slots):
                    for u in range(odd, U, 2):
                        m, at, n = units[u]
                        eng.wait_ge(mm, (i * slots + j) * U + (u + 1))
                        to = dst[:, bass.ds((i * slots + j) * per + m, 1), at:at + n].rearrange("p a n -> p (a n)")
                        if odd:
                            nc.scalar.activation(to, k.ps[:, u, 0:n], ACT.Copy).then_inc(free, 1)
                        else:
                            nc.vector.tensor_copy(to, k.ps[:, u, 0:n]).then_inc(free, 1)

        @block.vector
        def _(v):
            copies(v, free_v, 0)

        @block.scalar
        def _(eng):
            copies(eng, free_s, 1)


CHUNK_COLS = 256


def project(k, name, x, w_dram, first, cols, units, dest, k_tiles=KD):
    nc = k.nc
    wv = w_dram.rearrange("(k p) n -> p k n", p=P)
    chunks = cols // CHUNK_COLS
    pairs = chunks // 2
    U = len(units)
    half = U // 2
    assert chunks % 2 == 0 and U % 2 == 0 and U <= 8
    with Stage(nc, name) as s:
        raw = s.sb("w", [P, k_tiles, CHUNK_COLS])
        w = split_sb(s, nc, f"{name}_w", [P, 2, k_tiles, CHUNK_COLS])
        w_in, high_ok, low_ok, mm = s.sem("w_in"), s.sem("high_ok"), s.sem("low_ok"), s.sem("mm")
        free_v, free_s = s.sem("bank_free_v"), s.sem("bank_free_s")
        block = s.block()

        def width(u):
            return CHUNK_COLS if units[u][0] == "tokens" else units[u][3]

        @block.sync
        def _(sp):
            sp.dma_start(raw[:], wv[:, :, first:first + CHUNK_COLS]).then_inc(w_in, 16)
            with sp.Fori(1, chunks) as c:
                sp.wait_ge(low_ok, c)
                sp.dma_start(raw[:], wv[:, :, bass.ds(c * CHUNK_COLS + first, CHUNK_COLS)]).then_inc(w_in, 16)

        @block.tensor
        def _(pe):
            with pe.Fori(0, pairs) as i:
                for j in range(2):
                    c = i * 2 + j
                    pe.wait_ge(low_ok, c + 1)
                    for u, unit in enumerate(units):
                        pe.wait_ge(free_s if u % 2 else free_v, c * half + (u // 2 + 1))
                        out = k.ps[:, u, 0:width(u)]
                        for q in range(k_tiles):
                            if unit[0] == "tokens":
                                a, b = x[:, q, unit[1] * P:(unit[1] + 1) * P], w[:, j, q, :]
                            else:
                                _, m, at, n = unit
                                a, b = w[:, j, q, m * P:(m + 1) * P], x[:, q, at:at + n]
                            last = product(nc, out, a, b, q == 0, q == k_tiles - 1)
                        last.then_inc(mm, 1)

        def copies(eng, c, odd):
            for u in range(odd, U, 2):
                eng.wait_ge(mm, c * U + (u + 1))
                if odd:
                    nc.scalar.activation(dest(c, units[u]), k.ps[:, u, 0:width(u)], ACT.Copy).then_inc(free_s, 1)
                else:
                    nc.vector.tensor_copy(dest(c, units[u]), k.ps[:, u, 0:width(u)]).then_inc(free_v, 1)

        def run(eng, odd, part):
            eng.sem_inc(free_s if odd else free_v, half)
            part(0, 0, True)
            with eng.Fori(0, pairs - 1) as i:
                for j in range(2):
                    part(i * 2 + (j + 1), 1 - j, False)
                    copies(eng, i * 2 + j, odd)
            part(chunks - 1, 1, False)
            copies(eng, chunks - 2, odd)
            copies(eng, chunks - 1, odd)

        @block.scalar
        def _(eng):
            def high(c, j, start):
                eng.wait_ge(w_in, (c + 1) * 16)
                if not start:
                    eng.wait_ge(mm, (c - 1) * U if not isinstance(c, int) or c > 1 else U * 0 + 0) if False else None
                nc.scalar.activation(w.high[:, j], raw[:], ACT.Copy).then_inc(high_ok, 1)

            run(eng, 1, high)

        @block.vector
        def _(v):
            def low(c, j, start):
                v.wait_ge(high_ok, c + 1)
                nc.vector.tensor_tensor(w.low[:, j], raw[:], w.high[:, j].bitcast(F32), ALU.subtract).then_inc(low_ok, 1)

            run(v, 0, low)


def by_tokens(dst, at=0):
    return lambda c, unit: dst[:, unit[1], bass.ds(c * CHUNK_COLS + at, CHUNK_COLS)]


def token_units(tiles):
    return [("tokens", t) for t in range(tiles)]


def by_features(dst, at=0):
    per = CHUNK_COLS // P
    return lambda c, unit: dst[:, bass.ds(c * per + unit[1] + at, 1), unit[2]:unit[2] + unit[3]].rearrange("p a n -> p (a n)")


def feature_units(spans):
    return [("features", m, at, n) for m in range(CHUNK_COLS // P) for at, n in spans]



DA_H, DA_QK, DA_V = 4, 64, 128
GLA_H, GLA_K, GLA_V, RANK = 4, 64, 128, 16
GLA_QK = GLA_H * GLA_K
TAU = 16.0
KEYS = SEQ + CTX
N_CH = KEYS // CHUNK
CTX_CH = CTX // CHUNK


def gates(k, h_t, w_in, w2, gate_b, g):
    nc = k.nc
    first = 3 * 512 + 2 * GLA_QK + 2 * 512
    with Stage(nc, "gates") as s:
        w = s.sb("w", [P, KD, 2 * RANK])
        w2b = s.sb("w2b", [2 * RANK + 1, 2 * GLA_QK])
        low = s.sb("low", [2 * RANK + 1, KEYS])
        z = s.sb("z", [P, 2, 2 * GLA_QK])
        na = s.sb("na", [P, 2, 2 * GLA_QK])
        w_in_sem, cleared, mm, low_ok = s.sem("w_in"), s.sem("cleared"), s.sem("mm"), s.sem("low_ok")
        exped = s.sem("exped")
        zmm, zc, nab, lg, gd = s.sem("z_mm"), s.sem("z_copied"), s.sem("neg_abs"), s.sem("log"), s.sem("g_done")
        block = s.block()

        @block.sync
        def _(sp):
            sp.dma_start(w[:], w_in.rearrange("(k p) n -> p k n", p=P)[:, :, first:first + 2 * RANK]).then_inc(w_in_sem, 16)
            sp.wait_ge(cleared, 1)
            for d in range(2):
                cols = slice(d * GLA_QK, (d + 1) * GLA_QK)
                sp.dma_start(w2b[d * RANK:(d + 1) * RANK, cols], w2[d]).then_inc(w_in_sem, 16)
                sp.dma_start(w2b[2 * RANK:2 * RANK + 1, cols], gate_b[d:d + 1, :]).then_inc(w_in_sem, 16)

        @block.tensor
        def _(pe):
            pe.wait_ge(w_in_sem, 80)
            for b, (at, n) in enumerate(((0, 512), (512, 256))):
                for q in range(KD):
                    last = nc.tensor.matmul(k.ps[0:2 * RANK, b, 0:n], w[:, q, :], h_t[:, q, at:at + n],
                                            start=q == 0, stop=q == KD - 1)
                last.then_inc(mm, 1)
            pe.wait_ge(low_ok, 3)
            for t in range(ALL):
                if t >= 2:
                    pe.wait_ge(zc, t - 1)
                nc.tensor.matmul(k.ps[:, 2 + t % 2, :], low[:, t * P:(t + 1) * P], w2b[:], start=True, stop=True).then_inc(zmm, 1)

        @block.vector
        def _(v):
            nc.vector.memset(w2b[:], 0.0).then_inc(cleared, 1)
            nc.vector.memset(low[2 * RANK:2 * RANK + 1, :], 1.0).then_inc(low_ok, 1)
            for b, (at, n) in enumerate(((0, 512), (512, 256))):
                v.wait_ge(mm, b + 1)
                nc.vector.tensor_copy(low[0:2 * RANK, at:at + n], k.ps[0:2 * RANK, b, 0:n]).then_inc(low_ok, 1)
            for t in range(ALL + 1):
                if t < ALL:
                    j = t % 2
                    v.wait_ge(zc, t + 1)
                    if t >= 2:
                        v.wait_ge(lg, t - 1)
                    nc.vector.scalar_tensor_tensor(out=na[:, j, :], in0=z[:, j, :], scalar=-1.0, in1=z[:, j, :],
                                                   op0=ALU.mult, op1=ALU.min).then_inc(nab, 1)
                if t:
                    j = (t - 1) % 2
                    v.wait_ge(lg, t)
                    nc.vector.scalar_tensor_tensor(out=g[:, t - 1, :], in0=z[:, j, :], scalar=0.0, in1=na[:, j, :],
                                                   op0=ALU.min, op1=ALU.subtract).then_inc(gd, 1)

        @block.scalar
        def _(eng):
            for t in range(ALL + 1):
                if t < ALL:
                    j = t % 2
                    eng.wait_ge(zmm, t + 1)
                    if t >= 2:
                        eng.wait_ge(gd, t - 1)
                    nc.scalar.activation(z[:, j, :], k.ps[:, 2 + j, :], ACT.Copy).then_inc(zc, 1)
                if t:
                    j = (t - 1) % 2
                    eng.wait_ge(nab, t)
                    nc.scalar.activation(na[:, j, :], na[:, j, :], ACT.Exp).then_inc(exped, 1)
                    eng.wait_ge(exped, t)
                    nc.scalar.activation(na[:, j, :], na[:, j, :], ACT.Ln, bias=1.0).then_inc(lg, 1)


def gla_prepare(k, d, pair, g, qk_t, q_dec, k_inv, k_end_t, decay):
    nc = k.nc
    tri = k.c("tri_bwd" if d else "tri_fwd")
    end = 0 if d else CHUNK - 1
    with Stage(nc, f"gla_prep{d}{pair}") as s:
        b = s.sb("b", [P, KEYS])
        diff = s.sb("diff", [P, KEYS])
        e_q, e_k = s.sb("e_q", [P, SEQ]), s.sb("e_k", [P, SEQ])
        mm, bc, dd, ee, out = s.sem("mm"), s.sem("b_copied"), s.sem("diff_ok"), s.sem("exps"), s.sem("out")
        block = s.block()
        chunks = b[:].rearrange("p (c n) -> p c n", n=CHUNK)
        ends = chunks[:, :, end:end + 1]

        @block.tensor
        def _(pe):
            for t in range(ALL):
                at = 0 if t < NC else 1
                col = (t - (NC if at else 0)) * P
                last = nc.tensor.matmul(k.ps[:, at, col:col + P],
                                        g[:, t, d * GLA_QK + pair * P:d * GLA_QK + (pair + 1) * P], tri,
                                        start=True, stop=True)
            last.then_inc(mm, 1)

        @block.scalar
        def _(eng):
            eng.wait_ge(mm, 1)
            nc.scalar.activation(b[:, 0:CTX], k.ps[:, 0, 0:CTX], ACT.Copy, scale=1.0 / TAU).then_inc(bc, 1)
            nc.scalar.activation(b[:, CTX:KEYS], k.ps[:, 1, 0:SEQ], ACT.Copy, scale=1.0 / TAU).then_inc(bc, 1)
            eng.wait_ge(bc, 2)
            nc.scalar.activation(e_q[:], b[:, CTX:KEYS], ACT.Exp).then_inc(ee, 1)
            nc.scalar.activation(e_k[:], b[:, CTX:KEYS], ACT.Exp, scale=-1.0).then_inc(ee, 1)
            nc.scalar.activation(decay.unsqueeze(2), ends, ACT.Exp).then_inc(ee, 1)
            eng.wait_ge(dd, 1)
            nc.scalar.activation(diff[:], diff[:], ACT.Exp).then_inc(ee, 1)

        @block.vector
        def _(v):
            v.wait_ge(bc, 2)
            nc.vector.tensor_tensor(diff[:].rearrange("p (c n) -> p c n", n=CHUNK),
                                    ends.to_broadcast([P, N_CH, CHUNK]), chunks, ALU.subtract).then_inc(dd, 1)
            v.wait_ge(ee, 2)
            nc.vector.scalar_tensor_tensor(out=q_dec, in0=qk_t[:, pair, CTX:KEYS], scalar=GLA_K ** -0.5, in1=e_q[:],
                                           op0=ALU.mult, op1=ALU.mult).then_inc(out, 1)
            nc.vector.tensor_tensor(k_inv, qk_t[:, 2 + pair, CTX:KEYS], e_k[:], ALU.mult).then_inc(out, 1)
            v.wait_ge(ee, 4)
            nc.vector.tensor_tensor(k_end_t, qk_t[:, 2 + pair, :], diff[:], ALU.mult).then_inc(out, 1)


def gla_states(k, d, k_end, vals, decay, states):
    nc = k.nc
    order = scan_order(d)
    with Stage(nc, f"gla_state{d}") as s:
        mm, chain = s.sem("mm"), s.sem("chain")
        cleared = s.sem("cleared")
        block = s.block()

        @block.tensor
        def _(pe):
            for n, c in enumerate(order[:-1]):
                t, half = divmod(c, 2)
                rows = slice(half * CHUNK, (half + 1) * CHUNK)
                if n >= 8:
                    pe.wait_ge(chain, 2 * (n - 8) + 4)
                for pair in range(2):
                    for hh in range(2):
                        head = pair * 2 + hh
                        last = nc.tensor.matmul(k.ps[hh * GLA_K:(hh + 1) * GLA_K, n % 8, pair * P:(pair + 1) * P],
                                                k_end[pair][rows, t, hh * GLA_K:(hh + 1) * GLA_K],
                                                vals[rows, t, head * P:(head + 1) * P], start=True, stop=True)
                last.then_inc(mm, 1)

        @block.vector
        def _(v):
            for pair in range(2):
                nc.vector.memset(states[pair][:, 0, :], 0.0).then_inc(chain, 1)
            for n, c in enumerate(order[:-1]):
                v.wait_ge(mm, n + 1)
                v.wait_ge(chain, 2 * n + 2)
                for pair in range(2):
                    nc.vector.scalar_tensor_tensor(out=states[pair][:, n + 1, :], in0=states[pair][:, n, :],
                                                   scalar=decay[pair][:, c:c + 1], in1=k.ps[:, n % 8, pair * P:(pair + 1) * P],
                                                   op0=ALU.mult, op1=ALU.add).then_inc(chain, 1)


def scan_order(d):
    if d == 0:
        return list(range(N_CH))
    return list(range(CTX_CH))[::-1] + list(range(CTX_CH, N_CH))[::-1]


def gla_output(k, q_dec, k_inv, vals, states, out):
    nc = k.nc
    orders = [scan_order(d) for d in range(2)]
    with Stage(nc, "gla_out") as s:
        sc = s.sb("scores", [P, 2, GLA_H * P])
        score, masked, used, done, copied = s.sem("score"), s.sem("masked"), s.sem("used"), s.sem("done"), s.sem("copied")
        block = s.block()
        units = [(t, d) for t in range(NT) for d in range(2)]

        def region(first, h):
            return k.ps[:, first + h % 2, (h // 2) * P:(h // 2 + 1) * P]

        @block.tensor
        def _(pe):
            def scores(n):
                t, d = units[n]
                if n >= 2:
                    pe.wait_ge(masked, n - 1)
                for h in range(GLA_H):
                    rows = slice((h % 2) * GLA_K, (h % 2 + 1) * GLA_K)
                    last = nc.tensor.matmul(region(2 * (n % 2), h), k_inv[d][h // 2][rows, t * P:(t + 1) * P],
                                            q_dec[d][h // 2][rows, t * P:(t + 1) * P], start=True, stop=True)
                last.then_inc(score, 1)

            scores(0)
            for n, (t, d) in enumerate(units):
                if n + 1 < len(units):
                    scores(n + 1)
                pe.wait_ge(masked, n + 1)
                if t >= 2 and d == 0:
                    pe.wait_ge(copied, t - 1)
                for h in range(GLA_H):
                    rows = slice((h % 2) * GLA_K, (h % 2 + 1) * GLA_K)
                    o = region(4 + 2 * (t % 2), h)
                    at = (h % 2) * 2 * P + (h // 2) * P
                    nc.tensor.matmul(o, sc[:, n % 2, at:at + P], vals[:, NC + t, h * P:(h + 1) * P],
                                     start=d == 0 and h < 2, stop=False, skip_group_check=True)
                    for half in range(2):
                        c = 2 * t + half
                        last = nc.tensor.matmul(o[half * CHUNK:(half + 1) * CHUNK, :],
                                                q_dec[d][h // 2][rows, c * CHUNK:(c + 1) * CHUNK],
                                                states[d][h // 2][rows, orders[d].index(CTX_CH + c), :],
                                                start=False, stop=d == 1, skip_group_check=True)
                last.then_inc(used, 1)

        @block.vector
        def _(v):
            for n, (t, d) in enumerate(units):
                v.wait_ge(score, n + 1)
                if n >= 2:
                    v.wait_ge(used, n - 1)
                tri = k.c("tri_bwd" if d else "tri_fwd")
                nc.vector.tensor_tensor(sc[:, n % 2, :].rearrange("p (b h n) -> p b h n", b=2, h=2),
                                        k.ps[:, 2 * (n % 2):2 * (n % 2) + 2, 0:2 * P].rearrange("p b (h n) -> p b h n", h=2),
                                        tri.unsqueeze(1).unsqueeze(1).to_broadcast([P, 2, 2, P]), ALU.mult).then_inc(masked, 1)

        @block.scalar
        def _(eng):
            for t in range(NT):
                eng.wait_ge(used, 2 * t + 2)
                first = 4 + 2 * (t % 2)
                nc.scalar.activation(out(t).rearrange("p (h b n) -> p b h n", b=2, h=2),
                                     k.ps[:, first:first + 2, 0:2 * P].rearrange("p b (h n) -> p b h n", h=2),
                                     ACT.Copy).then_inc(copied, 1)


def rope(k, tiles):
    nc = k.nc
    table = k.c("rope").rearrange("p (t n) -> p t n", t=NT)
    with Stage(nc, "rope") as s:
        a, b = s.sb("a", [P, 2, 16, 2, 16]), s.sb("b", [P, 2, 16, 2, 16])
        done, added = s.sem("products"), s.sem("added")
        block = s.block()

        @block.vector
        def _(v):
            for t, (x, dst) in enumerate(tiles):
                j = t % 2
                xv = x.rearrange("p (g a h n) -> p g a h n", a=2, h=2, n=16)
                dv = dst.rearrange("p (g a h n) -> p g a h n", a=2, h=2, n=16)
                cos = table[:, t, 0:32].rearrange("p (a n) -> p a n", a=2).unsqueeze(1).to_broadcast([P, 16, 2, 16])
                sin = table[:, t, 32:64].rearrange("p (a n) -> p a n", a=2).unsqueeze(1).to_broadcast([P, 16, 2, 16])
                x1, x2 = xv[:, :, :, 0, :], xv[:, :, :, 1, :]
                for half, (u, w, op) in enumerate(((x1, x2, ALU.subtract), (x2, x1, ALU.add))):
                    n = 2 * t + half
                    if n >= 2:
                        v.wait_ge(added, n - 1)
                    nc.vector.tensor_tensor(a[:, half], u, cos, ALU.mult).then_inc(done, 1)
                    nc.vector.tensor_tensor(b[:, half], w, sin, ALU.mult).then_inc(done, 1)
                    v.wait_ge(done, 2 * n + 2)
                    nc.vector.tensor_tensor(dv[:, :, :, half, :], a[:, half], b[:, half], op).then_inc(added, 1)


def diff_attention(k, q_t, k_t, vals, lam_rows, lambda_init, out):
    nc = k.nc
    scale = DA_QK ** -0.5
    KT = KEYS // P
    units = [(h, t) for h in range(DA_H) for t in range(NT)]
    U = len(units)
    with Stage(nc, "diff_attn") as s:
        p = s.sb("p", [P, 2, 2, KEYS])
        a = s.sb("a", [P, 2, KEYS])
        at_ = s.sb("a_t", [P, 2, KEYS])
        mx = s.sb("mx", [P, 2 * U])
        den = s.sb("den", [P, 2 * U])
        lam = s.sb("lam", [P, 4])
        prod = s.sb("prod", [P, 2, DA_QK])
        small, lam_ok, lam_exp = s.sem("small"), s.sem("lam_sums"), s.sem("lam_exp")
        score, biased, soft = s.sem("score"), s.sem("bias"), s.sem("soft")
        comb, turned, a_in, pv, outc = s.sem("combined"), s.sem("turned"), s.sem("a_t_in"), s.sem("pv"), s.sem("out")
        block = s.block()

        @block.tensor
        def _(pe):
            def scores(u):
                h, t = units[u]
                for m in range(2):
                    n = 2 * u + m
                    if n >= 2:
                        pe.wait_ge(soft, n - 1)
                    rows = slice(m * DA_QK, (m + 1) * DA_QK)
                    for b, (at, w) in enumerate(((0, 512), (512, KEYS - 512))):
                        last = nc.tensor.matmul(k.ps[:, 2 * m + b, 0:w], q_t[rows, h, t * P:(t + 1) * P],
                                                k_t[rows, h, at:at + w], start=True, stop=True)
                    last.then_inc(score, 1)

            scores(0)
            for u, (h, t) in enumerate(units):
                if u + 1 < U:
                    scores(u + 1)
                pe.wait_ge(comb, u + 1)
                if u >= 1:
                    pe.wait_ge(a_in, u)
                for q in range(KT):
                    b, col = divmod(q, 4)
                    last = nc.tensor.transpose(k.ps[:, 4 + b, col * P:(col + 1) * P], a[:, u % 2, q * P:(q + 1) * P], k.c("ident"))
                last.then_inc(turned, 1)
                pe.wait_ge(a_in, u + 1)
                if u >= 2:
                    pe.wait_ge(outc, u - 1)
                for q in range(KT):
                    last = nc.tensor.matmul(k.ps[:, 6 + u % 2, 0:P], at_[:, u % 2, q * P:(q + 1) * P],
                                            vals[:, q, h * P:(h + 1) * P], start=q == 0, stop=q == KT - 1)
                last.then_inc(pv, 1)

        def banks(m):
            return k.ps[:, 2 * m:2 * m + 2, :].rearrange("p b n -> p (b n)")[:, 0:KEYS]

        @block.scalar
        def _(eng):
            eng.wait_ge(lam_ok, 2)
            nc.scalar.activation(lam[:, 2:4], lam[:, 0:2], ACT.Exp).then_inc(lam_exp, 1)
            for u in range(U + 1):
                if u < U:
                    for m in range(2):
                        n = 2 * u + m
                        eng.wait_ge(biased, n + 1)
                        if u >= 2:
                            eng.wait_ge(comb, u - 1)
                        nc.scalar.activation(p[:, u % 2, m, :], banks(m), ACT.Exp, bias=mx[:, n:n + 1], scale=scale,
                                             accum_out=den[:, n:n + 1]).then_inc(soft, 1)
                if u:
                    w = u - 1
                    eng.wait_ge(turned, w + 1)
                    if w >= 2:
                        eng.wait_ge(pv, w - 1)
                    nc.scalar.activation(at_[:, w % 2, :], k.ps[:, 4:6, :].rearrange("p b n -> p (b n)")[:, 0:KEYS],
                                         ACT.Copy).then_inc(a_in, 1)

        @block.vector
        def _(v):
            link = in_order(v, small)
            for i in range(2):
                link(nc.vector.tensor_tensor(prod[:, i, :], lam_rows[:, 2 * i, :], lam_rows[:, 2 * i + 1, :], ALU.mult))
            for i in range(2):
                nc.vector.tensor_reduce(lam[:, i:i + 1], prod[:, i, :], AX.X, ALU.add).then_inc(lam_ok, 1)
            v.wait_ge(lam_exp, 1)
            link(nc.vector.tensor_tensor(lam[:, 0:1], lam[:, 3:4], lam[:, 2:3], ALU.subtract))
            link(nc.vector.tensor_scalar(lam[:, 0:1], lam[:, 0:1], lambda_init, None, ALU.subtract))

            def maxima(u):
                for m in range(2):
                    n = 2 * u + m
                    v.wait_ge(score, n + 1)
                    link(nc.vector.tensor_reduce(mx[:, n:n + 1], banks(m), AX.X, ALU.max))
                    nc.vector.tensor_scalar(mx[:, n:n + 1], mx[:, n:n + 1], -scale, None, ALU.mult).then_inc(biased, 1)

            def copy_out(u):
                h, t = units[u]
                v.wait_ge(pv, u + 1)
                nc.vector.tensor_copy(out(t)[:, h * P:(h + 1) * P], k.ps[:, 6 + u % 2, 0:P]).then_inc(outc, 1)

            maxima(0)
            for u in range(U):
                if u + 1 < U:
                    maxima(u + 1)
                v.wait_ge(soft, 2 * u + 2)
                link(nc.vector.reciprocal(den[:, 2 * u:2 * u + 2], den[:, 2 * u:2 * u + 2]))
                link(nc.vector.tensor_tensor(den[:, 2 * u + 1:2 * u + 2], den[:, 2 * u + 1:2 * u + 2], lam[:, 0:1], ALU.mult))
                if u >= 2:
                    v.wait_ge(turned, u - 1)
                link(nc.vector.tensor_scalar(a[:, u % 2, :], p[:, u % 2, 0, :], den[:, 2 * u:2 * u + 1], None, ALU.mult))
                nc.vector.scalar_tensor_tensor(out=a[:, u % 2, :], in0=p[:, u % 2, 1, :], scalar=den[:, 2 * u + 1:2 * u + 2],
                                               in1=a[:, u % 2, :], op0=ALU.mult, op1=ALU.add).then_inc(comb, 1)
                if u:
                    copy_out(u - 1)
            copy_out(U - 1)


def norm_heads(k, name, x, groups, width, mult=None, eps=EPS):
    nc = k.nc
    with Stage(nc, name) as s:
        sq = s.sb("sq", [P, groups, width])
        ss, rs = s.sb("ss", [P, groups]), s.sb("rs", [P, groups])
        squared, chain, root = s.sem("squared"), s.sem("chain"), s.sem("root")
        block = s.block()

        @block.scalar
        def _(eng):
            nc.scalar.activation(sq[:], x, ACT.Square).then_inc(squared, 1)
            eng.wait_ge(chain, 2)
            nc.scalar.activation(rs[:], ss[:], ACT.Sqrt).then_inc(root, 1)

        @block.vector
        def _(v):
            link = in_order(v, chain)
            v.wait_ge(squared, 1)
            link(nc.vector.tensor_reduce(ss[:], sq[:], AX.X, ALU.add))
            link(nc.vector.tensor_scalar(ss[:], ss[:], 1.0 / width, eps, ALU.mult, ALU.add))
            v.wait_ge(root, 1)
            link(nc.vector.reciprocal(rs[:], rs[:]))
            link(nc.vector.tensor_tensor(x, x, rs[:].unsqueeze(2).to_broadcast([P, groups, width]), ALU.mult))
            for part, factor in mult or []:
                link(nc.vector.tensor_tensor(part, part, factor, ALU.mult))


def silu_rows(k, name, parts):
    nc = k.nc
    with Stage(nc, name) as s:
        done = s.sem("done")
        block = s.block()

        @block.scalar
        def _(eng):
            for x in parts:
                nc.scalar.activation(x, x, ACT.Silu).then_inc(done, 1)


def residual(k, name, y, gain, scaled=None):
    nc = k.nc
    with Stage(nc, name) as s:
        chain = s.sem("chain")
        block = s.block()

        @block.vector
        def _(v):
            link = in_order(v, chain)
            factor = gain.unsqueeze(1).to_broadcast([P, NT, D])
            if scaled is None:
                link(nc.vector.tensor_tensor(y, y, factor, ALU.mult))
            else:
                link(nc.vector.scalar_tensor_tensor(out=y, in0=y, scalar=scaled, in1=factor, op0=ALU.mult, op1=ALU.mult))
            link(nc.vector.tensor_tensor(k.x[:], k.x[:], y, ALU.add))


def first_mixer(k, es, mod_rows):
    nc, a = k.nc, k.a
    w_in = a["w_in"][0]
    q_dec = [[None] * 2 for _ in range(2)]
    outer = es.enter_context(ExitStack())

    def sb(stack, name, shape):
        return stack.enter_context(nc.sbuf_tensor(name, shape, F32))

    y = sb(outer, "mix", [P, NT, D])
    tok = sb(outer, "tok", [P, ALL, 5 * 512])
    qk_t = sb(outer, "gla_qk_t", [P, 4, KEYS])
    g = sb(outer, "log_gates", [P, ALL, 2 * GLA_QK])
    with ExitStack() as st:
        h_t = sb(st, "h_t", [P, KD, KEYS])
        cond = sb(st, "cond_cols", [P, 5, KD])
        with ExitStack() as st2:
            ctx = sb(st2, "ctx_rows", [P, NC, D])
            xn = sb(st2, "xn_all", [P, ALL, D])
            load_all(k, "ctx_in", [
                (ctx[:], a["ctx"][0].rearrange("(t p) d -> p t d", p=P)),
                (cond[:, 0, :], columns(a["norm_mix_g"][0])),
                (cond[:, 1, :], columns(mod_rows[0, 0:D])), (cond[:, 2, :], columns(mod_rows[0, D:2 * D])),
                (cond[:, 3, :], columns(mod_rows[1, 0:D])), (cond[:, 4, :], columns(mod_rows[1, D:2 * D]))])
            scale_gain(k, "cond", [(cond[:, 2, :], cond[:, 0, :]), (cond[:, 4, :], cond[:, 0, :])])
            norm_rows(k, "norm_mix", [(ctx[:, t, :], xn[:, t, :]) for t in range(NC)]
                      + [(k.x[:, t, :], xn[:, NC + t, :]) for t in range(NT)], D)
            turn(k, "turn_ctx", [([xn[:, t, i * P:(i + 1) * P] for t in range(NC)], h_t[:, i, 0:CTX],
                                  cond[:, 4, i:i + 1], cond[:, 3, i:i + 1]) for i in range(KD)], NC)
            turn(k, "turn_lat", [([xn[:, NC + t, i * P:(i + 1) * P] for t in range(NT)], h_t[:, i, CTX:KEYS],
                                  cond[:, 2, i:i + 1], cond[:, 1, i:i + 1]) for i in range(KD)], NT)
        project_tokens(k, "proj_q", h_t, ALL, w_in, 0, 2, tok)
        project_tokens(k, "proj_v", h_t, ALL, w_in, 2 * 512, 1, tok[:, :, 2 * 512:])
        project_tokens(k, "proj_gv", h_t, ALL, w_in, 3 * 512 + 2 * GLA_QK, 2, tok[:, :, 3 * 512:])
        project_features(k, "proj_gqk", h_t, [(0, 512), (512, 256)], w_in, 3 * 512, 1, qk_t)
        gates(k, h_t, w_in, a["gla_gate_w2"][0], a["gla_gate_b"][0], g)

    da_v = tok[:, :, 2 * 512:3 * 512]
    gla_v = tok[:, :, 3 * 512:4 * 512]
    with ExitStack() as st:
        q_t, k_t = sb(st, "q_t", [P, DA_H, SEQ]), sb(st, "k_t", [P, DA_H, KEYS])
        lam_rows = sb(st, "lam_rows", [P, 4, DA_QK])
        with ExitStack() as st2:
            rot = sb(st2, "rotated", [P, NT, 2 * 512])
            load_all(k, "lam_in", [(lam_rows[:], a["da_lambda"].to_broadcast([P, 4, DA_QK]))])
            rope(k, [(tok[:, NC + t, 0:1024], rot[:, t, :]) for t in range(NT)])
            turn(k, "turn_qk", [([rot[:, t, i * P:(i + 1) * P] for t in range(NT)],
                                 q_t[:, i, :] if i < 4 else k_t[:, i - 4, CTX:KEYS], None, None) for i in range(8)], NT)
            turn(k, "turn_kc", [([tok[:, t, (4 + i) * P:(5 + i) * P] for t in range(NC)],
                                 k_t[:, i, 0:CTX], None, None) for i in range(4)], NC)
        diff_attention(k, q_t, k_t, da_v, lam_rows, 0.8 - 0.6, lambda t: y[:, t, 0:512])

    with ExitStack() as st:
        q_dec, k_inv, k_end, states, decay = ([], [], [], [], [])
        for d in range(2):
            q_dec.append([sb(st, f"q_dec{d}{i}", [P, SEQ]) for i in range(2)])
            k_inv.append([sb(st, f"k_inv{d}{i}", [P, SEQ]) for i in range(2)])
            states.append([sb(st, f"states{d}{i}", [P, N_CH, GLA_V]) for i in range(2)])
        for d in range(2):
            with ExitStack() as st2:
                k_end = [sb(st2, f"k_end{d}{i}", [P, ALL, P]) for i in range(2)]
                decay = [sb(st2, f"decay{d}{i}", [P, N_CH]) for i in range(2)]
                k_end_t = [sb(st2, f"k_end_t{d}{i}", [P, KEYS]) for i in range(2)]
                for i in range(2):
                    gla_prepare(k, d, i, g, qk_t, q_dec[d][i][:], k_inv[d][i][:], k_end_t[i][:], decay[i][:])
                turn(k, f"turn_kend{d}", [([k_end_t[i][:, t * P:(t + 1) * P]], k_end[i][:, t, :], None, None)
                                          for i in range(2) for t in range(ALL)], 1)
                gla_states(k, d, k_end, gla_v, decay, states[d])
        gla_output(k, q_dec, k_inv, gla_v, states, lambda t: y[:, t, 512:1024])

    gate_r = tok[:, NC:ALL, 4 * 512:5 * 512]
    silu_rows(k, "silu_r", [gate_r])
    norm_heads(k, "norm_mix_heads", y[:].rearrange("p t (h n) -> p (t h) n", n=P), NT * 8, P,
               [(y[:, :, 512:1024], gate_r)])
    with ExitStack() as st:
        y_t = sb(st, "mix_t", [P, KD, SEQ])
        proj = sb(st, "mixed", [P, NT, D])
        gains = sb(st, "head_gains", [P, 2])
        gate = sb(st, "gate_rows", [P, D])
        load_all(k, "gains_in", [(gains[:, 0:1], a["da_subln_g"][0].rearrange("(p o) -> p o", o=1)),
                                 (gains[:, 1:2], a["gla_norm_g"][0].rearrange("(p o) -> p o", o=1)),
                                 (gate[:], mod_rows[0:1, 2 * D:3 * D].to_broadcast([P, D]))])
        scale_by(k, "lambda_gain", gains[:, 0:1], 1.0 - (0.8 - 0.6))
        turn(k, "turn_mix", [([y[:, t, i * P:(i + 1) * P] for t in range(NT)], y_t[:, i, :],
                              gains[:, 0:1] if i < 4 else gains[:, 1:2], None) for i in range(KD)], NT)
        project_tokens(k, "proj_out", y_t, NT, a["w_out"][0], 0, 2, proj)
        residual(k, "residual_mix", proj[:], gate[:])
    outer.close()


def scale_gain(k, name, pairs):
    nc = k.nc
    with Stage(nc, name) as s:
        done = s.sem("done")
        block = s.block()

        @block.vector
        def _(v):
            for scale, gain in pairs:
                nc.vector.scalar_tensor_tensor(out=scale, in0=scale, scalar=1.0, in1=gain, op0=ALU.add,
                                               op1=ALU.mult).then_inc(done, 1)


def scale_by(k, name, x, factor):
    nc = k.nc
    with Stage(nc, name) as s:
        done = s.sem("done")
        block = s.block()

        @block.vector
        def _(v):
            nc.vector.tensor_scalar(x, x, factor, None, ALU.mult).then_inc(done, 1)



GROUPS, PER_GROUP = 4, 8
N_E = GROUPS * PER_GROUP
TOP = 2
HID = 512
N_BLOCKS = N_E + (SEQ * TOP - N_E) // P
HT = HID // P


def clear_rows(k, name, rows_dram):
    nc = k.nc
    with Stage(nc, name) as s:
        per = 3
        z = s.sb("zeros", [P, per, D])
        ok, out = s.sem("ok"), s.sem("out")
        block = s.block()
        v3 = rows_dram.rearrange("(g t p) d -> g p t d", p=P, t=per)

        @block.vector
        def _(v):
            nc.vector.memset(z[:], 0.0).then_inc(ok, 1)

        @block.sync
        def _(sp):
            sp.wait_ge(ok, 1)
            for g in range(N_BLOCKS // per):
                sp.dma_start(v3[g], z[:]).then_inc(out, 16)
            sp.wait_ge(out, 16 * (N_BLOCKS // per))


def narrow_projection(k, name, h_t, w_rows, bias, n, out):
    nc = k.nc
    with Stage(nc, name) as s:
        lt = s.sb("logits_t", [n, SEQ])
        mm, lt_ok, turned = s.sem("mm"), s.sem("biased"), s.sem("turned")
        block = s.block()

        @block.tensor
        def _(pe):
            for q in range(KD):
                last = nc.tensor.matmul(k.ps[0:n, 0, :], w_rows[:, q, :], h_t[:, q, :], start=q == 0, stop=q == KD - 1)
            last.then_inc(mm, 1)
            pe.wait_ge(lt_ok, 1)
            for t in range(NT):
                last = nc.tensor.transpose(k.ps[:, 1, t * n:(t + 1) * n], lt[:, t * P:(t + 1) * P], k.c("ident")[0:n, 0:n])
            last.then_inc(turned, 1)

        @block.vector
        def _(v):
            v.wait_ge(mm, 1)
            nc.vector.tensor_scalar(lt[:], k.ps[0:n, 0, :], bias, None, ALU.add).then_inc(lt_ok, 1)
            v.wait_ge(turned, 1)
            nc.vector.tensor_copy(out, k.ps[:, 1, 0:NT * n].rearrange("p (t n) -> p t n", t=NT))


def route(k, logits, weights, dest, block_e):
    nc = k.nc
    with Stage(nc, "route") as s:
        def small(name, n, m):
            return s.sb(name, [P, n, m])

        gl, el = logits[:, :, 0:GROUPS], logits[:, :, GROUPS:]
        gm, gs, gi = small("gm", NT, 1), small("gs", NT, 1), small("gi", NT, 1)
        ge, gc, goh = small("ge", NT, GROUPS), small("gc", NT, GROUPS), small("goh", NT, GROUPS)
        em, cand, e2 = small("em", NT, N_E), small("cand", NT, N_E), small("e2", NT, N_E)
        tmp = small("tmp", NT, N_E)
        oh = [small(f"oh{i}", NT, N_E) for i in range(TOP)]
        top = [small(f"top{i}", NT, 1) for i in range(TOP)]
        both, pos = small("both", NT, N_E), small("pos", NT, N_E)
        tot = small("tot", NT, N_E)
        run = s.sb("run", [P, N_E])
        nb = s.sb("nb", [P, N_E])
        nb_i = s.sb("nb_i", [P, N_E], I32)
        ends = s.sb("ends", [P, 2, N_E])
        first = s.sb("first", [P, N_E])
        below = s.sb("below", [P, N_BLOCKS, N_E])
        bsum = s.sb("bsum", [P, N_BLOCKS])
        dest_f = s.sb("dest_f", [P, NT, TOP])
        chain, exps, mm = s.sem("chain"), s.sem("exps"), s.sem("mm")
        ready, both_ok = s.sem("ready"), s.sem("both_ok")
        block = s.block()

        @block.scalar
        def _(eng):
            eng.wait_ge(ready, 1)
            nc.scalar.activation(ge[:], ge[:], ACT.Exp).then_inc(exps, 1)
            eng.wait_ge(ready, 2)
            nc.scalar.activation(top[1][:], top[1][:], ACT.Exp).then_inc(exps, 1)

        @block.tensor
        def _(pe):
            pe.wait_ge(both_ok, 1)
            rhs = both[:].rearrange("p t e -> p (t e)")
            nc.tensor.matmul(k.ps[:, 0, 0:NT * N_E], k.c("before"), rhs, start=True, stop=True)
            nc.tensor.matmul(k.ps[:, 1, 0:NT * N_E], k.c("ones"), rhs, start=True, stop=True).then_inc(mm, 1)

        @block.vector
        def _(v):
            link = in_order(v, chain)
            V = nc.vector
            iota = k.c("iota")

            def first_of(values, best, out, width):
                c = gc if width == GROUPS else cand
                link(V.tensor_tensor(c[:], values, best.to_broadcast([P, NT, width]), ALU.is_equal))
                link(V.scalar_tensor_tensor(out=c[:], in0=c[:], scalar=-64.0,
                                            in1=iota[:, 0:width].unsqueeze(1).to_broadcast([P, NT, width]),
                                            op0=ALU.mult, op1=ALU.add))
                link(V.tensor_reduce(gi[:], c[:], AX.X, ALU.min))
                link(V.tensor_tensor(out, c[:], gi[:].to_broadcast([P, NT, width]), ALU.is_equal))

            link(V.tensor_reduce(gm[:], gl, AX.X, ALU.max))
            V.tensor_tensor(ge[:], gl, gm[:].to_broadcast([P, NT, GROUPS]), ALU.subtract).then_inc(ready, 1)
            first_of(gl, gm[:], goh[:], GROUPS)
            by_group = lambda x: x.rearrange("p t (g e) -> p t g e", g=GROUPS)
            chosen = goh[:].unsqueeze(3).to_broadcast([P, NT, GROUPS, PER_GROUP])
            link(V.tensor_tensor(by_group(em[:]), by_group(el), chosen, ALU.mult))
            link(V.tensor_scalar(gc[:], goh[:], 1.0, -NEG, ALU.subtract, ALU.mult))
            link(V.tensor_tensor(by_group(em[:]), by_group(em[:]),
                                 gc[:].unsqueeze(3).to_broadcast([P, NT, GROUPS, PER_GROUP]), ALU.add))
            link(V.tensor_reduce(top[0][:], em[:], AX.X, ALU.max))
            first_of(em[:], top[0][:], oh[0][:], N_E)
            link(V.scalar_tensor_tensor(out=e2[:], in0=oh[0][:], scalar=3 * NEG, in1=em[:], op0=ALU.mult, op1=ALU.add))
            link(V.tensor_reduce(top[1][:], e2[:], AX.X, ALU.max))
            first_of(e2[:], top[1][:], oh[1][:], N_E)
            V.tensor_tensor(both[:], oh[0][:], oh[1][:], ALU.add).then_inc(both_ok, 1)
            V.tensor_tensor(top[1][:], top[1][:], top[0][:], ALU.subtract).then_inc(ready, 1)
            v.wait_ge(exps, 2)
            link(V.tensor_reduce(gs[:], ge[:], AX.X, ALU.add))
            link(V.tensor_scalar(top[0][:], top[1][:], 1.0, None, ALU.add))
            link(V.tensor_tensor(gs[:], gs[:], top[0][:], ALU.mult))
            link(V.reciprocal(weights[:, :, 0:1], gs[:]))
            link(V.tensor_tensor(weights[:, :, 1:2], weights[:, :, 0:1], top[1][:], ALU.mult))
            v.wait_ge(mm, 1)
            flat = lambda x: x.rearrange("p t e -> p (t e)")
            link(V.tensor_copy(flat(pos[:]), k.ps[:, 0, 0:NT * N_E]))
            link(V.tensor_copy(flat(tot[:]), k.ps[:, 1, 0:NT * N_E]))
            link(V.tensor_copy(run[:], tot[:, 0, :]))
            for t in range(1, NT):
                link(V.tensor_tensor(pos[:, t, :], pos[:, t, :], run[:], ALU.add))
                link(V.tensor_tensor(run[:], run[:], tot[:, t, :], ALU.add))
            link(V.tensor_scalar(nb_i[:], run[:], float(P - 1), None, ALU.add))
            link(V.tensor_scalar(nb_i[:], nb_i[:], 7, None, ALU.arith_shift_right))
            link(V.tensor_copy(nb[:], nb_i[:]))
            link(V.tensor_copy(ends[:, 0, :], nb[:]))
            for n, step in enumerate((1, 2, 4, 8, 16)):
                a, b = ends[:, n % 2, :], ends[:, (n + 1) % 2, :]
                link(V.tensor_copy(b[:, 0:step], a[:, 0:step]))
                link(V.tensor_tensor(b[:, step:], a[:, step:], a[:, 0:N_E - step], ALU.add))
            end = ends[:, 1, :]
            link(V.tensor_tensor(first[:], end, nb[:], ALU.subtract))
            link(V.scalar_tensor_tensor(out=pos[:], in0=first[:].unsqueeze(1).to_broadcast([P, NT, N_E]), scalar=float(P),
                                        in1=pos[:], op0=ALU.mult, op1=ALU.add))
            for i in range(TOP):
                link(V.tensor_tensor(tmp[:], oh[i][:], pos[:], ALU.mult))
                link(V.tensor_reduce(dest_f[:, :, i:i + 1], tmp[:], AX.X, ALU.add))
            link(V.tensor_copy(dest, dest_f[:].rearrange("p t i -> p (t i)")))
            link(V.tensor_tensor(below[:], end.unsqueeze(1).to_broadcast([P, N_BLOCKS, N_E]),
                                 iota[:, 0:N_BLOCKS].unsqueeze(2).to_broadcast([P, N_BLOCKS, N_E]), ALU.is_le))
            link(V.tensor_reduce(bsum[:], below[:], AX.X, ALU.add))
            link(V.tensor_scalar(block_e[:, 0:N_BLOCKS], bsum[:], float(N_E - 1), None, ALU.min))
            link(V.tensor_copy(block_e[:, N_BLOCKS:], end[:, N_E - 1:]))


def scatter_rows(k, rows, dest, table):
    nc = k.nc
    with Stage(nc, "scatter") as s:
        out = k.scattered
        block = s.block()

        @block.gpsimd
        def _(pool):
            for t in range(NT):
                for i in range(TOP):
                    n = t * TOP + i
                    pool.indirect_dma_start(out=table, out_offset=bass.IndirectOffsetOnAxis(ap=dest[:, n:n + 1], axis=0),
                                            in_=rows[:, t, :], in_offset=None).then_inc(out, 16)
            pool.wait_ge(out, 16 * NT * TOP)


def gather_rows(k, rows, dest, table):
    nc = k.nc
    with Stage(nc, "gather") as s:
        loaded = k.gathered
        block = s.block()

        @block.gpsimd
        def _(pool):
            for n in range(NT * TOP):
                pool.indirect_dma_start(out=rows[:, n, :], out_offset=None, in_=table,
                                        in_offset=bass.IndirectOffsetOnAxis(ap=dest[:, n:n + 1], axis=0)).then_inc(loaded, 16)
            pool.wait_ge(loaded, 16 * NT * TOP)


def experts(k, name, start, count, used, table, block_e, w_gate, w_up, w_down):
    nc = k.nc
    pairs = (count - 1) // 2
    tail = list(range(2 * pairs, count))

    def if_used(eng):
        if used is None:
            return ExitStack()
        return eng.If(eng.value_load(used, min_val=0, max_val=N_BLOCKS) > start)

    wg = w_gate.rearrange("e (p k) n -> e p k n", k=KD)
    wu = w_up.rearrange("e (p k) n -> e p k n", k=KD)
    wd = w_down.rearrange("e (p c) n -> e p c n", c=HT)
    xv = table.rearrange("(b p) d -> b p d", p=P)
    yv = xv
    with Stage(nc, name) as s:
        g, u, d = s.sb("w_gate", [P, 2, KD, HID]), s.sb("w_up", [P, 2, KD, HID]), s.sb("w_down", [P, 2, HT, D])
        x, xt = s.sb("x", [P, 2, D]), s.sb("x_t", [P, KD, P])
        sg, hh, ht = s.sb("silu", [P, HID]), s.sb("hidden", [P, HID]), s.sb("hidden_t", [P, HT, P])
        y = s.sb("y", [P, 2, D])
        w_in, x_in = [s.sem(f"w_in{j}") for j in range(2)], [s.sem(f"x_in{j}") for j in range(2)]
        y_out = [s.sem(f"y_out{j}") for j in range(2)]
        x_turned, xt_ok, gate_mm, up_mm, silu_ok, h_ok = (s.sem(n) for n in ("x_turned", "xt_ok", "gate_mm", "up_mm", "silu_ok", "h_ok"))
        h_turned, ht_ok, down_mm, y_ok = (s.sem(n) for n in ("h_turned", "ht_ok", "down_mm", "y_ok"))
        block = s.block()

        @block.sync
        def _(sp):
            def load(b, j):
                e = sp.value_load(block_e[0:1, bass.ds(b + start, 1)], min_val=0, max_val=N_E - 1)
                one = lambda w: w[bass.ds(e, 1)].rearrange("a p k n -> p (a k) n")
                sp.dma_start(x[:, j, :], xv[bass.ds(b + start, 1)].rearrange("a p d -> p (a d)")).then_inc(x_in[j], 16)
                sp.dma_start(g[:, j], one(wg)).then_inc(w_in[j], 16)
                sp.dma_start(u[:, j], one(wu)).then_inc(w_in[j], 16)
                sp.dma_start(d[:, j], one(wd)).then_inc(w_in[j], 16)

            with if_used(sp):
                for b in range(2):
                    load(b, b)
                with sp.Fori(1, pairs) as i:
                    for j in range(2):
                        sp.wait_ge(down_mm, i * 2 + j)
                        load(i * 2 + j, j)
                for b in tail:
                    sp.wait_ge(down_mm, b)
                    load(b, b % 2)

        @block.tensor
        def _(pe):
            def turn_x(j, arrived):
                pe.wait_ge(x_in[j], arrived)
                for q in range(KD):
                    last = nc.tensor.transpose(k.ps[:, q // 4, (q % 4) * P:(q % 4 + 1) * P], x[:, j, q::KD], k.c("ident"))
                last.then_inc(x_turned, 1)

            def body(b, j, i, more):
                pe.wait_ge(xt_ok, b + 1)
                pe.wait_ge(w_in[j], (i + 1) * 48)
                pe.wait_ge(h_ok, b + 1)
                for w, bank, sem in ((g, 2, gate_mm), (u, 3, up_mm)):
                    for q in range(KD):
                        last = nc.tensor.matmul(k.ps[:, bank, :], xt[:, q, :], w[:, j, q, :], start=q == 0, stop=q == KD - 1)
                    last.then_inc(sem, 1)
                if more:
                    turn_x(1 - j, (i + 1 + j) * 16)
                pe.wait_ge(h_ok, b + 2)
                for c in range(HT):
                    last = nc.tensor.transpose(k.ps[:, 4, c * P:(c + 1) * P], hh[:, c::HT], k.c("ident"))
                last.then_inc(h_turned, 1)
                pe.wait_ge(ht_ok, b + 1)
                pe.wait_ge(y_ok, b + 1)
                for half in range(2):
                    for c in range(HT):
                        last = nc.tensor.matmul(k.ps[:, 5 + half, :], ht[:, c, :], d[:, j, c, half * BANK:(half + 1) * BANK],
                                                start=c == 0, stop=c == HT - 1)
                last.then_inc(down_mm, 1)

            with if_used(pe):
                pe.sem_inc(h_turned, 1)
                pe.sem_inc(down_mm, 1)
                turn_x(0, 16)
                with pe.Fori(0, pairs) as i:
                    for j in range(2):
                        body(i * 2 + j, j, i, True)
                for b in tail:
                    body(b, b % 2, pairs, b + 1 < count)

        @block.vector
        def _(v):
            def copy_x():
                return nc.vector.tensor_copy(xt[:].rearrange("p (b q) n -> p b (q n)", b=2), k.ps[:, 0:2, :])

            def body(b, more):
                v.wait_ge(silu_ok, b + 1)
                v.wait_ge(up_mm, b + 1)
                v.wait_ge(h_turned, b + 1)
                nc.vector.tensor_tensor(hh[:], sg[:], k.ps[:, 3, :], ALU.mult).then_inc(h_ok, 1)
                if more:
                    v.wait_ge(x_turned, b + 2)
                    copy_x().then_inc(xt_ok, 1)
                v.wait_ge(h_turned, b + 2)
                v.wait_ge(down_mm, b + 1)
                nc.vector.tensor_copy(ht[:].rearrange("p c n -> p (c n)"), k.ps[:, 4, :]).then_inc(ht_ok, 1)

            with if_used(v):
                v.sem_inc(h_ok, 1)
                v.wait_ge(x_turned, 1)
                copy_x().then_inc(xt_ok, 1)
                with v.Fori(0, count - 1) as b:
                    body(b, True)
                body(count - 1, False)

        @block.scalar
        def _(eng):
            def body(b, j, i):
                eng.wait_ge(gate_mm, b + 1)
                eng.wait_ge(h_ok, b + 1)
                nc.scalar.activation(sg[:], k.ps[:, 2, :], ACT.Silu).then_inc(silu_ok, 1)
                eng.wait_ge(down_mm, b + 2)
                eng.wait_ge(y_out[j], (i + 1) * 16)
                nc.scalar.activation(y[:, j, :].rearrange("p (h n) -> p h n", h=2), k.ps[:, 5:7, :], ACT.Copy).then_inc(y_ok, 1)
                eng.wait_ge(y_ok, b + 2)
                eng.dma_start(yv[bass.ds(b + start, 1)].rearrange("a p d -> p (a d)"), y[:, j, :]).then_inc(y_out[j], 16)

            with if_used(eng):
                eng.sem_inc(y_ok, 1)
                for j in range(2):
                    eng.sem_inc(y_out[j], 16)
                with eng.Fori(0, pairs) as i:
                    for j in range(2):
                        body(i * 2 + j, j, i)
                for b in tail:
                    body(b, b % 2, pairs)
                for j in range(2):
                    eng.wait_ge(y_out[j], (1 + pairs + sum(b % 2 == j for b in tail)) * 16)


def combine(k, rows, weights, gate):
    nc = k.nc
    with Stage(nc, "combine") as s:
        chain = s.sem("chain")
        block = s.block()

        @block.vector
        def _(v):
            link = in_order(v, chain)
            for t in range(NT):
                link(nc.vector.tensor_scalar(rows[:, 2 * t, :], rows[:, 2 * t, :], weights[:, t, 0:1], None, ALU.mult))
                link(nc.vector.scalar_tensor_tensor(out=rows[:, 2 * t, :], in0=rows[:, 2 * t + 1, :], scalar=weights[:, t, 1:2],
                                                    in1=rows[:, 2 * t, :], op0=ALU.mult, op1=ALU.add))
                link(nc.vector.tensor_tensor(rows[:, 2 * t, :], rows[:, 2 * t, :], gate, ALU.mult))
                link(nc.vector.tensor_tensor(k.x[:, t, :], k.x[:, t, :], rows[:, 2 * t, :], ALU.add))


def rows_affine(k, name, x, gain, shift=None):
    nc = k.nc
    with Stage(nc, name) as s:
        chain = s.sem("chain")
        block = s.block()

        @block.vector
        def _(v):
            link = in_order(v, chain)
            link(nc.vector.tensor_tensor(x, x, gain.unsqueeze(1).to_broadcast([P, NT, D]), ALU.mult))
            if shift is not None:
                link(nc.vector.tensor_tensor(x, x, shift.unsqueeze(1).to_broadcast([P, NT, D]), ALU.add))


def everywhere(row):
    return row.to_broadcast([P, row.shape[1]])


def first_experts(k, es, mod_rows):
    nc, a = k.nc, k.a
    table = k.scratch("expert_rows", [N_BLOCKS * P, D])

    def sb(stack, name, shape, dt=F32):
        return stack.enter_context(nc.sbuf_tensor(name, shape, dt))

    clear_rows(k, "clear_table", table)
    outer = es.enter_context(ExitStack())
    weights = sb(outer, "route_weights", [P, NT, TOP])
    dest = sb(outer, "route_dest", [P, NT * TOP], I32)
    block_e = sb(outer, "block_expert", [P, N_BLOCKS + 1], I32)
    with ExitStack() as st:
        h = sb(st, "h2", [P, NT, D])
        h_t = sb(st, "h2_t", [P, KD, SEQ])
        rows = sb(st, "mod_rows2", [P, 3, D])
        w_r = sb(st, "w_router", [P, KD, GROUPS + N_E])
        b_r = sb(st, "b_router", [GROUPS + N_E, 1])
        logits = sb(st, "logits", [P, NT, GROUPS + N_E])
        load_all(k, "router_in", [
            (rows[:, 0, :], everywhere(a["norm_ffn_g"])),
            (rows[:, 1, :], everywhere(mod_rows[0:1, 4 * D:5 * D])),
            (rows[:, 2, :], everywhere(mod_rows[0:1, 3 * D:4 * D])),
            (w_r[:, :, 0:GROUPS], a["router_group_w"][0].rearrange("(k p) n -> p k n", p=P)),
            (w_r[:, :, GROUPS:], a["router_expert_w"][0].rearrange("(k p) n -> p k n", p=P)),
            (b_r[0:GROUPS, :], a["router_group_b"][0].rearrange("(p o) -> p o", o=1)),
            (b_r[GROUPS:, :], a["router_expert_b"][0].rearrange("(p o) -> p o", o=1))])
        scale_gain(k, "ffn_gain", [(rows[:, 1, :], rows[:, 0, :])])
        norm_rows(k, "norm_ffn", [(k.x[:, t, :], h[:, t, :]) for t in range(NT)], D)
        rows_affine(k, "modulate2", h[:], rows[:, 1, :], rows[:, 2, :])
        turn(k, "turn_h2", [([h[:, t, i * P:(i + 1) * P] for t in range(NT)], h_t[:, i, :], None, None)
                            for i in range(KD)], NT)
        narrow_projection(k, "router", h_t, w_r, b_r[:, 0:1], GROUPS + N_E, logits[:])
        route(k, logits, weights, dest[:], block_e[:])
        scatter_rows(k, h, dest, table)
    used = block_e[0:1, N_BLOCKS:]
    for name, start, count, last in (("experts", 0, N_E, None), ("more_experts", N_E, N_BLOCKS - N_E, used)):
        experts(k, name, start, count, last, table, block_e,
                a["expert_w_gate"][0], a["expert_w_up"][0], a["expert_w_down"][0])
    with ExitStack() as st:
        rows = sb(st, "expert_rows_sb", [P, NT * TOP, D])
        gate = sb(st, "gate_rows2", [P, 2, D])
        load_all(k, "gate2_in", [(gate[:, 0, :], everywhere(mod_rows[0:1, 5 * D:6 * D])),
                                 (gate[:, 1, :], a["final_norm_g"].rearrange("(o n) -> o n", o=1).to_broadcast([P, D]))])
        gather_rows(k, rows, dest, table)
        combine(k, rows, weights, gate[:, 0, :])
        norm_rows(k, "norm_final", [(k.x[:, t, :], k.x[:, t, :]) for t in range(NT)], D)
        rows_affine(k, "final_gain", k.x[:], gate[:, 1, :])
    outer.close()



FF = 2816
FF_T = FF // P
FF_COLS = 256
RES = 0.5


def column_tables(k, name, rows):
    nc = k.nc
    total = sum(dst.shape[1] for _, dst in rows)
    assert total <= P
    with Stage(nc, name) as s:
        buf = s.sb("rows", [P, P])
        loaded, turned, done = s.sem("loaded"), s.sem("turned"), s.sem("done")
        block = s.block()

        @block.sync
        def _(sp):
            at = 0
            for src, dst in rows:
                sp.dma_start(buf[at:at + dst.shape[1], :], src).then_inc(loaded, 16)
                at += dst.shape[1]

        @block.tensor
        def _(pe):
            pe.wait_ge(loaded, 16 * len(rows))
            nc.tensor.transpose(k.ps[:, 0, 0:total], buf[0:total, :], k.c("ident")[0:total, 0:total]).then_inc(turned, 1)

        @block.vector
        def _(v):
            v.wait_ge(turned, 1)
            at = 0
            for _, dst in rows:
                nc.vector.tensor_copy(dst, k.ps[:, 0, at:at + dst.shape[1]]).then_inc(done, 1)
                at += dst.shape[1]


def by_tile(row):
    return row.rearrange("(k p) -> k p", p=P)


def ffn_hidden(k, name, u, w_gate, w_up, hidden):
    nc = k.nc
    pairs = FF_T // 2
    assert FF_T % 2 == 0
    wg, wu = (w.rearrange("(k p) n -> p k n", p=P) for w in (w_gate, w_up))
    with Stage(nc, name) as s:
        raw = s.sb("raw", [P, 2, 2, KD, P])
        w = split_sb(s, nc, f"{name}_w", [P, 2, 2, KD, P])
        sg = s.sb("silu", [P, 2, SEQ])
        whole = s.sb("whole", [P, 2, SEQ])
        w_in = [s.sem(f"w_in{j}") for j in range(2)]
        w_high, w_low, gate_mm, up_mm = s.sem("w_high"), s.sem("w_low"), s.sem("gate_mm"), s.sem("up_mm")
        silu_ok, whole_ok, h_high, h_low = s.sem("silu_ok"), s.sem("whole_ok"), s.sem("h_high"), s.sem("h_low")
        block = s.block()

        @block.sync
        def _(sp):
            def load(t, j):
                sp.dma_start(raw[:, j, 0], wg[:, :, bass.ds(t * P, P)]).then_inc(w_in[j], 16)
                sp.dma_start(raw[:, j, 1], wu[:, :, bass.ds(t * P, P)]).then_inc(w_in[j], 16)

            for t in range(2):
                load(t, t)
            with sp.Fori(1, pairs) as i:
                for j in range(2):
                    sp.wait_ge(w_low, i * 2 + (j - 1))
                    load(i * 2 + j, j)

        @block.tensor
        def _(pe):
            pe.sem_inc(up_mm, 1)
            with pe.Fori(0, pairs) as i:
                for j in range(2):
                    t = i * 2 + j
                    pe.wait_ge(w_low, t + 1)
                    pe.wait_ge(whole_ok, t + 1)
                    for side, sem in enumerate((gate_mm, up_mm)):
                        for q in range(KD):
                            last = product(nc, k.ps[:, 2 * j + side, :], w[:, j, side, q, :], u[:, q, :], q == 0, q == KD - 1)
                        last.then_inc(sem, 1)

        def tile_of(part, t):
            return part[:, bass.ds(t, 1), :].rearrange("p a n -> p (a n)")

        @block.scalar
        def _(eng):
            def high(t, j, i):
                eng.wait_ge(w_in[j], (i + 1) * 32)
                nc.scalar.activation(w.high[:, j], raw[:, j], ACT.Copy).then_inc(w_high, 1)

            def step(t, j):
                eng.wait_ge(gate_mm, t + 1)
                eng.wait_ge(whole_ok, t + 1)
                nc.scalar.activation(sg[:, j, :], k.ps[:, 2 * j, :], ACT.Silu).then_inc(silu_ok, 1)
                eng.wait_ge(whole_ok, t + 3)
                nc.scalar.activation(tile_of(hidden.high, t), whole[:, j, :], ACT.Copy).then_inc(h_high, 1)

            high(0, 0, 0)
            with eng.Fori(0, pairs - 1) as i:
                for j in range(2):
                    t = i * 2 + j
                    eng.wait_ge(up_mm, t + 1)
                    high(t + 1, 1 - j, i + j)
                    step(t, j)
            eng.wait_ge(up_mm, FF_T - 1)
            high(FF_T - 1, 1, pairs - 1)
            step(FF_T - 2, 0)
            step(FF_T - 1, 1)

        @block.vector
        def _(v):
            def low(t, j):
                v.wait_ge(w_high, t + 1)
                nc.vector.tensor_tensor(w.low[:, j], raw[:, j], w.high[:, j].bitcast(F32), ALU.subtract).then_inc(w_low, 1)

            def step(t, j):
                v.wait_ge(silu_ok, t + 1)
                v.wait_ge(up_mm, t + 2)
                nc.vector.tensor_tensor(whole[:, j, :], sg[:, j, :], k.ps[:, 2 * j + 1, :], ALU.mult).then_inc(whole_ok, 1)
                v.wait_ge(h_high, t + 1)
                nc.vector.tensor_tensor(tile_of(hidden.low, t), whole[:, j, :], tile_of(hidden.high, t).bitcast(F32),
                                        ALU.subtract).then_inc(h_low, 1)

            v.sem_inc(whole_ok, 2)
            low(0, 0)
            with v.Fori(0, pairs - 1) as i:
                for j in range(2):
                    low(i * 2 + (j + 1), 1 - j)
                    step(i * 2 + j, j)
            low(FF_T - 1, 1)
            step(FF_T - 2, 0)
            step(FF_T - 1, 1)


def ffn_down(k, name, hidden, w_down, f_t):
    nc = k.nc
    wd = w_down.rearrange("(t p) n -> t p n", p=P)
    with Stage(nc, name) as s:
        raw = s.sb("raw", [P, 2, 2, D])
        w = split_sb(s, nc, f"{name}_w", [P, 2, 2, D])
        w_in = [s.sem(f"w_in{j}") for j in range(2)]
        w_high, w_low, used, done = s.sem("w_high"), s.sem("w_low"), s.sem("used"), s.sem("done")
        block = s.block()
        loads = FF_T // 2
        assert FF_T % 2 == 0 and loads % 2 == 1

        @block.sync
        def _(sp):
            def load(b, j):
                sp.dma_start(raw[:, j], wd[bass.ds(b * 2, 2)].rearrange("a p n -> p a n")).then_inc(w_in[j], 16)

            for b in range(2):
                load(b, b)
            with sp.Fori(1, loads // 2) as i:
                for j in range(2):
                    sp.wait_ge(w_low, i * 2 + (j - 1))
                    load(i * 2 + j, j)
            sp.wait_ge(w_low, loads - 2)
            load(loads - 1, 0)

        @block.tensor
        def _(pe):
            def body(b, j, first=False, final=False):
                pe.wait_ge(w_low, b + 1)
                for a in range(2):
                    at = bass.ds(b * 2 + a, 1)
                    flat = lambda part: part[:, at, :].rearrange("p a n -> p (a n)")
                    rhs = Split(flat(hidden.high), flat(hidden.low))
                    for m in range(KD):
                        last = product(nc, k.ps[:, m, :], w[:, j, a, m * P:(m + 1) * P], rhs,
                                       first and a == 0, final and a == 1)
                last.then_inc(used, 1)

            for b in range(2):
                body(b, b, first=b == 0)
            with pe.Fori(1, loads // 2) as i:
                for j in range(2):
                    body(i * 2 + j, j)
            body(loads - 1, 0, final=True)

        @block.scalar
        def _(eng):
            def high(b, j, i):
                eng.wait_ge(w_in[j], (i + 1) * 16)
                nc.scalar.activation(w.high[:, j], raw[:, j], ACT.Copy).then_inc(w_high, 1)

            for b in range(2):
                high(b, b, 0)
            with eng.Fori(1, loads // 2) as i:
                for j in range(2):
                    eng.wait_ge(used, i * 2 + (j - 1))
                    high(i * 2 + j, j, i)
            eng.wait_ge(used, loads - 2)
            high(loads - 1, 0, loads // 2)
            eng.wait_ge(used, loads)
            for m in range(1, KD, 2):
                nc.scalar.activation(f_t[:, m, :], k.ps[:, m, :], ACT.Copy).then_inc(done, 1)

        @block.vector
        def _(v):
            def low(b, j):
                v.wait_ge(w_high, b + 1)
                nc.vector.tensor_tensor(w.low[:, j], raw[:, j], w.high[:, j].bitcast(F32), ALU.subtract).then_inc(w_low, 1)

            with v.Fori(0, loads // 2) as i:
                for j in range(2):
                    low(i * 2 + j, j)
            low(loads - 1, 0)
            v.wait_ge(used, loads)
            for m in range(0, KD, 2):
                nc.vector.tensor_copy(f_t[:, m, :], k.ps[:, m, :]).then_inc(done, 1)


def features_to_tokens(k, name, sources, dst):
    n = len(sources)
    per = min(4, n)
    turn(k, name, [([sources[j + q][:, t * P:(t + 1) * P] for q in range(per)], dst[:, t, j * P:(j + per) * P], None, None)
                   for t in range(NT) for j in range(0, n, per)], per)


def normed_input(k, name, gain_row, u_t):
    nc = k.nc
    with ExitStack() as st:
        xn = st.enter_context(nc.sbuf_tensor(f"{name}_xn", [P, NT, D], F32))
        gain = st.enter_context(nc.sbuf_tensor(f"{name}_gain", [P, KD], F32))
        column_tables(k, f"{name}_cols", [(by_tile(gain_row), gain[:])])
        norm_rows(k, f"{name}_norm", [(k.x[:, t, :], xn[:, t, :]) for t in range(NT)], D)
        turn(k, f"{name}_turn", [([xn[:, t, i * P:(i + 1) * P] for t in range(NT)], u_t[:, i, :], gain[:, i:i + 1], None)
                                 for i in range(KD)], NT)


def add_normed(k, name, f, gain_row, factor=None):
    nc = k.nc
    with ExitStack() as st:
        gain = st.enter_context(nc.sbuf_tensor(f"{name}_gain", [P, D], F32))
        load_all(k, f"{name}_in", [(gain[:], everywhere(gain_row))])
        norm_rows(k, f"{name}_norm", [(f[:, t, :], f[:, t, :]) for t in range(NT)], D)
        residual(k, f"{name}_add", f[:], gain[:], factor)


def ffn(k, name, layer, which):
    nc, a = k.nc, k.a
    nw = a["norm_w_2"][layer]
    first = 4 * which
    with ExitStack() as st:
        sb = lambda n, shape: st.enter_context(nc.sbuf_tensor(f"{name}_{n}", shape, F32))
        with ExitStack() as st2:
            hidden = split_sb(st2, nc, f"{name}_hidden", [P, FF_T, SEQ])
            with ExitStack() as st3:
                u = split_sb(st3, nc, f"{name}_u", [P, KD, SEQ])
                normed_input(k, f"{name}_pre", nw[first], u)
                ffn_hidden(k, f"{name}_up", u, a["ffn_w_gate_2"][layer, which], a["ffn_w_up_2"][layer, which], hidden)
            f_t = st2.enter_context(nc.sbuf_tensor(f"{name}_f_t", [P, KD, SEQ], F32))
            ffn_down(k, f"{name}_down", hidden, a["ffn_w_down_2"][layer, which], f_t)
            f = st2.enter_context(nc.sbuf_tensor(f"{name}_f", [P, NT, D], F32))
            features_to_tokens(k, f"{name}_turn", [f_t[:, i, :] for i in range(KD)], f)
            add_normed(k, f"{name}_post", f, nw[first + 1:first + 2], RES)


def soft_plus(k, name, x, out, n):
    nc = k.nc
    with Stage(nc, name) as s:
        na = s.sb("neg_abs", [P, n])
        negated, exped, logged, done = s.sem("negated"), s.sem("exped"), s.sem("logged"), s.sem("done")
        block = s.block()

        @block.vector
        def _(v):
            nc.vector.scalar_tensor_tensor(out=na[:], in0=x, scalar=-1.0, in1=x, op0=ALU.mult, op1=ALU.min).then_inc(negated, 1)
            v.wait_ge(logged, 1)
            nc.vector.scalar_tensor_tensor(out=out, in0=x, scalar=0.0, in1=na[:], op0=ALU.max, op1=ALU.add).then_inc(done, 1)

        @block.scalar
        def _(eng):
            eng.wait_ge(negated, 1)
            nc.scalar.activation(na[:], na[:], ACT.Exp).then_inc(exped, 1)
            eng.wait_ge(exped, 1)
            nc.scalar.activation(na[:], na[:], ACT.Ln, bias=1.0).then_inc(logged, 1)


def conv_silu(k, name, x_t, taps, bias, outs, n):
    nc = k.nc
    with Stage(nc, name) as s:
        acc = s.sb("acc", [P, 4, SEQ])
        first, added, done = s.sem("first"), s.sem("added"), s.sem("done")
        block = s.block()

        @block.scalar
        def _(eng):
            def finish(c):
                eng.wait_ge(added, 3 * (c + 1))
                nc.scalar.activation(outs[c], acc[:, c % 4, :], ACT.Silu,
                                     bias=0.0 if bias is None else bias[:, c:c + 1]).then_inc(done, 1)

            for c in range(n):
                if c >= 4:
                    eng.wait_ge(done, c - 3)
                nc.scalar.activation(acc[:, c % 4, :], x_t[:, c, 0:SEQ], ACT.Copy, scale=taps[:, c:c + 1]).then_inc(first, 1)
                if c >= 2:
                    finish(c - 2)
            finish(n - 2)
            finish(n - 1)

        @block.vector
        def _(v):
            for c in range(n):
                v.wait_ge(first, c + 1)
                for tap in range(1, 4):
                    if tap > 1:
                        v.wait_ge(added, 3 * c + tap - 1)
                    nc.vector.scalar_tensor_tensor(out=acc[:, c % 4, :], in0=x_t[:, c, tap:tap + SEQ],
                                                   scalar=taps[:, tap * n + c:tap * n + c + 1], in1=acc[:, c % 4, :],
                                                   op0=ALU.mult, op1=ALU.add).then_inc(added, 1)



WIN_H, WIN_D = 8, 64
DELTA_H, DELTA_D = 4, 128


def window_attention(k, qk_t, vals, out_t):
    nc = k.nc
    scale = WIN_D ** -0.5
    units = [(h, t) for h in range(WIN_H) for t in range(NT)]
    U = len(units)
    windows = k.c("windows")
    with Stage(nc, "windows") as s:
        sc, p, pt = s.sb("scores", [P, 2, SEQ]), s.sb("p", [P, 2, SEQ]), s.sb("p_t", [P, 2, SEQ])
        mx, den = s.sb("mx", [P, U]), s.sb("den", [P, U])
        score, masked, biased, soft = s.sem("score"), s.sem("masked"), s.sem("bias"), s.sem("soft")
        inverse, scaled, turned, pt_in = s.sem("inverse"), s.sem("scaled"), s.sem("turned"), s.sem("pt_in")
        pv, copied = s.sem("pv"), s.sem("copied")
        block = s.block()

        @block.tensor
        def _(pe):
            def scores(u):
                h, t = units[u]
                rows = slice((h % 2) * WIN_D, (h % 2 + 1) * WIN_D)
                if u >= 2:
                    pe.wait_ge(masked, u - 1)
                nc.tensor.matmul(k.ps[:, u % 2, 0:(t + 1) * P], qk_t[rows, h // 2, t * P:(t + 1) * P],
                                 qk_t[rows, 4 + h // 2, 0:(t + 1) * P], start=True, stop=True).then_inc(score, 1)

            scores(0)
            scores(1)
            for u, (h, t) in enumerate(units):
                pe.wait_ge(scaled, u + 1)
                if u >= 2:
                    pe.wait_ge(pt_in, u - 1)
                for q in range(t + 1):
                    last = nc.tensor.transpose(k.ps[:, 2 + u % 2, q * P:(q + 1) * P], p[:, u % 2, q * P:(q + 1) * P], k.c("ident"))
                last.then_inc(turned, 1)
                if u + 2 < U:
                    scores(u + 2)
                pe.wait_ge(pt_in, u + 1)
                if u >= 2:
                    pe.wait_ge(copied, u - 1)
                rows = slice((h % 2) * WIN_D, (h % 2 + 1) * WIN_D)
                for q in range(t + 1):
                    last = nc.tensor.matmul(k.ps[rows, 4 + u % 2, 0:P], vals[:, q, h * WIN_D:(h + 1) * WIN_D],
                                            pt[:, u % 2, q * P:(q + 1) * P], start=q == 0, stop=q == t)
                last.then_inc(pv, 1)

        @block.vector
        def _(v):
            def mask(u):
                h, t = units[u]
                w = (t + 1) * P
                v.wait_ge(score, u + 1)
                if u >= 2:
                    v.wait_ge(soft, u - 1)
                nc.vector.scalar_tensor_tensor(out=sc[:, u % 2, 0:w], in0=k.ps[:, u % 2, 0:w], scalar=scale,
                                               in1=windows[:, SEQ - w:SEQ], op0=ALU.mult, op1=ALU.add).then_inc(masked, 1)
                v.wait_ge(masked, u + 1)
                nc.vector.tensor_reduce(mx[:, u:u + 1], sc[:, u % 2, 0:w], AX.X, ALU.max, negate=True).then_inc(biased, 1)

            mask(0)
            for u, (h, t) in enumerate(units):
                if u + 1 < U:
                    mask(u + 1)
                w = (t + 1) * P
                v.wait_ge(soft, u + 1)
                nc.vector.reciprocal(den[:, u:u + 1], den[:, u:u + 1]).then_inc(inverse, 1)
                v.wait_ge(inverse, u + 1)
                nc.vector.tensor_scalar(p[:, u % 2, 0:w], p[:, u % 2, 0:w], den[:, u:u + 1], None, ALU.mult).then_inc(scaled, 1)

        @block.scalar
        def _(eng):
            def copy_out(u):
                h, t = units[u]
                rows = slice((h % 2) * WIN_D, (h % 2 + 1) * WIN_D)
                eng.wait_ge(pv, u + 1)
                nc.scalar.activation(out_t[rows, h // 2, t * P:(t + 1) * P], k.ps[rows, 4 + u % 2, 0:P], ACT.Copy).then_inc(copied, 1)

            for u in range(U + 1):
                if u < U:
                    w = (units[u][1] + 1) * P
                    eng.wait_ge(biased, u + 1)
                    if u >= 2:
                        eng.wait_ge(turned, u - 1)
                    nc.scalar.activation(p[:, u % 2, 0:w], sc[:, u % 2, 0:w], ACT.Exp, bias=mx[:, u:u + 1],
                                         accum_out=den[:, u:u + 1]).then_inc(soft, 1)
                if u:
                    c = u - 1
                    w = (units[c][1] + 1) * P
                    eng.wait_ge(turned, c + 1)
                    if c >= 2:
                        eng.wait_ge(pv, c - 1)
                    nc.scalar.activation(pt[:, c % 2, 0:w], k.ps[:, 2 + c % 2, 0:w], ACT.Copy).then_inc(pt_in, 1)
                    if c:
                        copy_out(c - 1)
            copy_out(U - 1)


def unit_columns(k, x_t, scales, eps=EPS):
    nc = k.nc
    n = len(scales)
    with Stage(nc, "unit") as s:
        sq, r = s.sb("sq", [P, 2, SEQ]), s.sb("r", [P, 2, SEQ])
        squared, summed, chain, root = s.sem("squared"), s.sem("summed"), s.sem("chain"), s.sem("root")
        block = s.block()

        @block.tensor
        def _(pe):
            for i in range(n):
                pe.wait_ge(squared, i + 1)
                if i >= 2:
                    pe.wait_ge(chain, 3 * (i - 2) + 1)
                nc.tensor.matmul(k.ps[:, i % 2, :], k.c("ones"), sq[:, i % 2, :], start=True, stop=True).then_inc(summed, 1)

        @block.scalar
        def _(eng):
            for i in range(n):
                if i >= 2:
                    eng.wait_ge(summed, i - 1)
                nc.scalar.activation(sq[:, i % 2, :], x_t[:, i, :], ACT.Square).then_inc(squared, 1)
                if i:
                    eng.wait_ge(chain, 3 * (i - 1) + 1)
                    nc.scalar.activation(r[:, (i - 1) % 2, :], r[:, (i - 1) % 2, :], ACT.Sqrt).then_inc(root, 1)
            eng.wait_ge(chain, 3 * (n - 1) + 1)
            nc.scalar.activation(r[:, (n - 1) % 2, :], r[:, (n - 1) % 2, :], ACT.Sqrt).then_inc(root, 1)

        @block.vector
        def _(v):
            link = in_order(v, chain)
            for i in range(n):
                v.wait_ge(summed, i + 1)
                link(nc.vector.tensor_scalar(r[:, i % 2, :], k.ps[:, i % 2, :], eps, None, ALU.add))
                v.wait_ge(root, i + 1)
                link(nc.vector.reciprocal(r[:, i % 2, :], r[:, i % 2, :]))
                link(nc.vector.scalar_tensor_tensor(out=x_t[:, i, :], in0=x_t[:, i, :], scalar=scales[i], in1=r[:, i % 2, :],
                                                    op0=ALU.mult, op1=ALU.mult))


def delta_gates(k, name, g, n, cum, last, exps, rest, ends):
    nc = k.nc
    with Stage(nc, name) as s:
        mm, chain, done = s.sem("mm"), s.sem("chain"), s.sem("done")
        sub = s.sem("sub")
        block = s.block()

        @block.tensor
        def _(pe):
            nc.tensor.matmul(k.ps[:, 0, 0:n], k.c("tri_fwd"), g, start=True, stop=True)
            nc.tensor.matmul(k.ps[:, 1, 0:n], k.c("same_chunk"), g, start=True, stop=True)
            for half in range(2):
                pick = k.c("same_chunk")[:, half * CHUNK:half * CHUNK + 1].to_broadcast([P, P])
                m = nc.tensor.matmul(k.ps[:, 2 + half, 0:n], pick, g, start=True, stop=True)
            m.then_inc(mm, 1)

        @block.vector
        def _(v):
            link = in_order(v, chain)
            v.wait_ge(mm, 1)
            link(nc.vector.tensor_copy(cum, k.ps[:, 0, 0:n]))
            link(nc.vector.tensor_copy(last, k.ps[:, 1, 0:n]))
            nc.vector.tensor_tensor(rest, last, cum, ALU.subtract).then_inc(sub, 1)

        @block.scalar
        def _(eng):
            eng.wait_ge(chain, 1)
            nc.scalar.activation(exps, cum, ACT.Exp).then_inc(done, 1)
            nc.scalar.activation(ends, k.ps[:, 2:4, 0:n], ACT.Exp).then_inc(done, 1)
            eng.wait_ge(sub, 1)
            nc.scalar.activation(rest, rest, ACT.Exp).then_inc(done, 1)


def delta_pairs(k, q_t, k_t, g, beta, cum, a_t, qk_t, q_dec):
    nc = k.nc
    H, W = DELTA_H, DELTA_H * P
    with Stage(nc, "delta_pairs") as s:
        dec, strict, eg = s.sb("decay", [P, 2, W]), s.sb("strict", [P, 2, W]), s.sb("exp_cum", [P, 2, W])
        mm, shifted, dec_ok, done = s.sem("mm"), s.sem("shifted"), s.sem("decay_ok"), s.sem("done")
        chain = s.sem("chain")
        block = s.block()

        @block.tensor
        def _(pe):
            for t in range(NT):
                b = 4 * (t % 2)
                if t >= 2:
                    pe.wait_ge(done, t - 1)
                cols = slice(t * P, (t + 1) * P)
                for h in range(H):
                    at = slice(h * P, (h + 1) * P)
                    nc.tensor.matmul(k.ps[:, b, at], g[:, t, h:h + 1].to_broadcast([P, P]), k.c("tri_fwd"), start=True, stop=True)
                    nc.tensor.matmul(k.ps[:, b + 1, at], beta[:, t, h:h + 1].to_broadcast([P, P]), k.c("ident"), start=True, stop=True)
                    nc.tensor.matmul(k.ps[:, b + 2, at], k_t[:, h, cols], k_t[:, h, cols], start=True, stop=True)
                    last = nc.tensor.matmul(k.ps[:, b + 3, at], k_t[:, h, cols], q_t[:, h, cols], start=True, stop=True)
                last.then_inc(mm, 1)

        @block.scalar
        def _(eng):
            for t in range(NT):
                eng.wait_ge(shifted, t + 1)
                nc.scalar.activation(eg[:, t % 2, :], k.ps[:, 4 * (t % 2), :], ACT.Exp).then_inc(dec_ok, 1)
                nc.scalar.activation(dec[:, t % 2, :], dec[:, t % 2, :], ACT.Exp).then_inc(dec_ok, 1)

        @block.vector
        def _(v):
            link = in_order(v, chain)
            heads = lambda x: x.rearrange("p (h n) -> p h n", h=H)
            for t in range(NT):
                b, j = 4 * (t % 2), t % 2
                v.wait_ge(mm, t + 1)
                for h in range(H):
                    at = slice(h * P, (h + 1) * P)
                    i = nc.vector.scalar_tensor_tensor(out=dec[:, j, at], in0=k.ps[:, b, at], scalar=cum[:, t, h:h + 1],
                                                       in1=k.c("add_incl"), op0=ALU.subtract, op1=ALU.add)
                    link(i) if h < H - 1 else i.then_inc(shifted, 1)
                v.wait_ge(dec_ok, 2 * t + 2)
                link(nc.vector.tensor_tensor(heads(strict[:, j, :]), heads(dec[:, j, :]),
                                             k.c("strict").unsqueeze(1).to_broadcast([P, H, P]), ALU.mult))
                link(nc.vector.tensor_tensor(strict[:, j, :], strict[:, j, :], k.ps[:, b + 1, :], ALU.mult))
                link(nc.vector.tensor_tensor(a_t[:, t, :], strict[:, j, :], k.ps[:, b + 2, :], ALU.mult))
                link(nc.vector.tensor_tensor(q_dec[:, :, t * P:(t + 1) * P], q_t[:, 0:H, t * P:(t + 1) * P], heads(eg[:, j, :]), ALU.mult))
                nc.vector.tensor_tensor(qk_t[:, t, :], dec[:, j, :], k.ps[:, b + 3, :], ALU.mult).then_inc(done, 1)


def delta_inverse(k, a_t, x, z):
    nc = k.nc
    W = DELTA_H * P
    H = DELTA_H
    heads = lambda v: v.rearrange("p (h n) -> p h n", h=H)
    with Stage(nc, "delta_inverse") as s:
        part, prod = s.sb("part", [P, 2, W]), s.sb("prod", [P, 2, W])
        parted, mm1, prod_ok, mm2, done = (s.sem(n) for n in ("parted", "product_mm", "product_ok", "update_mm", "done"))
        init = s.sem("init")
        chain = s.sem("chain")
        block = s.block()
        units = [(level, t) for level in range(1, 7) for t in range(NT)]

        @block.vector
        def _(v):
            link = in_order(v, init)
            for t in range(NT):
                for m in (x, z):
                    link(nc.vector.tensor_copy(heads(m[:, t, :]), k.c("ident").unsqueeze(1).to_broadcast([P, H, P])))

            def cut(u):
                level, t = units[u]
                if u >= 2:
                    v.wait_ge(mm1, u - 1)
                nc.vector.tensor_tensor(heads(part[:, u % 2, :]), heads(a_t[:, t, :]),
                                        k.c(f"merge{level}").unsqueeze(1).to_broadcast([P, H, P]), ALU.mult).then_inc(parted, 1)

            cut(0)
            for u, (level, t) in enumerate(units):
                if u + 1 < len(units):
                    cut(u + 1)
                b = 4 * (u % 2)
                v.wait_ge(mm2, u + 1)
                nc.vector.tensor_tensor(x[:, t, :], x[:, t, :], k.ps[:, b + 1, :], ALU.subtract).then_inc(done, 1)
                nc.vector.tensor_tensor(z[:, t, :], z[:, t, :], k.ps[:, b + 2, :], ALU.subtract).then_inc(done, 1)

        @block.scalar
        def _(eng):
            for u in range(len(units)):
                eng.wait_ge(mm1, u + 1)
                if u >= 2:
                    eng.wait_ge(mm2, u - 1)
                nc.scalar.activation(prod[:, u % 2, :], k.ps[:, 4 * (u % 2), :], ACT.Copy).then_inc(prod_ok, 1)

        @block.tensor
        def _(pe):
            pe.wait_ge(init, 2 * NT)

            def product(u):
                level, t = units[u]
                pe.wait_ge(parted, u + 1)
                if level > 1:
                    pe.wait_ge(done, 2 * (u - NT) + 2)
                if u >= 2:
                    pe.wait_ge(prod_ok, u - 1)
                for h in range(H):
                    at = slice(h * P, (h + 1) * P)
                    last = nc.tensor.matmul(k.ps[:, 4 * (u % 2), at], part[:, u % 2, at], x[:, t, at], start=True, stop=True)
                last.then_inc(mm1, 1)

            product(0)
            for u, (level, t) in enumerate(units):
                if u + 1 < len(units):
                    product(u + 1)
                pe.wait_ge(prod_ok, u + 1)
                if u >= 2:
                    pe.wait_ge(done, 2 * (u - 2) + 2)
                for h in range(H):
                    at = slice(h * P, (h + 1) * P)
                    nc.tensor.matmul(k.ps[:, 4 * (u % 2) + 1, at], z[:, t, at], prod[:, u % 2, at], start=True, stop=True)
                    last = nc.tensor.matmul(k.ps[:, 4 * (u % 2) + 2, at], prod[:, u % 2, at], z[:, t, at], start=True, stop=True)
                last.then_inc(mm2, 1)


def delta_solve(k, z, v_beta, k_beta, u, w_t):
    nc = k.nc
    with Stage(nc, "delta_solve") as s:
        mm, u_ok, w_ok = s.sem("mm"), s.sem("u_ok"), s.sem("w_ok")
        block = s.block()

        @block.tensor
        def _(pe):
            for t in range(NT):
                for h in range(DELTA_H):
                    at = slice(h * P, (h + 1) * P)
                    nc.tensor.matmul(k.ps[:, t, at], z[:, t, at], v_beta[:, t, at], start=True, stop=True)
                    last = nc.tensor.matmul(k.ps[:, 4 + t, at], k_beta[:, t, at], z[:, t, at], start=True, stop=True)
                last.then_inc(mm, 1)

        @block.vector
        def _(v):
            for t in range(NT):
                v.wait_ge(mm, t + 1)
                nc.vector.tensor_copy(u[:, t, :], k.ps[:, t, :]).then_inc(u_ok, 1)

        @block.scalar
        def _(eng):
            for t in range(NT):
                eng.wait_ge(mm, t + 1)
                nc.scalar.activation(w_t[:, :, t * P:(t + 1) * P], k.ps[:, 4 + t, :].rearrange("p (h n) -> p h n", h=DELTA_H),
                                     ACT.Copy).then_inc(w_ok, 1)


def delta_scan(k, u, w_t, q_dec, qk_t, k_dec, ends, out):
    nc = k.nc
    H, W = DELTA_H, DELTA_H * P
    chunks = SEQ // CHUNK
    heads = lambda x: x.rearrange("p (h n) -> p h n", h=H)
    with Stage(nc, "delta_scan") as s:
        state, faded = s.sb("state", [P, 2, W]), s.sb("faded", [P, W])
        vn = s.sb("v_new", [P, 2, W])
        w_mm, vn_ok, o_mm, s_mm, s_ok, f_ok, o_ok = (s.sem(n) for n in
                                                     ("w_mm", "v_new_ok", "o_mm", "s_mm", "state_ok", "faded_ok", "out_ok"))
        block = s.block()

        @block.tensor
        def _(pe):
            for c in range(chunks):
                t, half = divmod(c, 2)
                rows = slice(half * CHUNK, (half + 1) * CHUNK)
                cols = slice(c * CHUNK, (c + 1) * CHUNK)
                pe.wait_ge(s_ok, c + 1)
                for h in range(H):
                    at = slice(h * P, (h + 1) * P)
                    last = nc.tensor.matmul(k.ps[rows, c % 2, at], w_t[:, h, cols], state[:, c % 2, at], start=True, stop=True)
                last.then_inc(w_mm, 1)
                if c >= 2:
                    pe.wait_ge(o_ok, c - 1)
                for h in range(H):
                    at = slice(h * P, (h + 1) * P)
                    nc.tensor.matmul(k.ps[rows, 2 + c % 2, at], q_dec[:, h, cols], state[:, c % 2, at],
                                     start=h == 0, stop=False, skip_group_check=True)
                pe.wait_ge(vn_ok, c + 1)
                for h in range(H):
                    at = slice(h * P, (h + 1) * P)
                    last = nc.tensor.matmul(k.ps[:, 4 + c % 2, at], k_dec[rows, t, at], vn[rows, c % 2, at], start=True, stop=True)
                last.then_inc(s_mm, 1)
                for h in range(H):
                    at = slice(h * P, (h + 1) * P)
                    last = nc.tensor.matmul(k.ps[rows, 2 + c % 2, at], qk_t[rows, t, h * P + half * CHUNK:h * P + (half + 1) * CHUNK],
                                            vn[rows, c % 2, at], start=False, stop=True, skip_group_check=True)
                last.then_inc(o_mm, 1)

        @block.vector
        def _(v):
            nc.vector.memset(state[:, 0, :], 0.0).then_inc(s_ok, 1)
            for c in range(chunks):
                t, half = divmod(c, 2)
                rows = slice(half * CHUNK, (half + 1) * CHUNK)
                v.wait_ge(s_ok, c + 1)
                nc.vector.tensor_tensor(heads(faded[:]), heads(state[:, c % 2, :]),
                                        ends[:, half, t * H:(t + 1) * H].unsqueeze(2).to_broadcast([P, H, P]), ALU.mult).then_inc(f_ok, 1)
                v.wait_ge(w_mm, c + 1)
                if c >= 2:
                    v.wait_ge(o_mm, c - 1)
                nc.vector.tensor_tensor(vn[rows, c % 2, :], u[rows, t, :], k.ps[rows, c % 2, :], ALU.subtract).then_inc(vn_ok, 1)
                v.wait_ge(s_mm, c + 1)
                v.wait_ge(f_ok, c + 1)
                nc.vector.tensor_tensor(state[:, (c + 1) % 2, :], faded[:], k.ps[:, 4 + c % 2, :], ALU.add).then_inc(s_ok, 1)

        @block.scalar
        def _(eng):
            for c in range(chunks):
                t, half = divmod(c, 2)
                rows = slice(half * CHUNK, (half + 1) * CHUNK)
                eng.wait_ge(o_mm, c + 1)
                nc.scalar.activation(out[rows, t, :], k.ps[rows, 2 + c % 2, :], ACT.Copy).then_inc(o_ok, 1)


def vector_steps(k, name, steps):
    with Stage(k.nc, name) as s:
        chain = s.sem("chain")
        block = s.block()

        @block.vector
        def _(v):
            link = in_order(v, chain)
            for step in steps:
                link(step(k.nc.vector))


def exp_rows(k, name, x, func=ACT.Exp):
    with Stage(k.nc, name) as s:
        done = s.sem("done")
        block = s.block()

        @block.scalar
        def _(eng):
            k.nc.scalar.activation(x, x, func).then_inc(done, 1)


def even_layer(k):
    nc, a = k.nc, k.a
    w_in = a["even_w_in_2"][0]
    nw = a["norm_w_2"][0]
    H = DELTA_H
    with ExitStack() as st:
        def sb(stack, name, shape):
            return stack.enter_context(nc.sbuf_tensor(f"even_{name}", shape, F32))

        mix_t = sb(st, "mix_t", [P, KD, SEQ])
        z = sb(st, "z", [P, NT, 512])
        qkv = sb(st, "qkv", [P, 12, SEQ])
        ba = sb(st, "beta_a", [P, NT, 2 * H])
        cols = sb(st, "cols", [P, 48 + 1])
        with ExitStack() as s2:
            u_t = sb(s2, "u_t", [P, KD, SEQ])
            normed_input(k, "even_pre", nw[2], u_t)
            with ExitStack() as s3:
                qk_t, va = sb(s3, "qk_t", [P, 8, SEQ]), sb(s3, "va", [P, NT, 512])
                project_features(k, "even_qk", u_t, [(0, SEQ)], w_in, 0, 2, qk_t)
                project_tokens(k, "even_va", u_t, NT, w_in, 2 * 512, 1, va)
                window_attention(k, qk_t, va, mix_t)
            project_tokens(k, "even_z", u_t, NT, w_in, 6 * 512, 1, z)
            with ExitStack() as s3:
                w_ba, b_ba = sb(s3, "w_ba", [P, KD, 2 * H]), sb(s3, "b_ba", [2 * H, 1])
                vector_steps(k, "even_clear", [lambda v: v.memset(b_ba[:], 0.0)])
                load_all(k, "even_ba_in", [(w_ba[:], w_in.rearrange("(k p) n -> p k n", p=P)[:, :, 7 * 512:]),
                                           (b_ba[H:, :], a["even_dt_bias_2"][0].rearrange("(p o) -> p o", o=1))])
                narrow_projection(k, "even_ba", u_t, w_ba, b_ba[:, 0:1], 2 * H, ba[:])
            with ExitStack() as s3:
                x_t = sb(s3, "x_t", [P, 12, SEQ + 3])
                vector_steps(k, "even_pad", [lambda v: v.memset(x_t[:, :, 0:3], 0.0)])
                project_features(k, "even_qkv", u_t, [(0, SEQ)], w_in, 3 * 512, 3, x_t[:, :, 3:])
                column_tables(k, "even_cols", [(a["even_conv_w_2"][0].rearrange("k (c p) -> (k c) p", p=P), cols[:, 0:48]),
                                               (a["even_head_norm_w_2"], cols[:, 48:49])])
                conv_silu(k, "even_conv", x_t, cols[:, 0:48], None, [qkv[:, i, :] for i in range(12)], 12)
        unit_columns(k, qkv, [DELTA_D ** -0.5] * H + [1.0] * H)
        n = NT * H
        beta, g = sb(st, "beta", [P, NT, H]), sb(st, "g", [P, NT, H])
        a_log = sb(st, "a_log", [P, H])
        sums = {x: sb(st, x, [P, NT, H]) for x in ("cum", "last", "exps", "rest")}
        flat = {x: y[:].rearrange("p t h -> p (t h)") for x, y in sums.items()}
        ends = sb(st, "ends", [P, 2, n])
        load_all(k, "even_alog_in", [(a_log[:], everywhere(a["even_a_log_2"]))])
        exp_rows(k, "even_alog", a_log[:])
        vector_steps(k, "even_split", [lambda v: v.tensor_copy(beta[:], ba[:, :, 0:H]), lambda v: v.tensor_copy(g[:], ba[:, :, H:])])
        gf = g[:].rearrange("p t h -> p (t h)")
        soft_plus(k, "even_softplus", gf, gf, n)
        exp_rows(k, "even_sigmoid", beta[:], ACT.Sigmoid)
        vector_steps(k, "even_decay", [lambda v: v.scalar_tensor_tensor(
            out=g[:], in0=g[:], scalar=-1.0, in1=a_log[:].unsqueeze(1).to_broadcast([P, NT, H]), op0=ALU.mult, op1=ALU.mult)])
        delta_gates(k, "even_sums", gf, n, flat["cum"], flat["last"], flat["exps"], flat["rest"], ends[:])
        with ExitStack() as s2:
            a_t, qk2 = sb(s2, "a_t", [P, NT, 512]), sb(s2, "qk2", [P, NT, 512])
            q_dec = sb(s2, "q_dec", [P, H, SEQ])
            w_t, u = sb(s2, "w_t", [P, H, SEQ]), sb(s2, "u", [P, NT, 512])
            k_tok, v_tok = sb(s2, "k_tok", [P, NT, 512]), sb(s2, "v_tok", [P, NT, 512])
            k_beta = sb(s2, "k_beta", [P, NT, 512])
            delta_pairs(k, qkv[:, 0:H], qkv[:, H:2 * H], g, beta, sums["cum"], a_t, qk2, q_dec)
            features_to_tokens(k, "even_ktok", [qkv[:, H + i, :] for i in range(H)], k_tok)
            features_to_tokens(k, "even_vtok", [qkv[:, 2 * H + i, :] for i in range(H)], v_tok)
            with ExitStack() as s3:
                x, zz = sb(s3, "inv", [P, NT, 512]), sb(s3, "inv_t", [P, NT, 512])
                delta_inverse(k, a_t, x, zz)
                wide = lambda y: y[:].rearrange("p t (h n) -> p (t h) n", h=H)
                per = lambda y: y[:].rearrange("p t h -> p (t h)").unsqueeze(2).to_broadcast([P, n, P])
                vector_steps(k, "even_scale", [
                    lambda v: v.tensor_tensor(wide(v_tok), wide(v_tok), per(beta), ALU.mult),
                    lambda v: v.tensor_tensor(sums["last"][:], beta[:], sums["exps"][:], ALU.mult),
                    lambda v: v.tensor_tensor(wide(k_beta), wide(k_tok), per(sums["last"]), ALU.mult),
                    lambda v: v.tensor_tensor(wide(k_tok), wide(k_tok), per(sums["rest"]), ALU.mult)])
                delta_solve(k, zz, v_tok, k_beta, u, w_t)
            o = sb(s2, "o", [P, NT, 512])
            delta_scan(k, u, w_t, q_dec, qk2, k_tok, ends, o)
            silu_rows(k, "even_silu_z", [z[:]])
            norm_heads(k, "even_heads", o[:].rearrange("p t (h n) -> p (t h) n", h=H), n, P, [(o[:], z[:])])
            turn(k, "even_turn_o", [([o[:, t, h * P:(h + 1) * P] for t in range(NT)], mix_t[:, 4 + h, :], cols[:, 48:49], None)
                                    for h in range(H)], NT)
        m = sb(st, "m", [P, NT, D])
        project_tokens(k, "even_out", mix_t, NT, a["even_w_out_2"][0], 0, 2, m)
        add_normed(k, "even_post", m, nw[3:4])



SSD_IN = 2 * D
SSD_P, SSD_G, SSD_N = 64, 4, 128
SSD_H = SSD_IN // SSD_P
SSD_R = SSD_H // SSD_G


def ssd_scan(k, xdt, b_tok, bc_t, acc, cum, exps, rest, ends):
    nc = k.nc
    R, W = SSD_R, SSD_R * SSD_P
    units = [(t, g) for t in range(NT) for g in range(SSD_G)]
    U = len(units)
    with Stage(nc, "ssd") as s:
        state = s.sb("state", [P, SSD_G, 2, W])
        seg, mix = s.sb("seg", [P, R, P]), s.sb("mix", [P, R, P])
        cb_mm, shifted, seg_ok, mixed = s.sem("cb_mm"), s.sem("shifted"), s.sem("seg_ok"), s.sem("mixed")
        upd_mm, diag_mm, off_mm, s_ok, y_ok = (s.sem(n) for n in ("update_mm", "diag_mm", "off_mm", "state_ok", "y_ok"))
        chain, faded_ok = s.sem("chain"), s.sem("faded_ok")
        faded = s.sb("faded", [P, W])
        x_end, x_end_ok = s.sb("x_end", [P, 2, W]), s.sem("x_end_ok")
        block = s.block()

        @block.tensor
        def _(pe):
            def decays(n):
                t, g = units[n]
                cols = slice(t * P, (t + 1) * P)
                if n:
                    pe.wait_ge(mixed, n)
                for r in range(R):
                    h = g * R + r
                    nc.tensor.matmul(k.ps[:, r // 4, (r % 4) * P:(r % 4 + 1) * P], acc[:, t, h:h + 1].to_broadcast([P, P]),
                                     k.c("tri_fwd"), start=True, stop=True)
                nc.tensor.matmul(k.ps[:, 2, 0:P], bc_t[:, g, cols], bc_t[:, SSD_G + g, cols], start=True, stop=True).then_inc(cb_mm, 1)

            decays(0)
            for n, (t, g) in enumerate(units):
                pe.wait_ge(s_ok, 2 * n + 1)
                if n:
                    pe.wait_ge(y_ok, n)
                pe.wait_ge(x_end_ok, n + 1)
                for half in range(2):
                    rows = slice(half * CHUNK, (half + 1) * CHUNK)
                    nc.tensor.matmul(k.ps[:, 4 + half, :], b_tok[rows, t, g * SSD_N:(g + 1) * SSD_N],
                                     x_end[rows, n % 2, :], start=True, stop=True).then_inc(upd_mm, 1)
                nc.tensor.matmul(k.ps[0:CHUNK, 3, :], bc_t[:, SSD_G + g, t * P:t * P + CHUNK], state[:, g, 0, :],
                                 start=True, stop=True)
                pe.wait_ge(mixed, n + 1)
                for r in range(R):
                    h = g * R + r
                    last = nc.tensor.matmul(k.ps[:, 6, r * SSD_P:(r + 1) * SSD_P], mix[:, r, :], xdt[:, t, h * SSD_P:(h + 1) * SSD_P],
                                            start=True, stop=True)
                last.then_inc(diag_mm, 1)
                if n + 1 < U:
                    decays(n + 1)
                pe.wait_ge(s_ok, 2 * n + 2)
                nc.tensor.matmul(k.ps[CHUNK:P, 3, :], bc_t[:, SSD_G + g, t * P + CHUNK:(t + 1) * P], state[:, g, 1, :],
                                 start=True, stop=True).then_inc(off_mm, 1)

        @block.scalar
        def _(eng):
            for n in range(U):
                eng.wait_ge(shifted, n + 1)
                nc.scalar.activation(seg[:], seg[:], ACT.Exp).then_inc(seg_ok, 1)

        @block.vector
        def _(v):
            link = in_order(v, chain)
            heads = lambda x: x.rearrange("p (r n) -> p r n", r=R)
            link(nc.vector.memset(state[:], 0.0))

            def advance(n, half, done):
                t, g = units[n]
                at = t * SSD_H + g * R
                link(nc.vector.tensor_tensor(heads(faded[:]), heads(state[:, g, half, :]),
                                             ends[:, half, at:at + R].unsqueeze(2).to_broadcast([P, R, SSD_P]), ALU.mult))
                v.wait_ge(upd_mm, 2 * n + half + 1)
                return nc.vector.tensor_tensor(state[:, g, 1 - half, :], faded[:], k.ps[:, 4 + half, :], ALU.add)

            for n, (t, g) in enumerate(units):
                v.sem_inc(s_ok, 1)
                nc.vector.tensor_tensor(heads(x_end[:, n % 2, :]), heads(xdt[:, t, g * W:(g + 1) * W]),
                                        rest[:, t, g * R:(g + 1) * R].unsqueeze(2).to_broadcast([P, R, SSD_P]),
                                        ALU.mult).then_inc(x_end_ok, 1)
                v.wait_ge(cb_mm, n + 1)
                for r in range(R):
                    h = g * R + r
                    i = nc.vector.scalar_tensor_tensor(out=seg[:, r, :], in0=k.ps[:, r // 4, (r % 4) * P:(r % 4 + 1) * P],
                                                       scalar=cum[:, t, h:h + 1], in1=k.c("add_incl"), op0=ALU.subtract, op1=ALU.add)
                    link(i) if r < R - 1 else i.then_inc(shifted, 1)
                advance(n, 0, None).then_inc(s_ok, 1)
                v.wait_ge(seg_ok, n + 1)
                if n:
                    v.wait_ge(diag_mm, n)
                nc.vector.tensor_tensor(mix[:], seg[:], k.ps[:, 2, 0:P].unsqueeze(1).to_broadcast([P, R, P]), ALU.mult).then_inc(mixed, 1)
                v.wait_ge(s_ok, 2 * n + 2)
                v.wait_ge(diag_mm, n + 1)
                link(advance(n, 1, None))
                v.wait_ge(off_mm, n + 1)
                at = t * SSD_H + g * R
                out = xdt[:, t, g * W:(g + 1) * W]
                link(nc.vector.tensor_tensor(heads(out), heads(k.ps[:, 3, :]),
                                             exps[:, t, g * R:(g + 1) * R].unsqueeze(2).to_broadcast([P, R, SSD_P]), ALU.mult))
                i = nc.vector.tensor_tensor(out, out, k.ps[:, 6, :], ALU.add)
                i.then_inc(y_ok, 1)


def odd_layer(k):
    nc, a = k.nc, k.a
    w_in = a["odd_w_in_2"][0]
    nw = a["norm_w_2"][1]
    with ExitStack() as st:
        def sb(stack, name, shape):
            return stack.enter_context(nc.sbuf_tensor(f"odd_{name}", shape, F32))

        y = sb(st, "y", [P, NT, SSD_IN])
        xx = y[:].rearrange("p t (j n) -> p (t j) n", n=SEQ)
        with ExitStack() as s1:
            z = sb(s1, "z", [P, NT, SSD_IN])
            cols = sb(s1, "cols", [P, 24 * 4 + 24])
            dt = sb(s1, "dt", [P, NT, SSD_H])
            bc_t, b_tok = sb(s1, "bc_t", [P, 8, SEQ]), sb(s1, "b_tok", [P, NT, 512])
            la = sb(s1, "log_decay", [P, NT, SSD_H])
            head = sb(s1, "head_rows", [P, 2, SSD_H])
            sums = {x: sb(s1, x, [P, NT, SSD_H]) for x in ("cum", "last", "exps", "rest")}
            ends = sb(s1, "ends", [P, 2, NT * SSD_H])
            n = NT * SSD_H
            with ExitStack() as s2:
                x_t = sb(s2, "x_t", [P, 12, SEQ + 3])
                u_t = sb(s2, "u_t", [P, KD, SEQ])
                normed_input(k, "odd_pre", nw[2], u_t)
                project_tokens(k, "odd_z", u_t, NT, w_in, 0, 4, z)
                with ExitStack() as s3:
                    w_dt, b_dt = sb(s3, "w_dt", [P, KD, SSD_H]), sb(s3, "b_dt", [SSD_H, 1])
                    load_all(k, "odd_dt_in", [(w_dt[:], w_in.rearrange("(k p) n -> p k n", p=P)[:, :, SSD_IN + 3 * D:]),
                                              (b_dt[:], a["odd_dt_bias_2"][0].rearrange("(p o) -> p o", o=1)),
                                              (head[:, 0, :], everywhere(a["odd_a_log_2"])),
                                              (head[:, 1, :], everywhere(a["odd_d_skip_2"]))])
                    narrow_projection(k, "odd_dt", u_t, w_dt, b_dt[:, 0:1], SSD_H, dt[:])
                column_tables(k, "odd_cols", [(a["odd_conv_w_2"][0].rearrange("k (c p) -> (k c) p", p=P), cols[:, 0:96]),
                                              (a["odd_conv_b_2"].rearrange("o (c p) -> (o c) p", p=P), cols[:, 96:120])])
                vector_steps(k, "odd_pad", [lambda v: v.memset(x_t[:, :, 0:3], 0.0)])
                outs = [xx[:, i, :] for i in range(16)] + [bc_t[:, i, :] for i in range(8)]
                for half in range(2):
                    project_features(k, f"odd_xbc{half}", u_t, [(0, SEQ)], w_in, SSD_IN + half * 3 * 512, 3, x_t[:, :, 3:])
                    part = slice(half * 12, half * 12 + 12)
                    taps = sb(s2, f"taps{half}", [P, 48])
                    vector_steps(k, f"odd_taps{half}", [lambda v, q=q, part=part, taps=taps: v.tensor_copy(
                        taps[:, q * 12:(q + 1) * 12], cols[:, q * 24 + part.start:q * 24 + part.stop]) for q in range(4)])
                    conv_silu(k, f"odd_conv{half}", x_t, taps[:], cols[:, 96 + part.start:96 + part.stop], outs[part], 12)
            features_to_tokens(k, "odd_btok", [bc_t[:, i, :] for i in range(4)], b_tok)
            exp_rows(k, "odd_alog", head[:, 0, :])
            dtf = dt[:].rearrange("p t h -> p (t h)")
            soft_plus(k, "odd_softplus", dtf, dtf, n)
            vector_steps(k, "odd_decay", [lambda v: v.scalar_tensor_tensor(
                out=la[:], in0=dt[:], scalar=-1.0, in1=head[:, 0, :].unsqueeze(1).to_broadcast([P, NT, SSD_H]), op0=ALU.mult, op1=ALU.mult)])
            flat = {x: y[:].rearrange("p t h -> p (t h)") for x, y in sums.items()}
            delta_gates(k, "odd_sums", la[:].rearrange("p t h -> p (t h)"), n, flat["cum"], flat["last"], flat["exps"], flat["rest"], ends[:])
            with ExitStack() as s2:
                xs = sb(s2, "xs", [P, NT, SSD_IN])
                features_to_tokens(k, "odd_xtok", [xx[:, i, :] for i in range(16)], xs)
                wide = lambda v: v[:].rearrange("p t (h n) -> p (t h) n", n=SSD_P)
                per = lambda v: v.rearrange("p t h -> p (t h)").unsqueeze(2).to_broadcast([P, n, SSD_P])
                vector_steps(k, "odd_xdt", [lambda v: v.tensor_tensor(wide(y), wide(xs), per(dt[:]), ALU.mult)])
                ssd_scan(k, y, b_tok, bc_t, la, sums["cum"], sums["exps"], sums["rest"], ends)
                skip = head[:, 1, :].unsqueeze(2).to_broadcast([P, SSD_H, SSD_P])
                heads = lambda v: v.rearrange("p (h n) -> p h n", n=SSD_P)
                steps = []
                for t in range(NT):
                    steps += [lambda v, t=t: v.tensor_tensor(heads(xs[:, t, :]), heads(xs[:, t, :]), skip, ALU.mult),
                              lambda v, t=t: v.tensor_tensor(y[:, t, :], y[:, t, :], xs[:, t, :], ALU.add)]
                vector_steps(k, "odd_skip", steps)
            silu_rows(k, "odd_silu_z", [z[:, t, :] for t in range(NT)])
            vector_steps(k, "odd_gate", [lambda v: v.tensor_tensor(y[:], y[:], z[:], ALU.mult)])
        groups = [y[:, t, g * 512:(g + 1) * 512] for t in range(NT) for g in range(4)]
        norm_rows(k, "odd_groups", [(v, v) for v in groups], 512)
        y_t = sb(st, "y_t", [P, 16, SEQ])
        gains = sb(st, "out_gain", [P, 16])
        column_tables(k, "odd_gain", [(a["odd_out_norm_w_2"].rearrange("o (c p) -> (o c) p", p=P), gains[:])])
        turn(k, "odd_turn_y", [([y[:, t, i * P:(i + 1) * P] for t in range(NT)], y_t[:, i, :], gains[:, i:i + 1], None)
                               for i in range(16)], NT)
        m = sb(st, "m", [P, NT, D])
        project_tokens(k, "odd_out", y_t, NT, a["odd_w_out_2"][0], 0, 2, m, k_tiles=16)
        add_normed(k, "odd_post", m, nw[3:4])


def second_block(k):
    ffn(k, "f0", 0, 0)
    even_layer(k)
    ffn(k, "f1", 0, 1)
    ffn(k, "f2", 1, 0)
    odd_layer(k)
    ffn(k, "f3", 1, 1)


def build_program(nc, args, out):
    with ExitStack() as es:
        k = Core(nc, args, es)
        mod_rows = k.scratch("mod_rows", [2, 6 * D])
        load_all(k, "start", [(k.table[:], args["const_table"]),
                              (k.x[:], args["x"][0].rearrange("(t p) d -> p t d", p=P))])
        modulation(k, mod_rows)
        first_mixer(k, es, mod_rows)
        first_experts(k, es, mod_rows)
        second_block(k)
        with Stage(nc, "finish") as s:
            stored = s.sem("stored")
            block = s.block()

            @block.sync
            def _(sp):
                sp.dma_start(out[0].rearrange("(t p) d -> p t d", p=P), k.x[:]).then_inc(stored, 16)
                sp.wait_ge(stored, 16)


def kernel(**inputs):
    import concourse.bacc as _bacc
    from concourse.bass_utils import run_bass_kernel_spmd as _run

    nc = _bacc.Bacc("TRN2", target_bir_lowering=False, num_devices=1)
    arrays, args = {}, {}
    for name, value in dict(inputs, const_table=CONST_DATA).items():
        a = np.ascontiguousarray(value)
        arrays[f"in_{name}"] = a
        args[name] = nc.dram_tensor(f"in_{name}", a.shape, mybir.dt.from_np(a.dtype), kind="ExternalInput").ap()
    out = nc.dram_tensor("out_0", (1, SEQ, D), F32, kind="ExternalOutput").ap()
    build_program(nc, args, out)
    r = _run(nc, [arrays], core_ids=[0])
    return r.results[0]["out_0"]
```

```python
from contextlib import ExitStack

import numpy as np

import concourse.bass as bass
from concourse import mybir
from concourse.alu_op_type import AluOpType as ALU

F32 = mybir.dt.float32
F32R = mybir.dt.float32r
I32 = mybir.dt.int32
U32 = mybir.dt.uint32
ACT = mybir.ActivationFunctionType
AX = mybir.AxisListType
P = 128
BANK = 512
EPS = 1e-6

D = 1024
KD = D // P
SEQ = 512
CTX = 256
NT = SEQ // P
NC = CTX // P
ALL = NT + NC
CHUNK = 64
NEG = -1e30


class Stage(ExitStack):

    def __init__(self, nc, name):
        super().__init__()
        self.nc, self.name, self.sems = nc, name, []

    def sb(self, name, shape, dt=F32):
        return self.enter_context(self.nc.sbuf_tensor(f"{self.name}_{name}", shape, dt))

    def sem(self, name):
        sem = self.enter_context(self.nc.semaphore(f"{self.name}_{name}"))
        self.sems.append(sem.num)
        return sem

    def block(self):
        return self.enter_context(self.nc.Block())

    def __exit__(self, *error):
        done = super().__exit__(*error)
        low = high = None
        for n in sorted(self.sems) + [None]:
            if n is not None and high is not None and n == high + 1:
                high = n
                continue
            if low is not None:
                self.nc.gpsimd.sem_clear(range(low, high + 1))
            low = high = n
        return done


def in_order(eng, sem):
    count = [0]

    def link(ins):
        count[0] += 1
        ins.then_inc(sem, 1)
        eng.wait_ge(sem, count[0])

    return link


def constants():
    p = np.arange(P)[:, None]
    f = np.arange(P)[None, :]
    same = (p // CHUNK) == (f // CHUNK)
    parts = {
        "ident": p == f,
        "tri_fwd": same & (p <= f),
        "tri_bwd": same & (p >= f),
        "before": p < f,
        "ones": np.ones((P, P)),
        "same_chunk": same,
        "strict": same & (p < f),
    }
    for n in range(1, 7):
        s = 2**n
        parts[f"merge{n}"] = (p // s == f // s) & (p % s < s // 2) & (f % s >= s // 2)
    parts["add_incl"] = np.where(same & (p <= f), 0.0, NEG)
    blocks = []
    for back in (3, 2, 1, 0):
        dist = p - f + P * back
        times = ((dist >= 0) & (dist <= 128)).astype(int)
        for dil in (4, 16):
            times = times + ((dist >= 0) & (dist % dil == 0) & (dist <= 128 * dil))
        blocks.append(np.where(times > 0, np.log(np.maximum(times, 1)), NEG))
    parts["windows"] = np.concatenate(blocks, axis=1)
    tok = np.arange(SEQ)
    pos = np.stack([tok // 64, tok % 64], axis=-1).astype(np.float32)
    inv = np.power(np.float32(10000.0), -np.arange(16, dtype=np.float32) / np.float32(16))
    ang = (pos[:, :, None] * inv).astype(np.float32).reshape(SEQ, 32)
    rope = np.concatenate([np.cos(ang), np.sin(ang)], axis=1)
    parts["rope"] = rope.reshape(NT, P, 64).transpose(1, 0, 2).reshape(P, NT * 64)
    parts["iota"] = np.broadcast_to(np.arange(64.0)[None, :], (P, 64))
    at, cols, data = {}, 0, []
    for name, a in parts.items():
        a = np.ascontiguousarray(a, dtype=np.float32)
        at[name] = (cols, a.shape[1])
        cols += a.shape[1]
        data.append(a)
    return np.concatenate(data, axis=1), at


CONST_DATA, CONST_AT = constants()


class Core:

    def __init__(self, nc, args, es):
        self.nc, self.a = nc, args
        self.table = es.enter_context(nc.sbuf_tensor("const_table", [P, CONST_DATA.shape[1]], F32))
        self.x = es.enter_context(nc.sbuf_tensor("x_tokens", [P, NT, D], F32))
        self.gains = es.enter_context(nc.sbuf_tensor("norm_gain_cols", [P, 2 * 6 * KD], F32))
        self.rs = es.enter_context(nc.sbuf_tensor("x_inverse_rms", [P, NT], F32))
        self.ps = es.enter_context(nc.psum_tensor("psum_banks", [P, 8, BANK], F32))
        self.expert_rows = self.scratch("expert_rows", [N_BLOCKS * P, D])
        self.scattered = es.enter_context(nc.semaphore("rows_scattered"))
        self.experts_in = es.enter_context(nc.semaphore("first_experts_in"))
        self.gathered = es.enter_context(nc.semaphore("rows_gathered"))

    def c(self, name):
        at, n = CONST_AT[name]
        return self.table[:, at:at + n]

    def norm_gain(self, layer, n):
        at = (layer * 6 + n) * KD
        return self.gains[:, at:at + KD]

    def scratch(self, name, shape, dt=F32):
        return self.nc.dram_tensor(name, shape, dt, kind="Internal").ap()


def load_all(k, name, loads):
    with Stage(k.nc, name) as s:
        loaded = s.sem("loaded")
        block = s.block()

        @block.sync
        def _(sp):
            for dst, src in loads:
                sp.dma_start(dst, src, allow_slow_non_contiguous=True).then_inc(loaded, 16)
            sp.wait_ge(loaded, 16 * len(loads))


def columns(row, n=KD):
    return row.rearrange("(k p) -> p k", p=P)


def modulation(k, mod_rows):
    nc, a = k.nc, k.a
    n_chunks = 6 * D // BANK
    with Stage(nc, "mod") as s:
        cond = s.sb("cond", [P, KD, 2])
        act = s.sb("act", [P, KD, 2])
        bias = s.sb("bias", [2, 6 * D])
        row = s.sb("row", [2, 6 * D])
        w = s.sb("w", [P, 3, KD, BANK])
        cond_in, w_in = s.sem("cond_in"), [s.sem(f"w_in{j}") for j in range(3)]
        act_ok, mm, bank_free, out = s.sem("act"), s.sem("mm"), s.sem("bank_free"), s.sem("out")
        block = s.block()
        wv = a["w_ada"][0].rearrange("(k p) n -> p k n", p=P)

        @block.sync
        def _(sp):
            sp.dma_start(cond[:, :, 0], columns(a["c"][0]), allow_slow_non_contiguous=True).then_inc(cond_in, 16)
            sp.dma_start(cond[:, :, 1], columns(a["c_ctx"]), allow_slow_non_contiguous=True).then_inc(cond_in, 16)
            for r in range(2):
                sp.dma_start(bias[r:r + 1, :], a["b_ada"]).then_inc(cond_in, 16)
            for n in range(3):
                sp.dma_start(w[:, n], wv[:, :, n * BANK:(n + 1) * BANK]).then_inc(w_in[n], 16)
            with sp.Fori(1, n_chunks // 3) as i:
                for j in range(3):
                    sp.wait_ge(mm, i * 3 + (j - 2))
                    sp.dma_start(w[:, j], wv[:, :, bass.ds((i * 3 + j) * BANK, BANK)]).then_inc(w_in[j], 16)
            sp.wait_ge(bank_free, 2 + n_chunks)
            sp.dma_start(mod_rows, row[:]).then_inc(out, 16)
            sp.wait_ge(out, 16)

        @block.scalar
        def _(eng):
            eng.wait_ge(cond_in, 64)
            nc.scalar.activation(act[:], cond[:], ACT.Silu).then_inc(act_ok, 1)

        @block.tensor
        def _(pe):
            pe.wait_ge(act_ok, 1)
            with pe.Fori(0, n_chunks // 3) as i:
                for j in range(3):
                    pe.wait_ge(w_in[j], (i + 1) * 16)
                    pe.wait_ge(bank_free, i * 3 + j + 1)
                    b = k.ps[0:2, j, :]
                    for t in range(KD):
                        last = nc.tensor.matmul(b, act[:, t, :], w[:, j, t, :], start=t == 0, stop=t == KD - 1)
                    last.then_inc(mm, 1)

        @block.vector
        def _(v):
            v.wait_ge(cond_in, 64)
            v.sem_inc(bank_free, 2)
            with v.Fori(0, n_chunks // 3) as i:
                for j in range(3):
                    v.wait_ge(mm, i * 3 + j + 1)
                    cols = bass.ds((i * 3 + j) * BANK, BANK)
                    nc.vector.tensor_tensor(row[:, cols], k.ps[0:2, j, :], bias[:, cols], ALU.add).then_inc(bank_free, 1)


def norm_rows(k, name, groups, width, eps=EPS, sums=None):
    nc = k.nc
    n = len(groups)
    with Stage(nc, name) as s:
        junk = s.sb("junk", [P, 2, width])
        ss = s.sb("ss", [P, n]) if sums is None else sums
        rs = s.sb("rs", [P, n])
        squares, root, chain = s.sem("squares"), s.sem("root"), s.sem("chain")
        block = s.block()

        @block.scalar
        def _(eng):
            for g, (src, _) in enumerate(groups if sums is None else []):
                if g > 1:
                    eng.wait_ge(squares, g - 1)
                nc.scalar.activation(junk[:, g % 2, :], src, ACT.Square, accum_out=ss[:, g:g + 1]).then_inc(squares, 1)
            eng.wait_ge(chain, 1)
            nc.scalar.activation(rs[:], ss[:], ACT.Sqrt).then_inc(root, 1)
            eng.wait_ge(chain, 2)
            for g in range(1, n, 2):
                nc.scalar.activation(groups[g][1], groups[g][0], ACT.Copy, scale=rs[:, g:g + 1])

        @block.vector
        def _(v):
            link = in_order(v, chain)
            if sums is None:
                v.wait_ge(squares, n)
            link(nc.vector.tensor_scalar(ss[:], ss[:], 1.0 / width, eps, ALU.mult, ALU.add))
            v.wait_ge(root, 1)
            link(nc.vector.reciprocal(rs[:], rs[:]))
            for g in range(0, n, 2):
                nc.vector.tensor_scalar(groups[g][1], groups[g][0], rs[:, g:g + 1], None, ALU.mult)


class Split:

    def __init__(self, high, low):
        self.high, self.low = high, low

    def __getitem__(self, at):
        return Split(self.high[at], self.low[at])


def split_sb(stack, nc, name, shape):
    return Split(*(stack.enter_context(nc.sbuf_tensor(f"{name}_{part}", shape, F32R)) for part in ("high", "low")))


def product(nc, out, lhs, rhs, start, stop):
    nc.tensor.matmul(out, lhs.high, rhs.high, start=start, stop=False, skip_group_check=True)
    nc.tensor.matmul(out, lhs.high, rhs.low, start=False, stop=False, skip_group_check=True)
    return nc.tensor.matmul(out, lhs.low, rhs.high, start=False, stop=stop, skip_group_check=True)


def load_ahead(sp, loads, loaded):
    for dst, src in loads:
        sp.dma_start(dst, src).then_inc(loaded, 16)
    if loads:
        sp.wait_ge(loaded, 16 * len(loads))


def turn(k, name, jobs, tiles, ahead=()):
    nc = k.nc
    cols = tiles * P
    split = isinstance(jobs[0][1], Split)
    with Stage(nc, name) as s:
        turned, out_v, out_s = s.sem("turned"), s.sem("out_v"), s.sem("out_s")
        whole_ok = s.sem("whole_ok")
        whole = s.sb("whole", [P, 2, cols]) if split and jobs[0][3] is not None else None
        ahead_in = s.sem("ahead_in")
        block = s.block()

        @block.sync
        def _(sp):
            load_ahead(sp, ahead, ahead_in)

        @block.tensor
        def _(pe):
            for i, (sources, _, _, _) in enumerate(jobs):
                if i >= 8:
                    if split:
                        pe.wait_ge(out_v, i - 7)
                    else:
                        pe.wait_ge(out_s if i % 2 else out_v, (i - 8) // 2 + 1)
                for t in range(tiles):
                    src = sources[t]
                    last = nc.tensor.transpose(k.ps[:, i % 8, t * P:(t + 1) * P], src, k.c("ident"))
                last.then_inc(turned, 1)

        @block.vector
        def _(v):
            for i in range(0, len(jobs), 1 if split else 2):
                _, dst, gain, shift = jobs[i]
                bank = k.ps[:, i % 8, 0:cols]
                if split:
                    v.wait_ge(out_s, i + 1)
                    high = dst.high.bitcast(F32)
                    if shift is not None:
                        nc.vector.tensor_scalar(whole[:, i % 2, :], bank, gain, shift, ALU.mult, ALU.add).then_inc(whole_ok, 1)
                        v.wait_ge(whole_ok, i + 1)
                        nc.vector.tensor_tensor(dst.low, whole[:, i % 2, :], high, ALU.subtract).then_inc(out_v, 1)
                    elif gain is not None:
                        nc.vector.scalar_tensor_tensor(out=dst.low, in0=bank, scalar=gain, in1=high, op0=ALU.mult,
                                                       op1=ALU.subtract).then_inc(out_v, 1)
                    else:
                        nc.vector.tensor_tensor(dst.low, bank, high, ALU.subtract).then_inc(out_v, 1)
                    continue
                v.wait_ge(turned, i + 1)
                if gain is None:
                    nc.vector.tensor_copy(dst, bank).then_inc(out_v, 1)
                elif shift is None:
                    nc.vector.tensor_scalar(dst, bank, gain, None, ALU.mult).then_inc(out_v, 1)
                else:
                    nc.vector.tensor_scalar(dst, bank, gain, shift, ALU.mult, ALU.add).then_inc(out_v, 1)

        @block.scalar
        def _(eng):
            for i in range(0 if split else 1, len(jobs), 1 if split else 2):
                _, dst, gain, shift = jobs[i]
                eng.wait_ge(turned, i + 1)
                nc.scalar.activation(dst.high if split else dst, k.ps[:, i % 8, 0:cols], ACT.Identity,
                                     bias=0.0 if shift is None else shift,
                                     scale=1.0 if gain is None else gain).then_inc(out_s, 1)


CHUNK_COLS = 256


class Conv:

    def __init__(self, taps, bias, at, tiles):
        self.taps, self.bias, self.at, self.tiles = taps, bias, at, tiles

    def tap(self, n, tile):
        return self.taps[:, bass.ds(tile + (n * self.tiles + self.at), 1)]

    def shift(self, tile):
        return 0.0 if self.bias is None else self.bias[:, bass.ds(tile + self.at, 1)]


def first_chunk(raw, w_dram, first=0):
    return [(raw[:], w_dram.rearrange("(k p) n -> p k n", p=P)[:, :, first:first + CHUNK_COLS])]


def project(k, name, x, w_dram, parts, raw=None, k_tiles=KD):
    nc = k.nc
    wv = w_dram.rearrange("(k p) n -> p k n", p=P)
    chunks = sum(part[1] for part in parts) // CHUNK_COLS
    convolved = any(len(part) > 4 for part in parts)
    with Stage(nc, name) as s:
        loaded = raw is not None
        if not loaded:
            raw = s.sb("w", [P, k_tiles, CHUNK_COLS])
        w = split_sb(s, nc, f"{name}_w", [P, 2, k_tiles, CHUNK_COLS])
        w_in, high_ok, low_ok, mm = s.sem("w_in"), s.sem("high_ok"), s.sem("low_ok"), s.sem("mm")
        free_v, free_s = s.sem("bank_free_v"), s.sem("bank_free_s")
        if convolved:
            late = s.sb("late", [P, 2, SEQ + 3])
            acc = s.sb("acc", [P, 2, SEQ])
            cleared, tapped, silu_ok = s.sem("cleared"), s.sem("tapped"), s.sem("silu_ok")
        block = s.block()

        class Part:

            def __init__(self, spec, before):
                self.first, cols, self.units, self.dest = spec[:4]
                self.conv = spec[4] if len(spec) > 4 else None
                n, U = cols // CHUNK_COLS, len(self.units)
                assert n % 2 == 0 and U % 2 == 0 and U <= 8 and (self.conv is None or U == 2)
                self.pairs = n // 2
                self.reads = (0, 2 * U) if self.conv else (U // 2, U // 2)
                self.chunks, self.done, self.freed, self.tiles = before.after if before else (0, 0, (0, 0), 0)
                self.after = (self.chunks + n, self.done + n * U,
                              tuple(f + (n + 1) * r for f, r in zip(self.freed, self.reads)),
                              self.tiles + (n * U if self.conv else 0))
                self.final = self.after[0] == chunks

            def read(self, c, u):
                odd = 1 if self.conv else u % 2
                per = self.reads[odd]
                nth = 2 * (u + 1) if self.conv else u // 2 + 1
                return odd, c * per + (self.freed[odd] + per + nth)

        walk = []
        for spec in parts:
            walk.append(Part(spec, walk[-1] if walk else None))

        def width(unit):
            return CHUNK_COLS if unit[0] == "tokens" else unit[3]

        @block.sync
        def _(sp):
            for part in walk:
                if part.chunks:
                    sp.wait_ge(low_ok, part.chunks)
                if loaded and not part.chunks:
                    sp.sem_inc(w_in, 16)
                else:
                    sp.dma_start(raw[:], wv[:, :, part.first:part.first + CHUNK_COLS]).then_inc(w_in, 16)
                with sp.Fori(1, 2 * part.pairs) as c:
                    sp.wait_ge(low_ok, c + part.chunks)
                    sp.dma_start(raw[:], wv[:, :, bass.ds(c * CHUNK_COLS + part.first, CHUNK_COLS)]).then_inc(w_in, 16)

        @block.tensor
        def _(pe):
            pe.sem_inc(mm, 1)
            for part in walk:
                before = part.freed
                for sem, count, reads in zip((free_v, free_s), before, part.reads):
                    if count and not reads:
                        pe.wait_ge(sem, count)
                with pe.Fori(0, part.pairs) as i:
                    for j in range(2):
                        c = i * 2 + j
                        pe.wait_ge(low_ok, c + (part.chunks + 1))
                        for u, unit in enumerate(part.units):
                            odd, count = part.read(c, u)
                            pe.wait_ge(free_s if odd else free_v, count - part.reads[odd])
                            out = k.ps[:, u, 0:width(unit)]
                            for q in range(k_tiles):
                                if unit[0] == "tokens":
                                    a, b = x[:, q, unit[1] * P:(unit[1] + 1) * P], w[:, j, q, :]
                                else:
                                    _, m, at, n = unit
                                    a, b = w[:, j, q, m * P:(m + 1) * P], x[:, q, at:at + n]
                                last = product(nc, out, a, b, q == 0, q == k_tiles - 1)
                            last.then_inc(mm, 1)

        def run(eng, odd, split, convolve):
            free = free_s if odd else free_v
            split(0, 0, None)
            for part in walk:
                U = len(part.units)

                def copies(c):
                    for u in range(U):
                        if part.conv:
                            convolve(part, c, u)
                        elif u % 2 == odd:
                            eng.wait_ge(mm, c * U + (part.done + u + 2))
                            source = k.ps[:, u, 0:width(part.units[u])]
                            if odd:
                                nc.scalar.activation(part.dest(c, part.units[u]), source, ACT.Copy).then_inc(free, 1)
                            else:
                                nc.vector.tensor_copy(part.dest(c, part.units[u]), source).then_inc(free, 1)

                if part.reads[odd]:
                    if part.freed[odd]:
                        eng.wait_ge(free, part.freed[odd])
                    eng.sem_inc(free, part.reads[odd])
                loops = part.pairs - 1 if part.final else part.pairs
                if loops:
                    with eng.Fori(0, loops) as i:
                        for j in range(2):
                            c = i * 2 + j
                            split(c + (part.chunks + 1), 1 - j, c * U + (part.done + 1))
                            copies(c)
                if part.final:
                    c = 2 * part.pairs - 2
                    split(c + part.chunks + 1, 1, c * U + part.done + 1)
                    copies(c)
                    copies(c + 1)

        @block.scalar
        def _(eng):
            def high(c, j, slot_free):
                eng.wait_ge(w_in, (c + 1) * 16)
                if slot_free is not None:
                    eng.wait_ge(mm, slot_free)
                nc.scalar.activation(w.high[:, j], raw[:], ACT.Copy).then_inc(high_ok, 1)

            def convolve(part, c, u):
                tile = c * 2 + u
                bank = k.ps[:, u, :]
                eng.wait_ge(mm, c * 2 + (part.done + u + 2))
                eng.wait_ge(silu_ok, tile + (part.tiles + 1))
                nc.scalar.activation(late[:, u, 3:], bank, ACT.Copy).then_inc(free_s, 1)
                nc.scalar.activation(acc[:, u, :], bank, ACT.Copy, scale=part.conv.tap(3, tile)).then_inc(free_s, 1)
                eng.wait_ge(tapped, tile * 3 + (part.tiles * 3 + 3))
                nc.scalar.activation(part.dest(c, part.units[u]), acc[:, u, :], ACT.Silu,
                                     bias=part.conv.shift(tile)).then_inc(silu_ok, 1)

            if convolved:
                eng.sem_inc(silu_ok, 2)
                eng.wait_ge(cleared, 1)
            run(eng, 1, high, convolve)

        @block.vector
        def _(v):
            def low(c, j, _):
                v.wait_ge(high_ok, c + 1)
                nc.vector.tensor_tensor(w.low[:, j], raw[:], w.high[:, j].bitcast(F32), ALU.subtract).then_inc(low_ok, 1)

            def convolve(part, c, u):
                tile = c * 2 + u
                v.wait_ge(free_s, part.read(c, u)[1])
                for n in range(3):
                    if n:
                        v.wait_ge(tapped, tile * 3 + (part.tiles * 3 + n))
                    nc.vector.scalar_tensor_tensor(out=acc[:, u, :], in0=late[:, u, n:n + SEQ], scalar=part.conv.tap(n, tile),
                                                   in1=acc[:, u, :], op0=ALU.mult, op1=ALU.add).then_inc(tapped, 1)

            if convolved:
                nc.vector.memset(late[:, :, 0:3], 0.0).then_inc(cleared, 1)
            run(v, 0, low, convolve)


def by_tokens(dst, at=0):
    return lambda c, unit: dst[:, unit[1], bass.ds(c * CHUNK_COLS + at, CHUNK_COLS)]


def token_units(tiles):
    return [("tokens", t) for t in range(tiles)]


def by_features(dst):
    per = CHUNK_COLS // P
    return lambda c, unit: dst[:, bass.ds(c * per + unit[1], 1), unit[2]:unit[2] + unit[3]].rearrange("p a n -> p (a n)")


def feature_units(spans):
    return [("features", m, at, n) for m in range(CHUNK_COLS // P) for at, n in spans]


def split_rows(k, name, src, dst):
    nc = k.nc
    with Stage(nc, name) as s:
        high_ok, low_ok = s.sem("high_ok"), s.sem("low_ok")
        block = s.block()

        @block.scalar
        def _(eng):
            nc.scalar.activation(dst.high, src, ACT.Copy).then_inc(high_ok, 1)

        @block.vector
        def _(v):
            v.wait_ge(high_ok, 1)
            nc.vector.tensor_tensor(dst.low, src, dst.high.bitcast(F32), ALU.subtract).then_inc(low_ok, 1)



DA_H, DA_QK, DA_V = 4, 64, 128
GLA_H, GLA_K, GLA_V, RANK = 4, 64, 128, 16
GLA_QK = GLA_H * GLA_K
TAU = 16.0
KEYS = SEQ + CTX
N_CH = KEYS // CHUNK
CTX_CH = CTX // CHUNK


def rope(k, eng, ops, tiles, a, b, products, turned):
    table = k.c("rope").rearrange("p (t n) -> p t n", t=NT)
    scratch = lambda v, half: v[:, half, :].rearrange("p (g a n) -> p g a n", a=2, n=16)
    for n, (t, x) in enumerate(tiles):
        xv = x.rearrange("p (g a h n) -> p g a h n", a=2, h=2, n=16)
        cos = table[:, t, 0:32].rearrange("p (a n) -> p a n", a=2).unsqueeze(1).to_broadcast([P, 16, 2, 16])
        sin = table[:, t, 32:64].rearrange("p (a n) -> p a n", a=2).unsqueeze(1).to_broadcast([P, 16, 2, 16])
        x1, x2 = xv[:, :, :, 0, :], xv[:, :, :, 1, :]
        if n:
            eng.wait_ge(turned, 2 * n)
        for half, (u, w) in enumerate(((x1, x2), (x2, x1))):
            ops.tensor_tensor(scratch(a, half), u, cos, ALU.mult).then_inc(products, 1)
            ops.tensor_tensor(scratch(b, half), w, sin, ALU.mult).then_inc(products, 1)
        eng.wait_ge(products, 4 * n + 4)
        for half, op in enumerate((ALU.subtract, ALU.add)):
            ops.tensor_tensor(xv[:, :, :, half, :], scratch(a, half), scratch(b, half), op).then_inc(turned, 1)


def gates(k, h, w_in, w2, gate_b, g, rotated):
    nc = k.nc
    first = 3 * 512 + 2 * GLA_QK + 2 * 512
    with Stage(nc, "gates") as s:
        raw = s.sb("w", [P, KD, P])
        w = split_sb(s, nc, "gates_w", [P, KD, P])
        w2b = s.sb("w2b", [2 * RANK + 1, 2 * GLA_QK])
        low = s.sb("low", [2 * RANK + 1, KEYS])
        na = s.sb("na", [P, ALL, 2 * GLA_QK])
        w_in_sem, cleared, mm, low_ok = s.sem("w_in"), s.sem("cleared"), s.sem("mm"), s.sem("low_ok")
        exped, w_high, w_low = s.sem("exped"), s.sem("w_high"), s.sem("w_low")
        zmm, zc, nab, lg, gd = s.sem("z_mm"), s.sem("z_copied"), s.sem("neg_abs"), s.sem("log"), s.sem("g_done")
        tiles = list(enumerate(rotated))
        turns = [(s.sb(f"rope_a{n}", [P, 2, 512]), s.sb(f"rope_b{n}", [P, 2, 512]),
                  s.sem(f"rope_products{n}"), s.sem(f"rope_ok{n}")) for n in range(2)]
        block = s.block()

        @block.gpsimd
        def _(pool):
            rope(k, pool, nc.gpsimd, tiles[0:2], *turns[0])

        @block.sync
        def _(sp):
            sp.wait_ge(cleared, 2)
            sp.dma_start(raw[:, :, 0:2 * RANK],
                         w_in.rearrange("(k p) n -> p k n", p=P)[:, :, first:first + 2 * RANK]).then_inc(w_in_sem, 16)
            for d in range(2):
                cols = slice(d * GLA_QK, (d + 1) * GLA_QK)
                sp.dma_start(w2b[d * RANK:(d + 1) * RANK, cols], w2[d]).then_inc(w_in_sem, 16)
                sp.dma_start(w2b[2 * RANK:2 * RANK + 1, cols], gate_b[d:d + 1, :]).then_inc(w_in_sem, 16)

        @block.tensor
        def _(pe):
            pe.wait_ge(w_low, 1)
            for b, (at, n) in enumerate(((0, 512), (512, 256))):
                for q in range(KD):
                    last = product(nc, k.ps[:, b, 0:n], w[:, q, :], h[:, q, at:at + n], q == 0, q == KD - 1)
                last.then_inc(mm, 1)
            pe.wait_ge(low_ok, 3)
            for t in range(ALL):
                nc.tensor.matmul(k.ps[:, 2 + t, :], low[:, t * P:(t + 1) * P], w2b[:], start=True, stop=True).then_inc(zmm, 1)

        @block.vector
        def _(v):
            nc.vector.memset(raw[:], 0.0).then_inc(cleared, 1)
            nc.vector.memset(w2b[:], 0.0).then_inc(cleared, 1)
            nc.vector.memset(low[2 * RANK:2 * RANK + 1, :], 1.0).then_inc(low_ok, 1)
            v.wait_ge(w_high, 1)
            nc.vector.tensor_tensor(w.low[:], raw[:], w.high[:].bitcast(F32), ALU.subtract).then_inc(w_low, 1)
            rope(k, v, nc.vector, tiles[2:4], *turns[1])
            for b, (at, n) in enumerate(((0, 512), (512, 256))):
                v.wait_ge(mm, b + 1)
                nc.vector.tensor_copy(low[0:2 * RANK, at:at + n], k.ps[0:2 * RANK, b, 0:n]).then_inc(low_ok, 1)
            for t in range(ALL):
                v.wait_ge(zc, t + 1)
                nc.vector.scalar_tensor_tensor(out=na[:, t, :], in0=g[:, t, :], scalar=-1.0, in1=g[:, t, :],
                                               op0=ALU.mult, op1=ALU.min).then_inc(nab, 1)
            v.wait_ge(lg, 1)
            nc.vector.scalar_tensor_tensor(out=g[:], in0=g[:], scalar=0.0, in1=na[:], op0=ALU.min,
                                           op1=ALU.subtract).then_inc(gd, 1)

        @block.scalar
        def _(eng):
            eng.wait_ge(w_in_sem, 80)
            nc.scalar.activation(w.high[:], raw[:], ACT.Copy).then_inc(w_high, 1)
            for t in range(ALL):
                eng.wait_ge(zmm, t + 1)
                nc.scalar.activation(g[:, t, :], k.ps[:, 2 + t, :], ACT.Copy).then_inc(zc, 1)
            eng.wait_ge(nab, ALL)
            nc.scalar.activation(na[:], na[:], ACT.Exp).then_inc(exped, 1)
            eng.wait_ge(exped, 1)
            nc.scalar.activation(na[:], na[:], ACT.Ln, bias=1.0).then_inc(lg, 1)


def gla_prepare(k, d, pair, g, qk_t, q_dec, k_inv, k_end_t, decay):
    nc = k.nc
    tri = k.c("tri_bwd" if d else "tri_fwd")
    end = 0 if d else CHUNK - 1
    with Stage(nc, f"gla_prep{d}{pair}") as s:
        b = s.sb("b", [P, KEYS])
        diff = s.sb("diff", [P, KEYS])
        e_q, e_k = s.sb("e_q", [P, SEQ]), s.sb("e_k", [P, SEQ])
        mm, bc, dd, ee, out = s.sem("mm"), s.sem("b_copied"), s.sem("diff_ok"), s.sem("exps"), s.sem("out")
        block = s.block()
        chunks = b[:].rearrange("p (c n) -> p c n", n=CHUNK)
        ends = chunks[:, :, end:end + 1]

        @block.tensor
        def _(pe):
            for t in range(ALL):
                at = 0 if t < NC else 1
                col = (t - (NC if at else 0)) * P
                last = nc.tensor.matmul(k.ps[:, at, col:col + P],
                                        g[:, t, d * GLA_QK + pair * P:d * GLA_QK + (pair + 1) * P], tri,
                                        start=True, stop=True)
            last.then_inc(mm, 1)

        @block.scalar
        def _(eng):
            eng.wait_ge(mm, 1)
            nc.scalar.activation(b[:, 0:CTX], k.ps[:, 0, 0:CTX], ACT.Copy, scale=1.0 / TAU).then_inc(bc, 1)
            nc.scalar.activation(b[:, CTX:KEYS], k.ps[:, 1, 0:SEQ], ACT.Copy, scale=1.0 / TAU).then_inc(bc, 1)
            eng.wait_ge(bc, 2)
            nc.scalar.activation(e_q[:], b[:, CTX:KEYS], ACT.Exp).then_inc(ee, 1)
            nc.scalar.activation(e_k[:], b[:, CTX:KEYS], ACT.Exp, scale=-1.0).then_inc(ee, 1)
            nc.scalar.activation(decay.unsqueeze(2), ends, ACT.Exp).then_inc(ee, 1)
            eng.wait_ge(dd, 1)
            nc.scalar.activation(diff[:], diff[:], ACT.Exp).then_inc(ee, 1)

        @block.vector
        def _(v):
            v.wait_ge(bc, 2)
            nc.vector.tensor_tensor(diff[:].rearrange("p (c n) -> p c n", n=CHUNK),
                                    ends.to_broadcast([P, N_CH, CHUNK]), chunks, ALU.subtract).then_inc(dd, 1)
            v.wait_ge(ee, 2)
            nc.vector.scalar_tensor_tensor(out=q_dec, in0=qk_t[:, pair, CTX:KEYS], scalar=GLA_K ** -0.5, in1=e_q[:],
                                           op0=ALU.mult, op1=ALU.mult).then_inc(out, 1)
            nc.vector.tensor_tensor(k_inv, qk_t[:, 2 + pair, CTX:KEYS], e_k[:], ALU.mult).then_inc(out, 1)
            v.wait_ge(ee, 4)
            nc.vector.tensor_tensor(k_end_t, qk_t[:, 2 + pair, :], diff[:], ALU.mult).then_inc(out, 1)


def gla_states(k, d, k_end, vals, decay, states):
    nc = k.nc
    order = scan_order(d)
    with Stage(nc, f"gla_state{d}") as s:
        mm, chain = s.sem("mm"), s.sem("chain")
        cleared = s.sem("cleared")
        block = s.block()

        @block.tensor
        def _(pe):
            for n, c in enumerate(order[:-1]):
                t, half = divmod(c, 2)
                rows = slice(half * CHUNK, (half + 1) * CHUNK)
                if n >= 8:
                    pe.wait_ge(chain, 2 * (n - 8) + 4)
                for pair in range(2):
                    for hh in range(2):
                        head = pair * 2 + hh
                        last = nc.tensor.matmul(k.ps[hh * GLA_K:(hh + 1) * GLA_K, n % 8, pair * P:(pair + 1) * P],
                                                k_end[pair][rows, t, hh * GLA_K:(hh + 1) * GLA_K],
                                                vals[rows, t, head * P:(head + 1) * P], start=True, stop=True)
                last.then_inc(mm, 1)

        @block.vector
        def _(v):
            for pair in range(2):
                nc.vector.memset(states[pair][:, 0, :], 0.0).then_inc(chain, 1)
            for n, c in enumerate(order[:-1]):
                v.wait_ge(mm, n + 1)
                v.wait_ge(chain, 2 * n + 2)
                for pair in range(2):
                    nc.vector.scalar_tensor_tensor(out=states[pair][:, n + 1, :], in0=states[pair][:, n, :],
                                                   scalar=decay[pair][:, c:c + 1], in1=k.ps[:, n % 8, pair * P:(pair + 1) * P],
                                                   op0=ALU.mult, op1=ALU.add).then_inc(chain, 1)


def scan_order(d):
    if d == 0:
        return list(range(N_CH))
    return list(range(CTX_CH))[::-1] + list(range(CTX_CH, N_CH))[::-1]


def gla_output(k, q_dec, k_inv, vals, states, out):
    nc = k.nc
    orders = [scan_order(d) for d in range(2)]
    with Stage(nc, "gla_out") as s:
        sc = s.sb("scores", [P, 2, GLA_H * P])
        score, masked, used, done, copied = s.sem("score"), s.sem("masked"), s.sem("used"), s.sem("done"), s.sem("copied")
        block = s.block()
        units = [(t, d) for t in range(NT) for d in range(2)]

        def region(first, h):
            return k.ps[:, first + h % 2, (h // 2) * P:(h // 2 + 1) * P]

        @block.tensor
        def _(pe):
            def scores(n):
                t, d = units[n]
                if n >= 2:
                    pe.wait_ge(masked, n - 1)
                for h in range(GLA_H):
                    rows = slice((h % 2) * GLA_K, (h % 2 + 1) * GLA_K)
                    last = nc.tensor.matmul(region(2 * (n % 2), h), k_inv[d][h // 2][rows, t * P:(t + 1) * P],
                                            q_dec[d][h // 2][rows, t * P:(t + 1) * P], start=True, stop=True)
                last.then_inc(score, 1)

            scores(0)
            for n, (t, d) in enumerate(units):
                if n + 1 < len(units):
                    scores(n + 1)
                pe.wait_ge(masked, n + 1)
                if t >= 2 and d == 0:
                    pe.wait_ge(copied, t - 1)
                for h in range(GLA_H):
                    rows = slice((h % 2) * GLA_K, (h % 2 + 1) * GLA_K)
                    o = region(4 + 2 * (t % 2), h)
                    at = (h % 2) * 2 * P + (h // 2) * P
                    nc.tensor.matmul(o, sc[:, n % 2, at:at + P], vals[:, NC + t, h * P:(h + 1) * P],
                                     start=d == 0 and h < 2, stop=False, skip_group_check=True)
                    for half in range(2):
                        c = 2 * t + half
                        last = nc.tensor.matmul(o[half * CHUNK:(half + 1) * CHUNK, :],
                                                q_dec[d][h // 2][rows, c * CHUNK:(c + 1) * CHUNK],
                                                states[d][h // 2][rows, orders[d].index(CTX_CH + c), :],
                                                start=False, stop=d == 1, skip_group_check=True)
                last.then_inc(used, 1)

        @block.vector
        def _(v):
            for n, (t, d) in enumerate(units):
                v.wait_ge(score, n + 1)
                if n >= 2:
                    v.wait_ge(used, n - 1)
                tri = k.c("tri_bwd" if d else "tri_fwd")
                nc.vector.tensor_tensor(sc[:, n % 2, :].rearrange("p (b h n) -> p b h n", b=2, h=2),
                                        k.ps[:, 2 * (n % 2):2 * (n % 2) + 2, 0:2 * P].rearrange("p b (h n) -> p b h n", h=2),
                                        tri.unsqueeze(1).unsqueeze(1).to_broadcast([P, 2, 2, P]), ALU.mult).then_inc(masked, 1)

        @block.scalar
        def _(eng):
            for t in range(NT):
                eng.wait_ge(used, 2 * t + 2)
                first = 4 + 2 * (t % 2)
                nc.scalar.activation(out(t).rearrange("p (h b n) -> p b h n", b=2, h=2),
                                     k.ps[:, first:first + 2, 0:2 * P].rearrange("p b (h n) -> p b h n", h=2),
                                     ACT.Copy).then_inc(copied, 1)


def diff_attention(k, q_t, k_t, vals, lam_rows, lambda_init, out, zeroed):
    nc = k.nc
    scale = DA_QK ** -0.5
    KT = KEYS // P
    units = [(h, t) for h in range(DA_H) for t in range(NT)]
    U = len(units)
    with Stage(nc, "diff_attn") as s:
        p = s.sb("p", [P, 2, 2, KEYS])
        a = s.sb("a", [P, 2, KEYS])
        at_ = s.sb("a_t", [P, 2, KEYS])
        mx = s.sb("mx", [P, 2 * U])
        den = s.sb("den", [P, 2 * U])
        lam = s.sb("lam", [P, 4])
        prod = s.sb("prod", [P, 2, DA_QK])
        zeros, zeros_ok, zeros_out = s.sb("zeros", [P, 3, D]), s.sem("zeros_ok"), s.sem("zeros_out")
        small, lam_ok, lam_exp = s.sem("small"), s.sem("lam_sums"), s.sem("lam_exp")
        score, biased, soft = s.sem("score"), s.sem("bias"), s.sem("soft")
        comb, turned, a_in, pv, outc = s.sem("combined"), s.sem("turned"), s.sem("a_t_in"), s.sem("pv"), s.sem("out")
        block = s.block()

        @block.gpsimd
        def _(pool):
            nc.gpsimd.memset(zeros[:], 0.0).then_inc(zeros_ok, 1)

        @block.sync
        def _(sp):
            groups = zeroed.rearrange("(g t p) d -> g p t d", p=P, t=3)
            sp.wait_ge(zeros_ok, 1)
            for n in range(groups.shape[0]):
                sp.dma_start(groups[n], zeros[:]).then_inc(zeros_out, 16)
            sp.wait_ge(zeros_out, 16 * groups.shape[0])

        @block.tensor
        def _(pe):
            def scores(u):
                h, t = units[u]
                for m in range(2):
                    n = 2 * u + m
                    if n >= 2:
                        pe.wait_ge(soft, n - 1)
                    rows = slice(m * DA_QK, (m + 1) * DA_QK)
                    for b, (at, w) in enumerate(((0, 512), (512, KEYS - 512))):
                        last = nc.tensor.matmul(k.ps[:, 2 * m + b, 0:w], q_t[rows, h, t * P:(t + 1) * P],
                                                k_t[rows, h, at:at + w], start=True, stop=True)
                    last.then_inc(score, 1)

            scores(0)
            for u in range(U + 1):
                if u + 1 < U:
                    scores(u + 1)
                if u:
                    w = u - 1
                    h = units[w][0]
                    pe.wait_ge(a_in, w + 1)
                    if w >= 2:
                        pe.wait_ge(outc, w - 1)
                    for q in range(KT):
                        last = nc.tensor.matmul(k.ps[:, 6 + w % 2, 0:P], at_[:, w % 2, q * P:(q + 1) * P],
                                                vals[:, q, h * P:(h + 1) * P], start=q == 0, stop=q == KT - 1)
                    last.then_inc(pv, 1)
                if u < U:
                    pe.wait_ge(comb, u + 1)
                    for q in range(KT):
                        b, col = divmod(q, 4)
                        last = nc.tensor.transpose(k.ps[:, 4 + b, col * P:(col + 1) * P], a[:, u % 2, q * P:(q + 1) * P], k.c("ident"))
                    last.then_inc(turned, 1)

        def banks(m):
            return k.ps[:, 2 * m:2 * m + 2, :].rearrange("p b n -> p (b n)")[:, 0:KEYS]

        @block.scalar
        def _(eng):
            eng.wait_ge(lam_ok, 2)
            nc.scalar.activation(lam[:, 2:4], lam[:, 0:2], ACT.Exp).then_inc(lam_exp, 1)
            for u in range(U + 1):
                if u < U:
                    for m in range(2):
                        n = 2 * u + m
                        eng.wait_ge(biased, n + 1)
                        if u >= 2:
                            eng.wait_ge(comb, u - 1)
                        nc.scalar.activation(p[:, u % 2, m, :], banks(m), ACT.Exp, bias=mx[:, n:n + 1], scale=scale,
                                             accum_out=den[:, n:n + 1]).then_inc(soft, 1)
                if u:
                    w = u - 1
                    eng.wait_ge(turned, w + 1)
                    if w >= 2:
                        eng.wait_ge(pv, w - 1)
                    nc.scalar.activation(at_[:, w % 2, :], k.ps[:, 4:6, :].rearrange("p b n -> p (b n)")[:, 0:KEYS],
                                         ACT.Copy).then_inc(a_in, 1)

        @block.vector
        def _(v):
            link = in_order(v, small)
            for i in range(2):
                link(nc.vector.tensor_tensor(prod[:, i, :], lam_rows[:, 2 * i, :], lam_rows[:, 2 * i + 1, :], ALU.mult))
            for i in range(2):
                nc.vector.tensor_reduce(lam[:, i:i + 1], prod[:, i, :], AX.X, ALU.add).then_inc(lam_ok, 1)
            v.wait_ge(lam_exp, 1)
            link(nc.vector.tensor_tensor(lam[:, 0:1], lam[:, 3:4], lam[:, 2:3], ALU.subtract))
            link(nc.vector.tensor_scalar(lam[:, 0:1], lam[:, 0:1], lambda_init, None, ALU.subtract))

            def maxima(u):
                for m in range(2):
                    n = 2 * u + m
                    v.wait_ge(score, n + 1)
                    link(nc.vector.tensor_reduce(mx[:, n:n + 1], banks(m), AX.X, ALU.max))
                    nc.vector.tensor_scalar(mx[:, n:n + 1], mx[:, n:n + 1], -scale, None, ALU.mult).then_inc(biased, 1)

            def copy_out(u):
                h, t = units[u]
                v.wait_ge(pv, u + 1)
                nc.vector.tensor_copy(out(t)[:, h * P:(h + 1) * P], k.ps[:, 6 + u % 2, 0:P]).then_inc(outc, 1)

            maxima(0)
            for u in range(U):
                if u + 1 < U:
                    maxima(u + 1)
                v.wait_ge(soft, 2 * u + 2)
                link(nc.vector.reciprocal(den[:, 2 * u:2 * u + 2], den[:, 2 * u:2 * u + 2]))
                link(nc.vector.tensor_tensor(den[:, 2 * u + 1:2 * u + 2], den[:, 2 * u + 1:2 * u + 2], lam[:, 0:1], ALU.mult))
                if u >= 2:
                    v.wait_ge(turned, u - 1)
                link(nc.vector.tensor_scalar(a[:, u % 2, :], p[:, u % 2, 0, :], den[:, 2 * u:2 * u + 1], None, ALU.mult))
                nc.vector.scalar_tensor_tensor(out=a[:, u % 2, :], in0=p[:, u % 2, 1, :], scalar=den[:, 2 * u + 1:2 * u + 2],
                                               in1=a[:, u % 2, :], op0=ALU.mult, op1=ALU.add).then_inc(comb, 1)
                if u:
                    copy_out(u - 1)
            copy_out(U - 1)


def norm_heads(k, name, x, groups, width, mult=None, eps=EPS):
    nc = k.nc
    with Stage(nc, name) as s:
        sq = s.sb("sq", [P, groups, width])
        ss, rs = s.sb("ss", [P, groups]), s.sb("rs", [P, groups])
        squared, chain, root = s.sem("squared"), s.sem("chain"), s.sem("root")
        block = s.block()

        @block.scalar
        def _(eng):
            nc.scalar.activation(sq[:], x, ACT.Square).then_inc(squared, 1)
            eng.wait_ge(chain, 2)
            nc.scalar.activation(rs[:], ss[:], ACT.Sqrt).then_inc(root, 1)

        @block.vector
        def _(v):
            link = in_order(v, chain)
            v.wait_ge(squared, 1)
            link(nc.vector.tensor_reduce(ss[:], sq[:], AX.X, ALU.add))
            link(nc.vector.tensor_scalar(ss[:], ss[:], 1.0 / width, eps, ALU.mult, ALU.add))
            v.wait_ge(root, 1)
            link(nc.vector.reciprocal(rs[:], rs[:]))
            link(nc.vector.tensor_tensor(x, x, rs[:].unsqueeze(2).to_broadcast([P, groups, width]), ALU.mult))
            for part, factor in mult or []:
                link(nc.vector.tensor_tensor(part, part, factor, ALU.mult))


def silu_rows(k, name, parts):
    nc = k.nc
    with Stage(nc, name) as s:
        done = s.sem("done")
        block = s.block()

        @block.scalar
        def _(eng):
            for x in parts:
                nc.scalar.activation(x, x, ACT.Silu).then_inc(done, 1)


def residual(k, name, y, gain):
    nc = k.nc
    with Stage(nc, name) as s:
        chain = s.sem("chain")
        block = s.block()

        @block.vector
        def _(v):
            link = in_order(v, chain)
            factor = gain.unsqueeze(1).to_broadcast([P, NT, D])
            link(nc.vector.tensor_tensor(y, y, factor, ALU.mult))
            link(nc.vector.tensor_tensor(k.x[:], k.x[:], y, ALU.add))


def first_mixer(k, es, mod_rows):
    nc, a = k.nc, k.a
    w_in = a["w_in"][0]
    q_dec = [[None] * 2 for _ in range(2)]
    outer = es.enter_context(ExitStack())

    def sb(stack, name, shape):
        return stack.enter_context(nc.sbuf_tensor(name, shape, F32))

    tok = sb(outer, "tok", [P, ALL, 5 * 512])
    qk_t = sb(outer, "gla_qk_t", [P, 4, KEYS])
    g = sb(outer, "log_gates", [P, ALL, 2 * GLA_QK])
    with ExitStack() as st:
        h_t = split_sb(st, nc, "h_t", [P, KD, KEYS])
        cond = sb(st, "cond_cols", [P, 5, KD])
        with ExitStack() as st2:
            ctx = sb(st2, "ctx_rows", [P, NC, D])
            xn = sb(st2, "xn_all", [P, ALL, D])
            load_all(k, "ctx_in", [
                (ctx[:], a["ctx"][0].rearrange("(t p) d -> p t d", p=P)),
                (cond[:, 0, :], columns(a["norm_mix_g"][0])),
                (cond[:, 1, :], columns(mod_rows[0, 0:D])), (cond[:, 2, :], columns(mod_rows[0, D:2 * D])),
                (cond[:, 3, :], columns(mod_rows[1, 0:D])), (cond[:, 4, :], columns(mod_rows[1, D:2 * D]))])
            scale_gain(k, "cond", [(cond[:, 2, :], cond[:, 0, :]), (cond[:, 4, :], cond[:, 0, :])])
            norm_rows(k, "norm_mix", [(ctx[:, t, :], xn[:, t, :]) for t in range(NC)]
                      + [(k.x[:, t, :], xn[:, NC + t, :]) for t in range(NT)], D)
            turn(k, "turn_ctx", [([xn[:, t, i * P:(i + 1) * P] for t in range(NC)], h_t[:, i, 0:CTX],
                                  cond[:, 4, i:i + 1], cond[:, 3, i:i + 1]) for i in range(KD)], NC)
            turn(k, "turn_lat", [([xn[:, NC + t, i * P:(i + 1) * P] for t in range(NT)], h_t[:, i, CTX:KEYS],
                                  cond[:, 2, i:i + 1], cond[:, 1, i:i + 1]) for i in range(KD)], NT)
        project(k, "mix_in", h_t, w_in, [
            (0, 3 * 512, token_units(ALL), by_tokens(tok)),
            (3 * 512 + 2 * GLA_QK, 2 * 512, token_units(ALL), by_tokens(tok, 3 * 512)),
            (3 * 512, 2 * GLA_QK, feature_units([(0, 512), (512, 256)]), by_features(qk_t))])
        gates(k, h_t, w_in, a["gla_gate_w2"][0], a["gla_gate_b"][0], g, [tok[:, NC + t, 0:1024] for t in range(NT)])
    y = sb(outer, "mix", [P, NT, D])

    da_v = tok[:, :, 2 * 512:3 * 512]
    gla_v = tok[:, :, 3 * 512:4 * 512]
    with ExitStack() as st:
        q_t, k_t = sb(st, "q_t", [P, DA_H, SEQ]), sb(st, "k_t", [P, DA_H, KEYS])
        lam_rows = sb(st, "lam_rows", [P, 4, DA_QK])
        load_all(k, "lam_in", [(lam_rows[:], a["da_lambda"].to_broadcast([P, 4, DA_QK]))])
        turn(k, "turn_qk", [([tok[:, NC + t, i * P:(i + 1) * P] for t in range(NT)],
                             q_t[:, i, :] if i < 4 else k_t[:, i - 4, CTX:KEYS], None, None) for i in range(8)], NT)
        turn(k, "turn_kc", [([tok[:, t, (4 + i) * P:(5 + i) * P] for t in range(NC)],
                             k_t[:, i, 0:CTX], None, None) for i in range(4)], NC)
        diff_attention(k, q_t, k_t, da_v, lam_rows, 0.8 - 0.6, lambda t: y[:, t, 0:512],
                       k.expert_rows)

    with ExitStack() as st:
        q_dec, k_inv, k_end, states, decay = ([], [], [], [], [])
        for d in range(2):
            q_dec.append([sb(st, f"q_dec{d}{i}", [P, SEQ]) for i in range(2)])
            k_inv.append([sb(st, f"k_inv{d}{i}", [P, SEQ]) for i in range(2)])
            states.append([sb(st, f"states{d}{i}", [P, N_CH, GLA_V]) for i in range(2)])
        for d in range(2):
            with ExitStack() as st2:
                k_end = [sb(st2, f"k_end{d}{i}", [P, ALL, P]) for i in range(2)]
                decay = [sb(st2, f"decay{d}{i}", [P, N_CH]) for i in range(2)]
                k_end_t = [sb(st2, f"k_end_t{d}{i}", [P, KEYS]) for i in range(2)]
                for i in range(2):
                    gla_prepare(k, d, i, g, qk_t, q_dec[d][i][:], k_inv[d][i][:], k_end_t[i][:], decay[i][:])
                turn(k, f"turn_kend{d}", [([k_end_t[i][:, t * P:(t + 1) * P]], k_end[i][:, t, :], None, None)
                                          for i in range(2) for t in range(ALL)], 1)
                gla_states(k, d, k_end, gla_v, decay, states[d])
        gla_output(k, q_dec, k_inv, gla_v, states, lambda t: y[:, t, 512:1024])

    gate_r = tok[:, NC:ALL, 4 * 512:5 * 512]
    silu_rows(k, "silu_r", [gate_r])
    norm_heads(k, "norm_mix_heads", y[:].rearrange("p t (h n) -> p (t h) n", n=P), NT * 8, P,
               [(y[:, :, 512:1024], gate_r)])
    with ExitStack() as st:
        y_t = split_sb(st, nc, "mix_t", [P, KD, SEQ])
        raw = sb(st, "w_out_chunk", [P, KD, CHUNK_COLS])
        proj = tok[:, 0:NT, 0:D]
        gains = sb(st, "head_gains", [P, 2])
        gate = sb(st, "gate_rows", [P, D])
        load_all(k, "gains_in", [(gains[:, 0:1], a["da_subln_g"][0].rearrange("(p o) -> p o", o=1)),
                                 (gains[:, 1:2], a["gla_norm_g"][0].rearrange("(p o) -> p o", o=1)),
                                 (gate[:], mod_rows[0:1, 2 * D:3 * D].to_broadcast([P, D]))])
        scale_by(k, "lambda_gain", gains[:, 0:1], 1.0 - (0.8 - 0.6))
        turn(k, "turn_mix", [([y[:, t, i * P:(i + 1) * P] for t in range(NT)], y_t[:, i, :],
                              gains[:, 0:1] if i < 4 else gains[:, 1:2], None) for i in range(KD)], NT,
             first_chunk(raw, a["w_out"][0]))
        project(k, "proj_out", y_t, a["w_out"][0], [(0, D, token_units(NT), by_tokens(proj))], raw)
        residual(k, "residual_mix", proj, gate[:])
    outer.close()


def scale_gain(k, name, pairs):
    nc = k.nc
    with Stage(nc, name) as s:
        done = s.sem("done")
        block = s.block()

        @block.vector
        def _(v):
            for scale, gain in pairs:
                nc.vector.scalar_tensor_tensor(out=scale, in0=scale, scalar=1.0, in1=gain, op0=ALU.add,
                                               op1=ALU.mult).then_inc(done, 1)


def scale_by(k, name, x, factor):
    nc = k.nc
    with Stage(nc, name) as s:
        done = s.sem("done")
        block = s.block()

        @block.vector
        def _(v):
            nc.vector.tensor_scalar(x, x, factor, None, ALU.mult).then_inc(done, 1)



GROUPS, PER_GROUP = 4, 8
N_E = GROUPS * PER_GROUP
TOP = 2
HID = 512
N_BLOCKS = N_E + (SEQ * TOP - N_E) // P
MORE = N_BLOCKS - N_E
HT = HID // P


def narrow_projection(k, name, h, w_rows, bias, n, out):
    nc = k.nc
    with Stage(nc, name) as s:
        lt = s.sb("logits_t", [n, SEQ])
        w = split_sb(s, nc, f"{name}_w", [P, KD, P])
        w_high, w_low = s.sem("w_high"), s.sem("w_low")
        mm, lt_ok, turned = s.sem("mm"), s.sem("biased"), s.sem("turned")
        block = s.block()

        @block.tensor
        def _(pe):
            pe.wait_ge(w_low, 1)
            for q in range(KD):
                last = product(nc, k.ps[:, 0, :], w[:, q, :], h[:, q, :], q == 0, q == KD - 1)
            last.then_inc(mm, 1)
            pe.wait_ge(lt_ok, 1)
            for t in range(NT):
                last = nc.tensor.transpose(k.ps[:, 1, t * n:(t + 1) * n], lt[:, t * P:(t + 1) * P], k.c("ident")[0:n, 0:n])
            last.then_inc(turned, 1)

        @block.scalar
        def _(eng):
            nc.scalar.activation(w.high[:], w_rows[:], ACT.Copy).then_inc(w_high, 1)

        @block.vector
        def _(v):
            v.wait_ge(w_high, 1)
            nc.vector.tensor_tensor(w.low[:], w_rows[:], w.high[:].bitcast(F32), ALU.subtract).then_inc(w_low, 1)
            v.wait_ge(mm, 1)
            nc.vector.tensor_scalar(lt[:], k.ps[0:n, 0, :], bias, None, ALU.add).then_inc(lt_ok, 1)
            v.wait_ge(turned, 1)
            nc.vector.tensor_copy(out, k.ps[:, 1, 0:NT * n].rearrange("p (t n) -> p t n", t=NT))


def route(k, logits, weights, dest, block_e):
    nc = k.nc
    with Stage(nc, "route") as s:
        def small(name, n, m):
            return s.sb(name, [P, n, m])

        gl, el = logits[:, :, 0:GROUPS], logits[:, :, GROUPS:]
        gm, gs, gi = small("gm", NT, 1), small("gs", NT, 1), small("gi", NT, 1)
        ge, gc, goh = small("ge", NT, GROUPS), small("gc", NT, GROUPS), small("goh", NT, GROUPS)
        em, cand, e2 = small("em", NT, N_E), small("cand", NT, N_E), small("e2", NT, N_E)
        tmp = small("tmp", NT, N_E)
        oh = [small(f"oh{i}", NT, N_E) for i in range(TOP)]
        top = [small(f"top{i}", NT, 1) for i in range(TOP)]
        both, pos = small("both", NT, N_E), small("pos", NT, N_E)
        tot = small("tot", NT, N_E)
        run = s.sb("run", [P, N_E])
        nb = s.sb("nb", [P, N_E])
        nb_i = s.sb("nb_i", [P, N_E], I32)
        ends = s.sb("ends", [P, 2, N_E])
        first = s.sb("first", [P, N_E])
        below = s.sb("below", [P, MORE, N_E])
        bsum = s.sb("bsum", [P, MORE])
        over = s.sb("over", [P, NT, N_E])
        dest_f = s.sb("dest_f", [P, NT, TOP])
        chain, exps, mm = s.sem("chain"), s.sem("exps"), s.sem("mm")
        ready, both_ok = s.sem("ready"), s.sem("both_ok")
        block = s.block()

        @block.scalar
        def _(eng):
            eng.wait_ge(ready, 1)
            nc.scalar.activation(ge[:], ge[:], ACT.Exp).then_inc(exps, 1)
            eng.wait_ge(ready, 2)
            nc.scalar.activation(top[1][:], top[1][:], ACT.Exp).then_inc(exps, 1)

        @block.tensor
        def _(pe):
            pe.wait_ge(both_ok, 1)
            rhs = both[:].rearrange("p t e -> p (t e)")
            nc.tensor.matmul(k.ps[:, 0, 0:NT * N_E], k.c("before"), rhs, start=True, stop=True)
            nc.tensor.matmul(k.ps[:, 1, 0:NT * N_E], k.c("ones"), rhs, start=True, stop=True).then_inc(mm, 1)

        @block.vector
        def _(v):
            link = in_order(v, chain)
            V = nc.vector
            iota = k.c("iota")

            def first_of(values, best, out, width):
                c = gc if width == GROUPS else cand
                link(V.tensor_tensor(c[:], values, best.to_broadcast([P, NT, width]), ALU.is_equal))
                link(V.scalar_tensor_tensor(out=c[:], in0=c[:], scalar=-64.0,
                                            in1=iota[:, 0:width].unsqueeze(1).to_broadcast([P, NT, width]),
                                            op0=ALU.mult, op1=ALU.add))
                link(V.tensor_reduce(gi[:], c[:], AX.X, ALU.min))
                link(V.tensor_tensor(out, c[:], gi[:].to_broadcast([P, NT, width]), ALU.is_equal))

            link(V.tensor_reduce(gm[:], gl, AX.X, ALU.max))
            V.tensor_tensor(ge[:], gl, gm[:].to_broadcast([P, NT, GROUPS]), ALU.subtract).then_inc(ready, 1)
            first_of(gl, gm[:], goh[:], GROUPS)
            by_group = lambda x: x.rearrange("p t (g e) -> p t g e", g=GROUPS)
            chosen = goh[:].unsqueeze(3).to_broadcast([P, NT, GROUPS, PER_GROUP])
            link(V.tensor_tensor(by_group(em[:]), by_group(el), chosen, ALU.mult))
            link(V.tensor_scalar(gc[:], goh[:], 1.0, -NEG, ALU.subtract, ALU.mult))
            link(V.tensor_tensor(by_group(em[:]), by_group(em[:]),
                                 gc[:].unsqueeze(3).to_broadcast([P, NT, GROUPS, PER_GROUP]), ALU.add))
            link(V.tensor_reduce(top[0][:], em[:], AX.X, ALU.max))
            first_of(em[:], top[0][:], oh[0][:], N_E)
            link(V.scalar_tensor_tensor(out=e2[:], in0=oh[0][:], scalar=3 * NEG, in1=em[:], op0=ALU.mult, op1=ALU.add))
            link(V.tensor_reduce(top[1][:], e2[:], AX.X, ALU.max))
            first_of(e2[:], top[1][:], oh[1][:], N_E)
            V.tensor_tensor(both[:], oh[0][:], oh[1][:], ALU.add).then_inc(both_ok, 1)
            V.tensor_tensor(top[1][:], top[1][:], top[0][:], ALU.subtract).then_inc(ready, 1)
            v.wait_ge(exps, 2)
            link(V.tensor_reduce(gs[:], ge[:], AX.X, ALU.add))
            link(V.tensor_scalar(top[0][:], top[1][:], 1.0, None, ALU.add))
            link(V.tensor_tensor(gs[:], gs[:], top[0][:], ALU.mult))
            link(V.reciprocal(weights[:, :, 0:1], gs[:]))
            link(V.tensor_tensor(weights[:, :, 1:2], weights[:, :, 0:1], top[1][:], ALU.mult))
            v.wait_ge(mm, 1)
            flat = lambda x: x.rearrange("p t e -> p (t e)")
            link(V.tensor_copy(flat(pos[:]), k.ps[:, 0, 0:NT * N_E]))
            link(V.tensor_copy(flat(tot[:]), k.ps[:, 1, 0:NT * N_E]))
            link(V.tensor_copy(run[:], tot[:, 0, :]))
            for t in range(1, NT):
                link(V.tensor_tensor(pos[:, t, :], pos[:, t, :], run[:], ALU.add))
                link(V.tensor_tensor(run[:], run[:], tot[:, t, :], ALU.add))
            link(V.tensor_scalar(nb_i[:], run[:], float(P - 1), None, ALU.add))
            link(V.tensor_scalar(nb_i[:], nb_i[:], 7, None, ALU.arith_shift_right))
            link(V.tensor_scalar(nb[:], nb_i[:], 1.0, 0.0, ALU.subtract, ALU.max))
            link(V.tensor_copy(ends[:, 0, :], nb[:]))
            for n, step in enumerate((1, 2, 4, 8, 16)):
                a, b = ends[:, n % 2, :], ends[:, (n + 1) % 2, :]
                link(V.tensor_copy(b[:, 0:step], a[:, 0:step]))
                link(V.tensor_tensor(b[:, step:], a[:, step:], a[:, 0:N_E - step], ALU.add))
            end = ends[:, 1, :]
            link(V.tensor_tensor(first[:], end, nb[:], ALU.subtract))
            rows_of = lambda x: x.unsqueeze(1).to_broadcast([P, NT, N_E])
            link(V.tensor_scalar(over[:], pos[:], float(P), None, ALU.is_ge))
            link(V.tensor_tensor(first[:], first[:], iota[:, 0:N_E], ALU.subtract))
            link(V.tensor_scalar(first[:], first[:], float(N_E - 1), None, ALU.add))
            link(V.tensor_tensor(over[:], over[:], rows_of(first[:]), ALU.mult))
            link(V.tensor_tensor(over[:], over[:], rows_of(iota[:, 0:N_E]), ALU.add))
            link(V.scalar_tensor_tensor(out=pos[:], in0=over[:], scalar=float(P), in1=pos[:], op0=ALU.mult, op1=ALU.add))
            for i in range(TOP):
                link(V.tensor_tensor(tmp[:], oh[i][:], pos[:], ALU.mult))
                link(V.tensor_reduce(dest_f[:, :, i:i + 1], tmp[:], AX.X, ALU.add))
            link(V.tensor_copy(dest, dest_f[:].rearrange("p t i -> p (t i)")))
            link(V.tensor_tensor(below[:], end.unsqueeze(1).to_broadcast([P, MORE, N_E]),
                                 iota[:, 0:MORE].unsqueeze(2).to_broadcast([P, MORE, N_E]), ALU.is_le))
            link(V.tensor_reduce(bsum[:], below[:], AX.X, ALU.add))
            link(V.tensor_scalar(block_e[:, 0:MORE], bsum[:], float(N_E - 1), None, ALU.min))
            link(V.tensor_copy(block_e[:, MORE:], end[:, N_E - 1:]))


def scatter_rows(k, rows, dest, table):
    nc = k.nc
    with Stage(nc, "scatter") as s:
        out = k.scattered
        block = s.block()

        @block.gpsimd
        def _(pool):
            for t in range(NT):
                for i in range(TOP):
                    n = t * TOP + i
                    pool.indirect_dma_start(out=table, out_offset=bass.IndirectOffsetOnAxis(ap=dest[:, n:n + 1], axis=0),
                                            in_=rows[:, t, :], in_offset=None).then_inc(out, 16)
            pool.wait_ge(out, 16 * NT * TOP)


def gather_rows(k, rows, dest, table):
    nc = k.nc
    with Stage(nc, "gather") as s:
        loaded = k.gathered
        block = s.block()

        @block.gpsimd
        def _(pool):
            for n in range(NT * TOP):
                pool.indirect_dma_start(out=rows[:, n, :], out_offset=None, in_=table,
                                        in_offset=bass.IndirectOffsetOnAxis(ap=dest[:, n:n + 1], axis=0)).then_inc(loaded, 16)
            pool.wait_ge(loaded, 16 * NT * TOP)


def expert_weights(w, e, rows):
    return w.rearrange("e (p k) n -> e p k n", k=rows)[bass.ds(e, 1)].rearrange("a p k n -> p (a k) n")


def load_ahead_experts(k, slots, weights):
    with Stage(k.nc, "experts_ahead") as s:
        block = s.block()

        @block.sync
        def _(sp):
            for e in range(2):
                for slot, w, rows in zip(slots, weights, (KD, KD, HT)):
                    sp.dma_start(slot[:, e], expert_weights(w, e, rows)).then_inc(k.experts_in, 16)


def experts(k, name, start, count, block_e, table, slots, weights):
    nc = k.nc
    pairs = (count - 1) // 2
    tail = list(range(2 * pairs, count))

    def if_used(eng):
        if block_e is None:
            return ExitStack()
        return eng.If(eng.value_load(block_e[0:1, MORE:], min_val=0, max_val=MORE) > 0)

    xv = table.rearrange("(b p) d -> b p d", p=P)
    yv = xv
    with Stage(nc, name) as s:
        g, u, d = slots
        x, xt = s.sb("x", [P, 2, D]), s.sb("x_t", [P, KD, P])
        sg, hh, ht = s.sb("silu", [P, HID]), s.sb("hidden", [P, HID]), s.sb("hidden_t", [P, HT, P])
        y = s.sb("y", [P, 2, D])
        gu_in, d_in, x_in, y_out = ([s.sem(f"{n}{j}") for j in range(2)] for n in ("gate_up_in", "down_in", "x_in", "y_out"))
        x_turned, xt_ok, gate_mm, up_mm, silu_ok, h_ok = (s.sem(n) for n in ("x_turned", "xt_ok", "gate_mm", "up_mm", "silu_ok", "h_ok"))
        h_turned, ht_ok, down_mm, y_ok = (s.sem(n) for n in ("h_turned", "ht_ok", "down_mm", "y_ok"))
        block = s.block()

        @block.sync
        def _(sp):
            def load(b, j, used_before):
                ahead = block_e is None and used_before is None
                e = b if block_e is None else sp.value_load(block_e[0:1, bass.ds(b, 1)], min_val=0, max_val=N_E - 1)
                if used_before is not None:
                    sp.wait_ge(x_turned, used_before)
                sp.dma_start(x[:, j, :], xv[bass.ds(b + start, 1)].rearrange("a p d -> p (a d)")).then_inc(x_in[j], 16)
                if ahead:
                    sp.wait_ge(k.experts_in, 2 * 3 * 16)
                    sp.sem_inc(gu_in[j], 32)
                    sp.sem_inc(d_in[j], 16)
                    return
                if used_before is not None:
                    sp.wait_ge(up_mm, used_before)
                sp.dma_start(g[:, j], expert_weights(weights[0], e, KD)).then_inc(gu_in[j], 16)
                sp.dma_start(u[:, j], expert_weights(weights[1], e, KD)).then_inc(gu_in[j], 16)
                if used_before is not None:
                    sp.wait_ge(down_mm, used_before)
                sp.dma_start(d[:, j], expert_weights(weights[2], e, HT)).then_inc(d_in[j], 16)

            with if_used(sp):
                for b in range(2):
                    load(b, b, None)
                with sp.Fori(1, pairs) as i:
                    for j in range(2):
                        load(i * 2 + j, j, i * 2 + (j - 1))
                for b in tail:
                    load(b, b % 2, b - 1)

        @block.tensor
        def _(pe):
            def turn_x(j, arrived):
                pe.wait_ge(x_in[j], arrived)
                for q in range(KD):
                    last = nc.tensor.transpose(k.ps[:, q // 4, (q % 4) * P:(q % 4 + 1) * P], x[:, j, q::KD], k.c("ident"))
                last.then_inc(x_turned, 1)

            def gate_up(b, j, arrived):
                pe.wait_ge(xt_ok, b + 1)
                pe.wait_ge(gu_in[j], arrived * 2)
                pe.wait_ge(h_ok, b + 1)
                for w, bank, sem in ((g, 2, gate_mm), (u, 3, up_mm)):
                    for q in range(KD):
                        last = nc.tensor.matmul(k.ps[:, bank, :], xt[:, q, :], w[:, j, q, :], start=q == 0, stop=q == KD - 1)
                    last.then_inc(sem, 1)

            def turn_h(b):
                pe.wait_ge(h_ok, b + 2)
                for c in range(HT):
                    last = nc.tensor.transpose(k.ps[:, 4, c * P:(c + 1) * P], hh[:, c::HT], k.c("ident"))
                last.then_inc(h_turned, 1)

            def down(b, j, arrived):
                pe.wait_ge(ht_ok, b + 1)
                pe.wait_ge(d_in[j], arrived)
                pe.wait_ge(y_ok, b + 1)
                for half in range(2):
                    for c in range(HT):
                        last = nc.tensor.matmul(k.ps[:, 5 + half, :], ht[:, c, :], d[:, j, c, half * BANK:(half + 1) * BANK],
                                                start=c == 0, stop=c == HT - 1)
                last.then_inc(down_mm, 1)

            inner = (count - 2) // 2
            with if_used(pe):
                turn_x(0, 16)
                gate_up(0, 0, 16)
                turn_x(1, 16)
                turn_h(0)
                with pe.Fori(0, inner) as i:
                    gate_up(i * 2 + 1, 1, (i + 1) * 16)
                    turn_x(0, (i + 2) * 16)
                    down(i * 2, 0, (i + 1) * 16)
                    turn_h(i * 2 + 1)
                    gate_up(i * 2 + 2, 0, (i + 2) * 16)
                    turn_x(1, (i + 2) * 16)
                    down(i * 2 + 1, 1, (i + 1) * 16)
                    turn_h(i * 2 + 2)
                for b in range(2 * inner + 1, count):
                    gate_up(b, b % 2, (b // 2 + 1) * 16)
                    if b + 1 < count:
                        turn_x((b + 1) % 2, ((b + 1) // 2 + 1) * 16)
                    down(b - 1, (b - 1) % 2, ((b - 1) // 2 + 1) * 16)
                    turn_h(b)
                down(count - 1, (count - 1) % 2, ((count - 1) // 2 + 1) * 16)

        @block.vector
        def _(v):
            def copy_x():
                return nc.vector.tensor_copy(xt[:].rearrange("p (b q) n -> p b (q n)", b=2), k.ps[:, 0:2, :])

            def body(b, more):
                v.wait_ge(silu_ok, b + 1)
                v.wait_ge(up_mm, b + 1)
                nc.vector.tensor_tensor(hh[:], sg[:], k.ps[:, 3, :], ALU.mult).then_inc(h_ok, 1)
                if more:
                    v.wait_ge(x_turned, b + 2)
                    copy_x().then_inc(xt_ok, 1)
                v.wait_ge(h_turned, b + 1)
                nc.vector.tensor_copy(ht[:].rearrange("p c n -> p (c n)"), k.ps[:, 4, :]).then_inc(ht_ok, 1)

            with if_used(v):
                v.sem_inc(h_ok, 1)
                v.wait_ge(x_turned, 1)
                copy_x().then_inc(xt_ok, 1)
                with v.Fori(0, count - 1) as b:
                    body(b, True)
                body(count - 1, False)

        @block.scalar
        def _(eng):
            def silu(b):
                eng.wait_ge(gate_mm, b + 1)
                eng.wait_ge(h_ok, b + 1)
                nc.scalar.activation(sg[:], k.ps[:, 2, :], ACT.Silu).then_inc(silu_ok, 1)

            def store(b, j, i):
                eng.wait_ge(down_mm, b + 1)
                eng.wait_ge(y_out[j], (i + 1) * 16)
                nc.scalar.activation(y[:, j, :].rearrange("p (h n) -> p h n", h=2), k.ps[:, 5:7, :], ACT.Copy).then_inc(y_ok, 1)
                eng.wait_ge(y_ok, b + 2)
                eng.dma_start(yv[bass.ds(b + start, 1)].rearrange("a p d -> p (a d)"), y[:, j, :]).then_inc(y_out[j], 16)

            with if_used(eng):
                eng.sem_inc(y_ok, 1)
                for j in range(2):
                    eng.sem_inc(y_out[j], 16)
                silu(0)
                with eng.Fori(0, pairs) as i:
                    for j in range(2):
                        silu(i * 2 + (j + 1))
                        store(i * 2 + j, j, i)
                for b in tail:
                    if b + 1 < count:
                        silu(b + 1)
                    store(b, b % 2, pairs)
                for j in range(2):
                    eng.wait_ge(y_out[j], (1 + pairs + sum(b % 2 == j for b in tail)) * 16)


def combine(k, rows, weights, gate, gain):
    nc = k.nc
    with Stage(nc, "combine") as s:
        junk = s.sb("junk", [P, 2, D])
        rs = s.sb("rs", [P, NT])
        row0, both, scaled, added = s.sem("row0"), s.sem("both"), s.sem("gated"), s.sem("added")
        squares, mean, root, inverse, x_ok = (s.sem(n) for n in ("squares", "mean", "root", "inverse", "x_ok"))
        block = s.block()

        @block.scalar
        def _(eng):
            def square(t, out, n):
                if n > 1:
                    eng.wait_ge(squares, n - 1)
                nc.scalar.activation(junk[:, n % 2, :], k.x[:, t, :], ACT.Square, accum_out=out).then_inc(squares, 1)

            for t in range(NT):
                part = rows[:, 2 * t, :]
                nc.scalar.activation(part, part, ACT.Copy, scale=weights[:, t, 0:1]).then_inc(row0, 1)
            for t in range(NT):
                eng.wait_ge(added, t + 1)
                square(t, rs[:, t:t + 1], t)
                eng.wait_ge(mean, t + 1)
                nc.scalar.activation(rs[:, t:t + 1], rs[:, t:t + 1], ACT.Sqrt).then_inc(root, 1)
            for t in range(NT):
                eng.wait_ge(x_ok, t + 1)
                square(t, k.rs[:, t:t + 1], NT + t)
            eng.wait_ge(mean, NT + 1)
            nc.scalar.activation(k.rs[:], k.rs[:], ACT.Sqrt).then_inc(root, 1)

        @block.vector
        def _(v):
            def add(t):
                part = rows[:, 2 * t, :]
                v.wait_ge(row0, t + 1)
                nc.vector.scalar_tensor_tensor(out=part, in0=rows[:, 2 * t + 1, :], scalar=weights[:, t, 1:2],
                                               in1=part, op0=ALU.mult, op1=ALU.add).then_inc(both, 1)
                v.wait_ge(both, t + 1)
                nc.vector.tensor_tensor(part, part, gate, ALU.mult).then_inc(scaled, 1)
                v.wait_ge(scaled, t + 1)
                nc.vector.tensor_tensor(k.x[:, t, :], k.x[:, t, :], part, ALU.add).then_inc(added, 1)

            def normed(t):
                v.wait_ge(squares, t + 1)
                nc.vector.tensor_scalar(rs[:, t:t + 1], rs[:, t:t + 1], 1.0 / D, EPS, ALU.mult, ALU.add).then_inc(mean, 1)
                v.wait_ge(root, t + 1)
                nc.vector.reciprocal(rs[:, t:t + 1], rs[:, t:t + 1]).then_inc(inverse, 1)
                v.wait_ge(inverse, t + 1)
                nc.vector.scalar_tensor_tensor(out=k.x[:, t, :], in0=k.x[:, t, :], scalar=rs[:, t:t + 1], in1=gain,
                                               op0=ALU.mult, op1=ALU.mult).then_inc(x_ok, 1)

            add(0)
            for t in range(NT):
                if t + 1 < NT:
                    add(t + 1)
                normed(t)
            v.wait_ge(squares, 2 * NT)
            nc.vector.tensor_scalar(k.rs[:], k.rs[:], 1.0 / D, EPS, ALU.mult, ALU.add).then_inc(mean, 1)
            v.wait_ge(root, NT + 1)
            nc.vector.reciprocal(k.rs[:], k.rs[:]).then_inc(inverse, 1)


def rows_affine(k, name, x, gain, shift=None):
    nc = k.nc
    with Stage(nc, name) as s:
        chain = s.sem("chain")
        block = s.block()

        @block.vector
        def _(v):
            link = in_order(v, chain)
            link(nc.vector.tensor_tensor(x, x, gain.unsqueeze(1).to_broadcast([P, NT, D]), ALU.mult))
            if shift is not None:
                link(nc.vector.tensor_tensor(x, x, shift.unsqueeze(1).to_broadcast([P, NT, D]), ALU.add))


def everywhere(row):
    return row.to_broadcast([P, row.shape[1]])


def first_experts(k, es, mod_rows):
    nc, a = k.nc, k.a
    table = k.expert_rows

    def sb(stack, name, shape, dt=F32):
        return stack.enter_context(nc.sbuf_tensor(name, shape, dt))

    outer = es.enter_context(ExitStack())
    weights = sb(outer, "route_weights", [P, NT, TOP])
    dest = sb(outer, "route_dest", [P, NT * TOP], I32)
    block_e = sb(outer, "block_expert", [P, MORE + 1], I32)
    slots = [sb(outer, n, shape) for n, shape in (("expert_gate", [P, 2, KD, HID]), ("expert_up", [P, 2, KD, HID]),
                                                  ("expert_down", [P, 2, HT, D]))]
    w_experts = [a["expert_w_gate"][0], a["expert_w_up"][0], a["expert_w_down"][0]]
    with ExitStack() as st:
        h = sb(st, "h2", [P, NT, D])
        h_t = split_sb(st, nc, "h2_t", [P, KD, SEQ])
        rows = sb(st, "mod_rows2", [P, 3, D])
        w_r = sb(st, "w_router", [P, KD, P])
        b_r = sb(st, "b_router", [GROUPS + N_E, 1])
        logits = sb(st, "logits", [P, NT, GROUPS + N_E])
        vector_steps(k, "router_clear", [lambda v: v.memset(w_r[:], 0.0)])
        load_all(k, "router_in", [
            (rows[:, 0, :], everywhere(a["norm_ffn_g"])),
            (rows[:, 1, :], everywhere(mod_rows[0:1, 4 * D:5 * D])),
            (rows[:, 2, :], everywhere(mod_rows[0:1, 3 * D:4 * D])),
            (w_r[:, :, 0:GROUPS], a["router_group_w"][0].rearrange("(k p) n -> p k n", p=P)),
            (w_r[:, :, GROUPS:GROUPS + N_E], a["router_expert_w"][0].rearrange("(k p) n -> p k n", p=P)),
            (b_r[0:GROUPS, :], a["router_group_b"][0].rearrange("(p o) -> p o", o=1)),
            (b_r[GROUPS:, :], a["router_expert_b"][0].rearrange("(p o) -> p o", o=1))])
        load_ahead_experts(k, slots, w_experts)
        scale_gain(k, "ffn_gain", [(rows[:, 1, :], rows[:, 0, :])])
        norm_rows(k, "norm_ffn", [(k.x[:, t, :], h[:, t, :]) for t in range(NT)], D)
        rows_affine(k, "modulate2", h[:], rows[:, 1, :], rows[:, 2, :])
        turn(k, "turn_h2", [([h[:, t, i * P:(i + 1) * P] for t in range(NT)], h_t[:, i, :], None, None)
                            for i in range(KD)], NT)
        narrow_projection(k, "router", h_t, w_r, b_r[:, 0:1], GROUPS + N_E, logits[:])
        route(k, logits, weights, dest[:], block_e[:])
        scatter_rows(k, h, dest, table)
    experts(k, "experts", 0, N_E, None, table, slots, w_experts)
    experts(k, "more_experts", N_E, MORE, block_e, table, slots, w_experts)
    with ExitStack() as st:
        rows = sb(st, "expert_rows_sb", [P, NT * TOP, D])
        gate = sb(st, "gate_rows2", [P, 2, D])
        load_all(k, "gate2_in", [(gate[:, 0, :], everywhere(mod_rows[0:1, 5 * D:6 * D])),
                                 (gate[:, 1, :], a["final_norm_g"].rearrange("(o n) -> o n", o=1).to_broadcast([P, D]))])
        gather_rows(k, rows, dest, table)
        combine(k, rows, weights, gate[:, 0, :], gate[:, 1, :])
    outer.close()



FF = 2816
FF_T = FF // P
RES = 0.5


def column_tables(k, name, rows):
    nc = k.nc
    total = sum(dst.shape[1] for _, dst in rows)
    assert total <= P
    with Stage(nc, name) as s:
        buf = s.sb("rows", [P, P])
        loaded, turned, done = s.sem("loaded"), s.sem("turned"), s.sem("done")
        block = s.block()

        @block.sync
        def _(sp):
            at = 0
            for src, dst in rows:
                sp.dma_start(buf[at:at + dst.shape[1], :], src).then_inc(loaded, 16)
                at += dst.shape[1]

        @block.tensor
        def _(pe):
            pe.wait_ge(loaded, 16 * len(rows))
            nc.tensor.transpose(k.ps[:, 0, 0:total], buf[0:total, :], k.c("ident")[0:total, 0:total]).then_inc(turned, 1)

        @block.vector
        def _(v):
            v.wait_ge(turned, 1)
            at = 0
            for _, dst in rows:
                nc.vector.tensor_copy(dst, k.ps[:, 0, at:at + dst.shape[1]]).then_inc(done, 1)
                at += dst.shape[1]


def ffn_columns(w, t):
    return w.rearrange("(k p) n -> p k n", p=P)[:, :, bass.ds(t * P, P)]


def ffn_products(k, name, raw, u, w_gate, w_up, w_down, hidden):
    nc = k.nc
    pairs = FF_T // 2
    downs = FF_T // 2
    steps = FF_T + downs
    assert FF_T % 2 == 0 and downs % 2 == 1
    wd = w_down.rearrange("(t p) n -> t p n", p=P)
    with Stage(nc, name) as s:
        w = split_sb(s, nc, f"{name}_w", [P, 2, 2 * KD * P])
        sg = s.sb("silu", [P, 2, SEQ])
        whole = s.sb("whole", [P, 2, SEQ])
        w_in = [s.sem(f"w_in{j}") for j in range(2)]
        w_high, w_low, gate_mm, up_mm = s.sem("w_high"), s.sem("w_low"), s.sem("gate_mm"), s.sem("up_mm")
        silu_ok, whole_ok, h_high, h_low = s.sem("silu_ok"), s.sem("whole_ok"), s.sem("h_high"), s.sem("h_low")
        down_mm, done = s.sem("down_mm"), s.sem("done")
        block = s.block()

        def result(m):
            return raw[:].rearrange("p j n -> p (j n)")[:, m * SEQ:(m + 1) * SEQ]

        @block.sync
        def _(sp):
            def load(t, j):
                for side, half in enumerate((w_gate, w_up)):
                    to = raw[:, j, side * KD * P:(side + 1) * KD * P].rearrange("p (k n) -> p k n", k=KD)
                    sp.dma_start(to, ffn_columns(half, t)).then_inc(w_in[j], 16)

            def load_down(b, j):
                for a in range(2):
                    sp.dma_start(raw[:, j, a * D:(a + 1) * D],
                                 wd[bass.ds(b * 2 + a, 1)].rearrange("a p n -> p (a n)")).then_inc(w_in[j], 16)

            with sp.Fori(1, pairs) as i:
                for j in range(2):
                    sp.wait_ge(w_low, i * 2 + (j - 1))
                    load(i * 2 + j, j)
            with sp.Fori(0, downs // 2) as i:
                for j in range(2):
                    sp.wait_ge(w_low, i * 2 + (FF_T + j - 1))
                    load_down(i * 2 + j, j)
            sp.wait_ge(w_low, steps - 2)
            load_down(downs - 1, 0)

        @block.tensor
        def _(pe):
            pe.sem_inc(up_mm, 1)
            with pe.Fori(0, pairs) as i:
                for j in range(2):
                    t = i * 2 + j
                    pe.wait_ge(w_low, t + 1)
                    pe.wait_ge(whole_ok, t + 1)
                    for side, sem in enumerate((gate_mm, up_mm)):
                        for q in range(KD):
                            at = (side * KD + q) * P
                            last = product(nc, k.ps[:, 2 * j + side, :], w[:, j, at:at + P], u[:, q, :], q == 0, q == KD - 1)
                        last.then_inc(sem, 1)

            def down(b, j, first=False, final=False):
                pe.wait_ge(w_low, b + (FF_T + 1))
                if first:
                    pe.wait_ge(whole_ok, FF_T + 2)
                if final:
                    pe.wait_ge(h_low, FF_T)
                else:
                    pe.wait_ge(h_low, b * 2 + 2)
                for a in range(2):
                    at = bass.ds(b * 2 + a, 1)
                    flat = lambda part: part[:, at, :].rearrange("p a n -> p (a n)")
                    rhs = Split(flat(hidden.high), flat(hidden.low))
                    for m in range(KD):
                        cols = a * D + m * P
                        last = product(nc, k.ps[:, m, :], w[:, j, cols:cols + P], rhs, first and a == 0, final and a == 1)
                last.then_inc(down_mm, 1)

            for b in range(2):
                down(b, b, first=b == 0)
            with pe.Fori(1, downs // 2) as i:
                for j in range(2):
                    down(i * 2 + j, j)
            down(downs - 1, 0, final=True)

        def tile_of(part, t):
            return part[:, bass.ds(t, 1), :].rearrange("p a n -> p (a n)")

        @block.scalar
        def _(eng):
            def high(j, loaded):
                if loaded is not None:
                    eng.wait_ge(w_in[j], loaded * 32)
                nc.scalar.activation(w.high[:, j], raw[:, j], ACT.Copy).then_inc(w_high, 1)

            def step(t, j):
                eng.wait_ge(gate_mm, t + 1)
                eng.wait_ge(whole_ok, t + 1)
                nc.scalar.activation(sg[:, j, :], k.ps[:, 2 * j, :], ACT.Silu).then_inc(silu_ok, 1)
                eng.wait_ge(whole_ok, t + 3)
                nc.scalar.activation(tile_of(hidden.high, t), whole[:, j, :], ACT.Copy).then_inc(h_high, 1)

            high(0, None)
            high(1, None)
            step(0, 0)
            with eng.Fori(0, pairs - 1) as i:
                for j in range(2):
                    eng.wait_ge(up_mm, i * 2 + (j + 2))
                    high(j, i + 1)
                    step(i * 2 + (j + 1), 1 - j)
            eng.wait_ge(up_mm, FF_T)
            high(0, pairs)
            step(FF_T - 1, 1)
            eng.wait_ge(up_mm, FF_T + 1)
            high(1, pairs)
            with eng.Fori(1, downs // 2) as i:
                for j in range(2):
                    eng.wait_ge(down_mm, i * 2 + (j - 1))
                    high(j, i + pairs)
            eng.wait_ge(down_mm, downs - 2)
            high(0, downs // 2 + pairs)
            eng.wait_ge(down_mm, downs)
            for m in range(1, KD, 2):
                nc.scalar.activation(result(m), k.ps[:, m, :], ACT.Copy).then_inc(done, 1)

        @block.vector
        def _(v):
            def low(t, j):
                v.wait_ge(w_high, t + 1)
                nc.vector.tensor_tensor(w.low[:, j], raw[:, j], w.high[:, j].bitcast(F32), ALU.subtract).then_inc(w_low, 1)

            def step(t, j):
                v.wait_ge(silu_ok, t + 1)
                v.wait_ge(up_mm, t + 2)
                nc.vector.tensor_tensor(whole[:, j, :], sg[:, j, :], k.ps[:, 2 * j + 1, :], ALU.mult).then_inc(whole_ok, 1)
                v.wait_ge(h_high, t + 1)
                nc.vector.tensor_tensor(tile_of(hidden.low, t), whole[:, j, :], tile_of(hidden.high, t).bitcast(F32),
                                        ALU.subtract).then_inc(h_low, 1)

            v.sem_inc(whole_ok, 2)
            low(0, 0)
            with v.Fori(0, pairs) as i:
                for j in range(2):
                    low(i * 2 + (j + 1), 1 - j)
                    step(i * 2 + j, j)
            with v.Fori(0, downs // 2) as i:
                for j in range(2):
                    low(i * 2 + (FF_T + 1 + j), 1 - j)
            v.wait_ge(down_mm, downs)
            for m in range(0, KD, 2):
                nc.vector.tensor_copy(result(m), k.ps[:, m, :]).then_inc(done, 1)

def features_to_tokens(k, name, sources, dst):
    n = len(sources)
    per = min(4, n)
    turn(k, name, [([sources[j + q][:, t * P:(t + 1) * P] for q in range(per)], dst[:, t, j * P:(j + per) * P], None, None)
                   for t in range(NT) for j in range(0, n, per)], per)


def normed_input(k, name, gain, u, ahead=()):
    nc = k.nc
    with Stage(nc, name) as s:
        xn = s.sb("xn", [P, NT, D])
        scaled_v, scaled_s, turned = s.sem("scaled_v"), s.sem("scaled_s"), s.sem("turned")
        high_ok, low_ok = s.sem("high_ok"), s.sem("low_ok")
        ahead_in = s.sem("ahead_in")
        block = s.block()

        @block.sync
        def _(sp):
            load_ahead(sp, ahead, ahead_in)

        @block.tensor
        def _(pe):
            for t in range(NT):
                pe.wait_ge(scaled_s if t % 2 else scaled_v, t // 2 + 1)
                for i in range(KD):
                    last = nc.tensor.transpose(k.ps[:, i, t * P:(t + 1) * P], xn[:, t, i * P:(i + 1) * P], k.c("ident"))
                    if t == NT - 1:
                        last.then_inc(turned, 1)

        @block.scalar
        def _(eng):
            for t in range(1, NT, 2):
                nc.scalar.activation(xn[:, t, :], k.x[:, t, :], ACT.Copy, scale=k.rs[:, t:t + 1]).then_inc(scaled_s, 1)
            for i in range(KD):
                eng.wait_ge(turned, i + 1)
                nc.scalar.activation(u.high[:, i, :], k.ps[:, i, :], ACT.Copy, scale=gain[:, i:i + 1]).then_inc(high_ok, 1)

        @block.vector
        def _(v):
            for t in range(0, NT, 2):
                nc.vector.tensor_scalar(xn[:, t, :], k.x[:, t, :], k.rs[:, t:t + 1], None, ALU.mult).then_inc(scaled_v, 1)
            for i in range(KD):
                v.wait_ge(high_ok, i + 1)
                nc.vector.scalar_tensor_tensor(out=u.low[:, i, :], in0=k.ps[:, i, :], scalar=gain[:, i:i + 1],
                                               in1=u.high[:, i, :].bitcast(F32), op0=ALU.mult, op1=ALU.subtract).then_inc(low_ok, 1)


def add_normed(k, name, f, f_t, gain_row, factor=1.0):
    nc = k.nc
    with Stage(nc, name) as s:
        gain = s.sb("gain", [P, D])
        junk, part = s.sb("junk", [P, 2, D]), s.sb("part", [P, 2, D])
        rs = s.sb("rs", [P, NT])
        gain_in, turned, squares, mean, root = (s.sem(n) for n in ("gain_in", "turned", "squares", "mean", "root"))
        inverse, product_ok, x_ok, x_mean, x_root = (s.sem(n) for n in ("inverse", "product", "x_ok", "x_mean", "x_root"))
        block = s.block()

        @block.sync
        def _(sp):
            sp.dma_start(gain[:], everywhere(gain_row)).then_inc(gain_in, 16)

        @block.tensor
        def _(pe):
            if f is None:
                for t in range(NT):
                    for i in range(KD):
                        last = nc.tensor.transpose(k.ps[:, 2 * t + i // 4, (i % 4) * P:(i % 4 + 1) * P],
                                                   f_t[:, i, t * P:(t + 1) * P], k.c("ident"))
                    last.then_inc(turned, 1)

        def rows(t):
            return k.ps[:, 2 * t:2 * t + 2, :].rearrange("p b n -> p (b n)") if f is None else f[:, t, :]

        @block.scalar
        def _(eng):
            def square(src, out, n):
                if n > 1:
                    eng.wait_ge(squares, n - 1)
                nc.scalar.activation(junk[:, n % 2, :], src, ACT.Square, accum_out=out).then_inc(squares, 1)

            for t in range(NT + 1):
                if t < NT:
                    if f is None:
                        eng.wait_ge(turned, t + 1)
                    square(rows(t), rs[:, t:t + 1], t)
                if t:
                    eng.wait_ge(mean, t)
                    nc.scalar.activation(rs[:, t - 1:t], rs[:, t - 1:t], ACT.Sqrt).then_inc(root, 1)
            for t in range(NT):
                eng.wait_ge(x_ok, t + 1)
                square(k.x[:, t, :], k.rs[:, t:t + 1], NT + t)
            eng.wait_ge(x_mean, 1)
            nc.scalar.activation(k.rs[:], k.rs[:], ACT.Sqrt).then_inc(x_root, 1)

        @block.vector
        def _(v):
            def mean_of(t):
                v.wait_ge(squares, t + 1)
                nc.vector.tensor_scalar(rs[:, t:t + 1], rs[:, t:t + 1], 1.0 / (D * factor ** 2), EPS / factor ** 2,
                                        ALU.mult, ALU.add).then_inc(mean, 1)

            mean_of(0)
            v.wait_ge(gain_in, 16)
            for t in range(NT):
                if t + 1 < NT:
                    mean_of(t + 1)
                v.wait_ge(root, t + 1)
                nc.vector.reciprocal(rs[:, t:t + 1], rs[:, t:t + 1]).then_inc(inverse, 1)
                v.wait_ge(inverse, t + 1)
                if t > 1:
                    v.wait_ge(x_ok, t - 1)
                nc.vector.scalar_tensor_tensor(out=part[:, t % 2, :], in0=rows(t), scalar=rs[:, t:t + 1], in1=gain[:],
                                               op0=ALU.mult, op1=ALU.mult).then_inc(product_ok, 1)
                v.wait_ge(product_ok, t + 1)
                nc.vector.tensor_tensor(k.x[:, t, :], k.x[:, t, :], part[:, t % 2, :], ALU.add).then_inc(x_ok, 1)
            v.wait_ge(squares, 2 * NT)
            nc.vector.tensor_scalar(k.rs[:], k.rs[:], 1.0 / D, EPS, ALU.mult, ALU.add).then_inc(x_mean, 1)
            v.wait_ge(x_root, 1)
            nc.vector.reciprocal(k.rs[:], k.rs[:]).then_inc(inverse, 1)


def ffn(k, name, layer, which):
    nc, a = k.nc, k.a
    nw = a["norm_w_2"][layer]
    first = 4 * which
    w_gate, w_up, w_down = (a[w][layer, which] for w in ("ffn_w_gate_2", "ffn_w_up_2", "ffn_w_down_2"))
    with ExitStack() as st:
        raw = st.enter_context(nc.sbuf_tensor(f"{name}_raw", [P, 2, 2 * KD * P], F32))
        with ExitStack() as st2:
            hidden = split_sb(st2, nc, f"{name}_hidden", [P, FF_T, SEQ])
            u = split_sb(st2, nc, f"{name}_u", [P, KD, SEQ])
            ahead = [(raw[:, t, side * KD * P:(side + 1) * KD * P].rearrange("p (k n) -> p k n", k=KD), ffn_columns(w, t))
                     for t in range(2) for side, w in enumerate((w_gate, w_up))]
            normed_input(k, f"{name}_pre", k.norm_gain(layer, first), u, ahead)
            ffn_products(k, f"{name}_ffn", raw, u, w_gate, w_up, w_down, hidden)
        f_t = raw[:].rearrange("p j n -> p (j n)").rearrange("p (m n) -> p m n", n=SEQ)
        add_normed(k, f"{name}_post", None, f_t, nw[first + 1:first + 2], RES)


def soft_plus(k, name, x, out, n):
    nc = k.nc
    with Stage(nc, name) as s:
        na = s.sb("neg_abs", [P, n])
        negated, exped, logged, done = s.sem("negated"), s.sem("exped"), s.sem("logged"), s.sem("done")
        block = s.block()

        @block.vector
        def _(v):
            nc.vector.scalar_tensor_tensor(out=na[:], in0=x, scalar=-1.0, in1=x, op0=ALU.mult, op1=ALU.min).then_inc(negated, 1)
            v.wait_ge(logged, 1)
            nc.vector.scalar_tensor_tensor(out=out, in0=x, scalar=0.0, in1=na[:], op0=ALU.max, op1=ALU.add).then_inc(done, 1)

        @block.scalar
        def _(eng):
            eng.wait_ge(negated, 1)
            nc.scalar.activation(na[:], na[:], ACT.Exp).then_inc(exped, 1)
            eng.wait_ge(exped, 1)
            nc.scalar.activation(na[:], na[:], ACT.Ln, bias=1.0).then_inc(logged, 1)



WIN_H, WIN_D = 8, 64
DELTA_H, DELTA_D = 4, 128


def window_attention(k, qk_t, vals, out_t):
    nc = k.nc
    scale = WIN_D ** -0.5
    units = [(h, t) for h in range(WIN_H) for t in range(NT)]
    U = len(units)
    windows = k.c("windows")
    with Stage(nc, "windows") as s:
        sc, p, pt = s.sb("scores", [P, 3, SEQ]), s.sb("p", [P, 2, SEQ]), s.sb("p_t", [P, 2, SEQ])
        mx, den = s.sb("mx", [P, U]), s.sb("den", [P, U])
        score, masked, biased, soft = s.sem("score"), s.sem("masked"), s.sem("bias"), s.sem("soft")
        inverse, scaled, turned, pt_in = s.sem("inverse"), s.sem("scaled"), s.sem("turned"), s.sem("pt_in")
        pv, copied = s.sem("pv"), s.sem("copied")
        score_banks = (0, 1, 6)
        block = s.block()

        @block.tensor
        def _(pe):
            def scores(u):
                h, t = units[u]
                rows = slice((h % 2) * WIN_D, (h % 2 + 1) * WIN_D)
                if u >= 3:
                    pe.wait_ge(masked, u - 2)
                nc.tensor.matmul(k.ps[:, score_banks[u % 3], 0:(t + 1) * P], qk_t[rows, h // 2, t * P:(t + 1) * P],
                                 qk_t[rows, 4 + h // 2, 0:(t + 1) * P], start=True, stop=True).then_inc(score, 1)

            def values(u):
                h, t = units[u]
                pe.wait_ge(pt_in, u + 1)
                if u >= 2:
                    pe.wait_ge(copied, u - 1)
                rows = slice((h % 2) * WIN_D, (h % 2 + 1) * WIN_D)
                for q in range(t + 1):
                    last = nc.tensor.matmul(k.ps[rows, 4 + u % 2, 0:P], vals[:, q, h * WIN_D:(h + 1) * WIN_D],
                                            pt[:, u % 2, q * P:(q + 1) * P], start=q == 0, stop=q == t)
                last.then_inc(pv, 1)

            for u in range(3):
                scores(u)
            for u, (h, t) in enumerate(units):
                if u + 3 < U:
                    scores(u + 3)
                pe.wait_ge(scaled, u + 1)
                if u >= 2:
                    pe.wait_ge(pt_in, u - 1)
                for q in range(t + 1):
                    last = nc.tensor.transpose(k.ps[:, 2 + u % 2, q * P:(q + 1) * P], p[:, u % 2, q * P:(q + 1) * P], k.c("ident"))
                last.then_inc(turned, 1)
                if u:
                    values(u - 1)
            values(U - 1)

        @block.vector
        def _(v):
            def width(u):
                return (units[u][1] + 1) * P

            def mask(u):
                w = width(u)
                v.wait_ge(score, u + 1)
                if u >= 3:
                    v.wait_ge(soft, u - 2)
                nc.vector.scalar_tensor_tensor(out=sc[:, u % 3, 0:w], in0=k.ps[:, score_banks[u % 3], 0:w], scalar=scale,
                                               in1=windows[:, SEQ - w:SEQ], op0=ALU.mult, op1=ALU.add).then_inc(masked, 1)

            def bias(u):
                v.wait_ge(masked, u + 1)
                nc.vector.tensor_reduce(mx[:, u:u + 1], sc[:, u % 3, 0:width(u)], AX.X, ALU.max, negate=True).then_inc(biased, 1)

            for u in range(2):
                mask(u)
                bias(u)
            for u in range(U):
                w = width(u)
                if u + 2 < U:
                    mask(u + 2)
                v.wait_ge(soft, u + 1)
                nc.vector.reciprocal(den[:, u:u + 1], den[:, u:u + 1]).then_inc(inverse, 1)
                if u + 2 < U:
                    bias(u + 2)
                v.wait_ge(inverse, u + 1)
                nc.vector.tensor_scalar(p[:, u % 2, 0:w], p[:, u % 2, 0:w], den[:, u:u + 1], None, ALU.mult).then_inc(scaled, 1)

        @block.scalar
        def _(eng):
            def copy_out(u):
                h, t = units[u]
                rows = slice((h % 2) * WIN_D, (h % 2 + 1) * WIN_D)
                eng.wait_ge(pv, u + 1)
                nc.scalar.activation(out_t[rows, h // 2, t * P:(t + 1) * P], k.ps[rows, 4 + u % 2, 0:P], ACT.Copy).then_inc(copied, 1)

            for u in range(U + 1):
                if u < U:
                    w = (units[u][1] + 1) * P
                    eng.wait_ge(biased, u + 1)
                    if u >= 2:
                        eng.wait_ge(turned, u - 1)
                    nc.scalar.activation(p[:, u % 2, 0:w], sc[:, u % 3, 0:w], ACT.Exp, bias=mx[:, u:u + 1],
                                         accum_out=den[:, u:u + 1]).then_inc(soft, 1)
                if u:
                    c = u - 1
                    w = (units[c][1] + 1) * P
                    eng.wait_ge(turned, c + 1)
                    if c >= 2:
                        eng.wait_ge(pv, c - 1)
                    nc.scalar.activation(pt[:, c % 2, 0:w], k.ps[:, 2 + c % 2, 0:w], ACT.Copy).then_inc(pt_in, 1)
                    if c:
                        copy_out(c - 1)
            copy_out(U - 1)


def unit_columns(k, x_t, scales, eps=EPS):
    nc = k.nc
    n = len(scales)
    with Stage(nc, "unit") as s:
        sq, r = s.sb("sq", [P, 2, SEQ]), s.sb("r", [P, 2, SEQ])
        squared, summed, chain, root = s.sem("squared"), s.sem("summed"), s.sem("chain"), s.sem("root")
        block = s.block()

        @block.tensor
        def _(pe):
            for i in range(n):
                pe.wait_ge(squared, i + 1)
                if i >= 2:
                    pe.wait_ge(chain, 3 * (i - 2) + 1)
                nc.tensor.matmul(k.ps[:, i % 2, :], k.c("ones"), sq[:, i % 2, :], start=True, stop=True).then_inc(summed, 1)

        @block.scalar
        def _(eng):
            for i in range(n):
                if i >= 2:
                    eng.wait_ge(summed, i - 1)
                nc.scalar.activation(sq[:, i % 2, :], x_t[:, i, :], ACT.Square).then_inc(squared, 1)
                if i:
                    eng.wait_ge(chain, 3 * (i - 1) + 1)
                    nc.scalar.activation(r[:, (i - 1) % 2, :], r[:, (i - 1) % 2, :], ACT.Sqrt).then_inc(root, 1)
            eng.wait_ge(chain, 3 * (n - 1) + 1)
            nc.scalar.activation(r[:, (n - 1) % 2, :], r[:, (n - 1) % 2, :], ACT.Sqrt).then_inc(root, 1)

        @block.vector
        def _(v):
            link = in_order(v, chain)
            for i in range(n):
                v.wait_ge(summed, i + 1)
                link(nc.vector.tensor_scalar(r[:, i % 2, :], k.ps[:, i % 2, :], eps, None, ALU.add))
                v.wait_ge(root, i + 1)
                link(nc.vector.reciprocal(r[:, i % 2, :], r[:, i % 2, :]))
                link(nc.vector.scalar_tensor_tensor(out=x_t[:, i, :], in0=x_t[:, i, :], scalar=scales[i], in1=r[:, i % 2, :],
                                                    op0=ALU.mult, op1=ALU.mult))


def delta_gates(k, name, g, n, cum, last, exps, rest, ends):
    nc = k.nc
    with Stage(nc, name) as s:
        mm, chain, done = s.sem("mm"), s.sem("chain"), s.sem("done")
        sub = s.sem("sub")
        block = s.block()

        @block.tensor
        def _(pe):
            nc.tensor.matmul(k.ps[:, 0, 0:n], k.c("tri_fwd"), g, start=True, stop=True)
            nc.tensor.matmul(k.ps[:, 1, 0:n], k.c("same_chunk"), g, start=True, stop=True)
            for half in range(2):
                pick = k.c("same_chunk")[:, half * CHUNK:half * CHUNK + 1].to_broadcast([P, P])
                m = nc.tensor.matmul(k.ps[:, 2 + half, 0:n], pick, g, start=True, stop=True)
            m.then_inc(mm, 1)

        @block.vector
        def _(v):
            link = in_order(v, chain)
            v.wait_ge(mm, 1)
            link(nc.vector.tensor_copy(cum, k.ps[:, 0, 0:n]))
            link(nc.vector.tensor_copy(last, k.ps[:, 1, 0:n]))
            nc.vector.tensor_tensor(rest, last, cum, ALU.subtract).then_inc(sub, 1)

        @block.scalar
        def _(eng):
            eng.wait_ge(chain, 1)
            nc.scalar.activation(exps, cum, ACT.Exp).then_inc(done, 1)
            nc.scalar.activation(ends, k.ps[:, 2:4, 0:n], ACT.Exp).then_inc(done, 1)
            eng.wait_ge(sub, 1)
            nc.scalar.activation(rest, rest, ACT.Exp).then_inc(done, 1)


def delta_pairs(k, q_t, k_t, g, beta, cum, a_t, qk_t, q_dec):
    nc = k.nc
    H, W = DELTA_H, DELTA_H * P
    with Stage(nc, "delta_pairs") as s:
        dec, strict, eg = s.sb("decay", [P, 2, W]), s.sb("strict", [P, 2, W]), s.sb("exp_cum", [P, 2, W])
        mm, shifted, dec_ok, done = s.sem("mm"), s.sem("shifted"), s.sem("decay_ok"), s.sem("done")
        chain = s.sem("chain")
        block = s.block()

        @block.tensor
        def _(pe):
            for t in range(NT):
                b = 4 * (t % 2)
                if t >= 2:
                    pe.wait_ge(done, t - 1)
                cols = slice(t * P, (t + 1) * P)
                for h in range(H):
                    at = slice(h * P, (h + 1) * P)
                    nc.tensor.matmul(k.ps[:, b, at], g[:, t, h:h + 1].to_broadcast([P, P]), k.c("tri_fwd"), start=True, stop=True)
                    nc.tensor.matmul(k.ps[:, b + 1, at], beta[:, t, h:h + 1].to_broadcast([P, P]), k.c("ident"), start=True, stop=True)
                    nc.tensor.matmul(k.ps[:, b + 2, at], k_t[:, h, cols], k_t[:, h, cols], start=True, stop=True)
                    last = nc.tensor.matmul(k.ps[:, b + 3, at], k_t[:, h, cols], q_t[:, h, cols], start=True, stop=True)
                last.then_inc(mm, 1)

        @block.scalar
        def _(eng):
            for t in range(NT):
                eng.wait_ge(shifted, t + 1)
                nc.scalar.activation(eg[:, t % 2, :], k.ps[:, 4 * (t % 2), :], ACT.Exp).then_inc(dec_ok, 1)
                nc.scalar.activation(dec[:, t % 2, :], dec[:, t % 2, :], ACT.Exp).then_inc(dec_ok, 1)

        @block.vector
        def _(v):
            link = in_order(v, chain)
            heads = lambda x: x.rearrange("p (h n) -> p h n", h=H)
            for t in range(NT):
                b, j = 4 * (t % 2), t % 2
                v.wait_ge(mm, t + 1)
                for h in range(H):
                    at = slice(h * P, (h + 1) * P)
                    i = nc.vector.scalar_tensor_tensor(out=dec[:, j, at], in0=k.ps[:, b, at], scalar=cum[:, t, h:h + 1],
                                                       in1=k.c("add_incl"), op0=ALU.subtract, op1=ALU.add)
                    link(i) if h < H - 1 else i.then_inc(shifted, 1)
                v.wait_ge(dec_ok, 2 * t + 2)
                link(nc.vector.tensor_tensor(heads(strict[:, j, :]), heads(dec[:, j, :]),
                                             k.c("strict").unsqueeze(1).to_broadcast([P, H, P]), ALU.mult))
                link(nc.vector.tensor_tensor(strict[:, j, :], strict[:, j, :], k.ps[:, b + 1, :], ALU.mult))
                link(nc.vector.tensor_tensor(a_t[:, t, :], strict[:, j, :], k.ps[:, b + 2, :], ALU.mult))
                link(nc.vector.tensor_tensor(q_dec[:, :, t * P:(t + 1) * P], q_t[:, 0:H, t * P:(t + 1) * P], heads(eg[:, j, :]), ALU.mult))
                nc.vector.tensor_tensor(qk_t[:, t, :], dec[:, j, :], k.ps[:, b + 3, :], ALU.mult).then_inc(done, 1)


def delta_inverse(k, a_t, x, z):
    nc = k.nc
    W = DELTA_H * P
    H = DELTA_H
    heads = lambda v: v.rearrange("p (h n) -> p h n", h=H)
    with Stage(nc, "delta_inverse") as s:
        part, prod = s.sb("part", [P, 3, W]), s.sb("prod", [P, 2, W])
        parted, mm1, prod_ok, mm2, done = (s.sem(n) for n in ("parted", "product_mm", "product_ok", "update_mm", "done"))
        init = s.sem("init")
        chain = s.sem("chain")
        block = s.block()
        units = [(level, t) for level in range(1, 7) for t in range(NT)]

        @block.vector
        def _(v):
            link = in_order(v, init)
            for t in range(NT):
                for m in (x, z):
                    link(nc.vector.tensor_copy(heads(m[:, t, :]), k.c("ident").unsqueeze(1).to_broadcast([P, H, P])))

            def cut(u):
                level, t = units[u]
                if u >= 3:
                    v.wait_ge(mm1, u - 2)
                nc.vector.tensor_tensor(heads(part[:, u % 3, :]), heads(a_t[:, t, :]),
                                        k.c(f"merge{level}").unsqueeze(1).to_broadcast([P, H, P]), ALU.mult).then_inc(parted, 1)

            cut(0)
            cut(1)
            for u, (level, t) in enumerate(units):
                if u + 2 < len(units):
                    cut(u + 2)
                b = 4 * (u % 2)
                v.wait_ge(mm2, u + 1)
                nc.vector.tensor_tensor(x[:, t, :], x[:, t, :], k.ps[:, b + 1, :], ALU.subtract).then_inc(done, 1)
                nc.vector.tensor_tensor(z[:, t, :], z[:, t, :], k.ps[:, b + 2, :], ALU.subtract).then_inc(done, 1)

        @block.scalar
        def _(eng):
            for u in range(len(units)):
                eng.wait_ge(mm1, u + 1)
                if u >= 2:
                    eng.wait_ge(mm2, u - 1)
                nc.scalar.activation(prod[:, u % 2, :], k.ps[:, 4 * (u % 2), :], ACT.Copy).then_inc(prod_ok, 1)

        @block.tensor
        def _(pe):
            pe.wait_ge(init, 2 * NT)

            def product(u):
                level, t = units[u]
                pe.wait_ge(parted, u + 1)
                if level > 1:
                    pe.wait_ge(done, 2 * (u - NT) + 2)
                if u >= 2:
                    pe.wait_ge(prod_ok, u - 1)
                for h in range(H):
                    at = slice(h * P, (h + 1) * P)
                    last = nc.tensor.matmul(k.ps[:, 4 * (u % 2), at], part[:, u % 3, at], x[:, t, at], start=True, stop=True)
                last.then_inc(mm1, 1)

            product(0)
            for u, (level, t) in enumerate(units):
                if u + 1 < len(units):
                    product(u + 1)
                pe.wait_ge(prod_ok, u + 1)
                if u >= 2:
                    pe.wait_ge(done, 2 * (u - 2) + 2)
                for h in range(H):
                    at = slice(h * P, (h + 1) * P)
                    nc.tensor.matmul(k.ps[:, 4 * (u % 2) + 1, at], z[:, t, at], prod[:, u % 2, at], start=True, stop=True)
                    last = nc.tensor.matmul(k.ps[:, 4 * (u % 2) + 2, at], prod[:, u % 2, at], z[:, t, at], start=True, stop=True)
                last.then_inc(mm2, 1)


def delta_solve(k, z, v_beta, k_beta, u, w_t):
    nc = k.nc
    with Stage(nc, "delta_solve") as s:
        mm, u_ok, w_ok = s.sem("mm"), s.sem("u_ok"), s.sem("w_ok")
        block = s.block()

        @block.tensor
        def _(pe):
            for t in range(NT):
                for h in range(DELTA_H):
                    at = slice(h * P, (h + 1) * P)
                    nc.tensor.matmul(k.ps[:, t, at], z[:, t, at], v_beta[:, t, at], start=True, stop=True)
                    last = nc.tensor.matmul(k.ps[:, 4 + t, at], k_beta[:, t, at], z[:, t, at], start=True, stop=True)
                last.then_inc(mm, 1)

        @block.vector
        def _(v):
            for t in range(NT):
                v.wait_ge(mm, t + 1)
                nc.vector.tensor_copy(u[:, t, :], k.ps[:, t, :]).then_inc(u_ok, 1)

        @block.scalar
        def _(eng):
            for t in range(NT):
                eng.wait_ge(mm, t + 1)
                nc.scalar.activation(w_t[:, :, t * P:(t + 1) * P], k.ps[:, 4 + t, :].rearrange("p (h n) -> p h n", h=DELTA_H),
                                     ACT.Copy).then_inc(w_ok, 1)


def delta_scan(k, u, w_t, q_dec, qk_t, k_dec, ends, out):
    nc = k.nc
    H, W = DELTA_H, DELTA_H * P
    chunks = SEQ // CHUNK
    heads = lambda x: x.rearrange("p (h n) -> p h n", h=H)
    with Stage(nc, "delta_scan") as s:
        state, faded = s.sb("state", [P, 2, W]), s.sb("faded", [P, W])
        vn = s.sb("v_new", [P, 2, W])
        w_mm, vn_ok, o_mm, s_mm, s_ok, f_ok, o_ok = (s.sem(n) for n in
                                                     ("w_mm", "v_new_ok", "o_mm", "s_mm", "state_ok", "faded_ok", "out_ok"))
        block = s.block()

        @block.tensor
        def _(pe):
            for c in range(chunks):
                t, half = divmod(c, 2)
                rows = slice(half * CHUNK, (half + 1) * CHUNK)
                cols = slice(c * CHUNK, (c + 1) * CHUNK)
                pe.wait_ge(s_ok, c + 1)
                for h in range(H):
                    at = slice(h * P, (h + 1) * P)
                    last = nc.tensor.matmul(k.ps[rows, c % 2, at], w_t[:, h, cols], state[:, c % 2, at], start=True, stop=True)
                last.then_inc(w_mm, 1)
                if c >= 2:
                    pe.wait_ge(o_ok, c - 1)
                for h in range(H):
                    at = slice(h * P, (h + 1) * P)
                    nc.tensor.matmul(k.ps[rows, 2 + c % 2, at], q_dec[:, h, cols], state[:, c % 2, at],
                                     start=h == 0, stop=False, skip_group_check=True)
                pe.wait_ge(vn_ok, c + 1)
                for h in range(H):
                    at = slice(h * P, (h + 1) * P)
                    last = nc.tensor.matmul(k.ps[:, 4 + c % 2, at], k_dec[rows, t, at], vn[rows, c % 2, at], start=True, stop=True)
                last.then_inc(s_mm, 1)
                for h in range(H):
                    at = slice(h * P, (h + 1) * P)
                    last = nc.tensor.matmul(k.ps[rows, 2 + c % 2, at], qk_t[rows, t, h * P + half * CHUNK:h * P + (half + 1) * CHUNK],
                                            vn[rows, c % 2, at], start=False, stop=True, skip_group_check=True)
                last.then_inc(o_mm, 1)

        @block.vector
        def _(v):
            nc.vector.memset(state[:, 0, :], 0.0).then_inc(s_ok, 1)
            for c in range(chunks):
                t, half = divmod(c, 2)
                rows = slice(half * CHUNK, (half + 1) * CHUNK)
                v.wait_ge(s_ok, c + 1)
                nc.vector.tensor_tensor(heads(faded[:]), heads(state[:, c % 2, :]),
                                        ends[:, half, t * H:(t + 1) * H].unsqueeze(2).to_broadcast([P, H, P]), ALU.mult).then_inc(f_ok, 1)
                v.wait_ge(w_mm, c + 1)
                if c >= 2:
                    v.wait_ge(o_mm, c - 1)
                nc.vector.tensor_tensor(vn[rows, c % 2, :], u[rows, t, :], k.ps[rows, c % 2, :], ALU.subtract).then_inc(vn_ok, 1)
                v.wait_ge(s_mm, c + 1)
                v.wait_ge(f_ok, c + 1)
                nc.vector.tensor_tensor(state[:, (c + 1) % 2, :], faded[:], k.ps[:, 4 + c % 2, :], ALU.add).then_inc(s_ok, 1)

        @block.scalar
        def _(eng):
            for c in range(chunks):
                t, half = divmod(c, 2)
                rows = slice(half * CHUNK, (half + 1) * CHUNK)
                eng.wait_ge(o_mm, c + 1)
                nc.scalar.activation(out[rows, t, :], k.ps[rows, 2 + c % 2, :], ACT.Copy).then_inc(o_ok, 1)


def vector_steps(k, name, steps):
    with Stage(k.nc, name) as s:
        chain = s.sem("chain")
        block = s.block()

        @block.vector
        def _(v):
            link = in_order(v, chain)
            for step in steps:
                link(step(k.nc.vector))


def exp_rows(k, name, x, func=ACT.Exp):
    with Stage(k.nc, name) as s:
        done = s.sem("done")
        block = s.block()

        @block.scalar
        def _(eng):
            k.nc.scalar.activation(x, x, func).then_inc(done, 1)


def even_layer(k):
    nc, a = k.nc, k.a
    w_in = a["even_w_in_2"][0]
    nw = a["norm_w_2"][0]
    H = DELTA_H
    with ExitStack() as st:
        def sb(stack, name, shape):
            return stack.enter_context(nc.sbuf_tensor(f"even_{name}", shape, F32))

        mix_t = split_sb(st, nc, "even_mix_t", [P, KD, SEQ])
        z = sb(st, "z", [P, NT, 512])
        qkv = sb(st, "qkv", [P, 12, SEQ])
        ba = sb(st, "beta_a", [P, NT, 2 * H])
        out_raw = sb(st, "w_out_chunk", [P, KD, CHUNK_COLS])
        cols = sb(st, "cols", [P, 48 + 1])
        with ExitStack() as s2:
            u_t = split_sb(s2, nc, "even_u_t", [P, KD, SEQ])
            raw = sb(s2, "w_in_chunk", [P, KD, CHUNK_COLS])
            normed_input(k, "even_pre", k.norm_gain(0, 2), u_t, first_chunk(raw, w_in))
            column_tables(k, "even_cols", [(a["even_conv_w_2"][0].rearrange("k (c p) -> (k c) p", p=P), cols[:, 0:48]),
                                           (a["even_head_norm_w_2"], cols[:, 48:49])])
            with ExitStack() as s3:
                qk_t, va = sb(s3, "qk_t", [P, 8, SEQ]), sb(s3, "va", [P, NT, 512])
                project(k, "even_qkvz", u_t, w_in, [
                    (0, 2 * 512, feature_units([(0, SEQ)]), by_features(qk_t)),
                    (2 * 512, 512, token_units(NT), by_tokens(va)),
                    (6 * 512, 512, token_units(NT), by_tokens(z)),
                    (3 * 512, 3 * 512, feature_units([(0, SEQ)]), by_features(qkv), Conv(cols[:, 0:48], None, 0, 12))], raw)
                heads = sb(s3, "window_heads", [P, 4, SEQ])
                window_attention(k, qk_t, va, heads)
                split_rows(k, "even_split_heads", heads[:], mix_t[:, 0:4, :])
            with ExitStack() as s3:
                w_ba, b_ba = sb(s3, "w_ba", [P, KD, P]), sb(s3, "b_ba", [2 * H, 1])
                vector_steps(k, "even_clear", [lambda v: v.memset(b_ba[:], 0.0), lambda v: v.memset(w_ba[:], 0.0)])
                load_all(k, "even_ba_in", [(w_ba[:, :, 0:2 * H], w_in.rearrange("(k p) n -> p k n", p=P)[:, :, 7 * 512:]),
                                           (b_ba[H:, :], a["even_dt_bias_2"][0].rearrange("(p o) -> p o", o=1))])
                narrow_projection(k, "even_ba", u_t, w_ba, b_ba[:, 0:1], 2 * H, ba[:])
        unit_columns(k, qkv, [DELTA_D ** -0.5] * H + [1.0] * H)
        n = NT * H
        beta, g = sb(st, "beta", [P, NT, H]), sb(st, "g", [P, NT, H])
        a_log = sb(st, "a_log", [P, H])
        sums = {x: sb(st, x, [P, NT, H]) for x in ("cum", "last", "exps", "rest")}
        flat = {x: y[:].rearrange("p t h -> p (t h)") for x, y in sums.items()}
        ends = sb(st, "ends", [P, 2, n])
        load_all(k, "even_alog_in", [(a_log[:], everywhere(a["even_a_log_2"]))])
        exp_rows(k, "even_alog", a_log[:])
        vector_steps(k, "even_split", [lambda v: v.tensor_copy(beta[:], ba[:, :, 0:H]), lambda v: v.tensor_copy(g[:], ba[:, :, H:])])
        gf = g[:].rearrange("p t h -> p (t h)")
        soft_plus(k, "even_softplus", gf, gf, n)
        exp_rows(k, "even_sigmoid", beta[:], ACT.Sigmoid)
        vector_steps(k, "even_decay", [lambda v: v.scalar_tensor_tensor(
            out=g[:], in0=g[:], scalar=-1.0, in1=a_log[:].unsqueeze(1).to_broadcast([P, NT, H]), op0=ALU.mult, op1=ALU.mult)])
        delta_gates(k, "even_sums", gf, n, flat["cum"], flat["last"], flat["exps"], flat["rest"], ends[:])
        with ExitStack() as s2:
            a_t, qk2 = sb(s2, "a_t", [P, NT, 512]), sb(s2, "qk2", [P, NT, 512])
            q_dec = sb(s2, "q_dec", [P, H, SEQ])
            w_t, u = sb(s2, "w_t", [P, H, SEQ]), sb(s2, "u", [P, NT, 512])
            k_tok, v_tok = sb(s2, "k_tok", [P, NT, 512]), sb(s2, "v_tok", [P, NT, 512])
            k_beta = sb(s2, "k_beta", [P, NT, 512])
            delta_pairs(k, qkv[:, 0:H], qkv[:, H:2 * H], g, beta, sums["cum"], a_t, qk2, q_dec)
            features_to_tokens(k, "even_ktok", [qkv[:, H + i, :] for i in range(H)], k_tok)
            features_to_tokens(k, "even_vtok", [qkv[:, 2 * H + i, :] for i in range(H)], v_tok)
            with ExitStack() as s3:
                x, zz = sb(s3, "inv", [P, NT, 512]), sb(s3, "inv_t", [P, NT, 512])
                delta_inverse(k, a_t, x, zz)
                wide = lambda y: y[:].rearrange("p t (h n) -> p (t h) n", h=H)
                per = lambda y: y[:].rearrange("p t h -> p (t h)").unsqueeze(2).to_broadcast([P, n, P])
                vector_steps(k, "even_scale", [
                    lambda v: v.tensor_tensor(wide(v_tok), wide(v_tok), per(beta), ALU.mult),
                    lambda v: v.tensor_tensor(sums["last"][:], beta[:], sums["exps"][:], ALU.mult),
                    lambda v: v.tensor_tensor(wide(k_beta), wide(k_tok), per(sums["last"]), ALU.mult),
                    lambda v: v.tensor_tensor(wide(k_tok), wide(k_tok), per(sums["rest"]), ALU.mult)])
                delta_solve(k, zz, v_tok, k_beta, u, w_t)
            o = sb(s2, "o", [P, NT, 512])
            delta_scan(k, u, w_t, q_dec, qk2, k_tok, ends, o)
            silu_rows(k, "even_silu_z", [z[:]])
            norm_heads(k, "even_heads", o[:].rearrange("p t (h n) -> p (t h) n", h=H), n, P, [(o[:], z[:])])
            turn(k, "even_turn_o", [([o[:, t, h * P:(h + 1) * P] for t in range(NT)], mix_t[:, 4 + h, :], cols[:, 48:49], None)
                                    for h in range(H)], NT, first_chunk(out_raw, a["even_w_out_2"][0]))
        m = sb(st, "m", [P, NT, D])
        project(k, "even_out", mix_t, a["even_w_out_2"][0], [(0, D, token_units(NT), by_tokens(m))], out_raw)
        add_normed(k, "even_post", m, None, nw[3:4])



SSD_IN = 2 * D
SSD_P, SSD_G, SSD_N = 64, 4, 128
SSD_H = SSD_IN // SSD_P
SSD_R = SSD_H // SSD_G


def ssd_scan(k, xdt, b_tok, bc_t, acc, cum, exps, rest, ends, xs, skip, z, squares):
    nc = k.nc
    R, W = SSD_R, SSD_R * SSD_P
    units = [(t, g) for t in range(NT) for g in range(SSD_G)]
    U = len(units)
    with Stage(nc, "ssd") as s:
        state = s.sb("state", [P, SSD_G, 2, W])
        seg, mix = s.sb("seg", [P, R, P]), s.sb("mix", [P, R, P])
        cb_mm, shifted, seg_ok, mixed = s.sem("cb_mm"), s.sem("shifted"), s.sem("seg_ok"), s.sem("mixed")
        upd_mm, diag_mm, off_mm, s_ok, y_ok = (s.sem(n) for n in ("update_mm", "diag_mm", "off_mm", "state_ok", "y_ok"))
        chain, faded_ok = s.sem("chain"), s.sem("faded_ok")
        faded = s.sb("faded", [P, 2, W])
        x_end, x_end_ok = s.sb("x_end", [P, 2, W]), s.sem("x_end_ok")
        junk = s.sb("junk", [P, 2, W])
        skip_ok, summed, silu_ok, gated, squared = (s.sem(n) for n in ("skip_ok", "summed", "silu_ok", "gated", "squared"))
        block = s.block()

        @block.tensor
        def _(pe):
            def decays(n):
                t, g = units[n]
                cols = slice(t * P, (t + 1) * P)
                if n:
                    pe.wait_ge(mixed, n)
                for r in range(R):
                    h = g * R + r
                    nc.tensor.matmul(k.ps[:, r // 4, (r % 4) * P:(r % 4 + 1) * P], acc[:, t, h:h + 1].to_broadcast([P, P]),
                                     k.c("tri_fwd"), start=True, stop=True)
                nc.tensor.matmul(k.ps[:, 2, 0:P], bc_t[:, g, cols], bc_t[:, SSD_G + g, cols], start=True, stop=True).then_inc(cb_mm, 1)

            decays(0)
            for n, (t, g) in enumerate(units):
                pe.wait_ge(s_ok, 2 * n + 1)
                pe.wait_ge(x_end_ok, n + 1)
                for half in range(2):
                    rows = slice(half * CHUNK, (half + 1) * CHUNK)
                    nc.tensor.matmul(k.ps[:, 4 + half, :], b_tok[rows, t, g * SSD_N:(g + 1) * SSD_N],
                                     x_end[rows, n % 2, :], start=True, stop=True).then_inc(upd_mm, 1)
                if n:
                    pe.wait_ge(y_ok, n)
                nc.tensor.matmul(k.ps[0:CHUNK, 3, :], bc_t[:, SSD_G + g, t * P:t * P + CHUNK], state[:, g, 0, :],
                                 start=True, stop=True)
                pe.wait_ge(mixed, n + 1)
                if n + 1 < U:
                    decays(n + 1)
                for r in range(R):
                    h = g * R + r
                    last = nc.tensor.matmul(k.ps[:, 6, r * SSD_P:(r + 1) * SSD_P], mix[:, r, :], xdt[:, t, h * SSD_P:(h + 1) * SSD_P],
                                            start=True, stop=True)
                last.then_inc(diag_mm, 1)
                pe.wait_ge(s_ok, 2 * n + 2)
                nc.tensor.matmul(k.ps[CHUNK:P, 3, :], bc_t[:, SSD_G + g, t * P + CHUNK:(t + 1) * P], state[:, g, 1, :],
                                 start=True, stop=True).then_inc(off_mm, 1)

        @block.gpsimd
        def _(pool):
            heads = lambda x: x.rearrange("p (r n) -> p r n", r=R)

            def fade(n, half):
                t, g = units[n]
                at = t * SSD_H + g * R
                pool.wait_ge(s_ok, 2 * n + half + 1)
                nc.gpsimd.tensor_tensor(heads(faded[:, half, :]), heads(state[:, g, half, :]),
                                        ends[:, half, at:at + R].unsqueeze(2).to_broadcast([P, R, SSD_P]),
                                        ALU.mult).then_inc(faded_ok, 1)

            def to_end(n):
                t, g = units[n]
                if n >= 2:
                    pool.wait_ge(upd_mm, 2 * (n - 2) + 2)
                nc.gpsimd.tensor_tensor(heads(x_end[:, n % 2, :]), heads(xdt[:, t, g * W:(g + 1) * W]),
                                        rest[:, t, g * R:(g + 1) * R].unsqueeze(2).to_broadcast([P, R, SSD_P]),
                                        ALU.mult).then_inc(x_end_ok, 1)

            def skipped(n):
                t, g = units[n]
                part = xs[:, t, g * W:(g + 1) * W]
                nc.gpsimd.tensor_tensor(heads(part), heads(part), skip[:, g * R:(g + 1) * R].unsqueeze(2).to_broadcast([P, R, SSD_P]),
                                        ALU.mult).then_inc(skip_ok, 1)

            def finish(n):
                t, g = units[n]
                at = slice(g * W, (g + 1) * W)
                pool.wait_ge(skip_ok, n + 1)
                pool.wait_ge(y_ok, n + 1)
                nc.gpsimd.tensor_tensor(xdt[:, t, at], xdt[:, t, at], xs[:, t, at], ALU.add).then_inc(summed, 1)
                pool.wait_ge(summed, n + 1)
                pool.wait_ge(silu_ok, n + 1)
                nc.gpsimd.tensor_tensor(xdt[:, t, at], xdt[:, t, at], z[:, t, at], ALU.mult).then_inc(gated, 1)

            to_end(0)
            for n in range(U):
                fade(n, 0)
                if n + 1 < U:
                    to_end(n + 1)
                fade(n, 1)
                skipped(n)
                if n:
                    finish(n - 1)
            finish(U - 1)

        @block.scalar
        def _(eng):
            def square(n):
                t, g = units[n]
                eng.wait_ge(gated, n + 1)
                if n >= 2:
                    eng.wait_ge(squared, n - 1)
                nc.scalar.activation(junk[:, n % 2, :], xdt[:, t, g * W:(g + 1) * W], ACT.Square,
                                     accum_out=squares[:, n:n + 1]).then_inc(squared, 1)

            for n, (t, g) in enumerate(units):
                eng.wait_ge(shifted, n + 1)
                nc.scalar.activation(seg[:], seg[:], ACT.Exp).then_inc(seg_ok, 1)
                part = z[:, t, g * W:(g + 1) * W]
                nc.scalar.activation(part, part, ACT.Silu).then_inc(silu_ok, 1)
                if n >= 2:
                    square(n - 2)
            square(U - 2)
            square(U - 1)

        @block.vector
        def _(v):
            link = in_order(v, chain)
            heads = lambda x: x.rearrange("p (r n) -> p r n", r=R)
            nc.vector.memset(state[:], 0.0).then_inc(s_ok, 1)

            def advance(n, half):
                g = units[n][1]
                v.wait_ge(faded_ok, 2 * n + half + 1)
                v.wait_ge(upd_mm, 2 * n + half + 1)
                nc.vector.tensor_tensor(state[:, g, 1 - half, :], faded[:, half, :], k.ps[:, 4 + half, :], ALU.add).then_inc(s_ok, 1)

            def prepare(n):
                t, g = units[n]
                v.wait_ge(cb_mm, n + 1)
                for r in range(R):
                    h = g * R + r
                    last = nc.vector.scalar_tensor_tensor(out=seg[:, r, :], in0=k.ps[:, r // 4, (r % 4) * P:(r % 4 + 1) * P],
                                                          scalar=cum[:, t, h:h + 1], in1=k.c("add_incl"), op0=ALU.subtract, op1=ALU.add)
                last.then_inc(shifted, 1)

            v.wait_ge(s_ok, 1)
            prepare(0)
            for n, (t, g) in enumerate(units):
                advance(n, 0)
                v.wait_ge(seg_ok, n + 1)
                if n:
                    v.wait_ge(diag_mm, n)
                nc.vector.tensor_tensor(mix[:], seg[:], k.ps[:, 2, 0:P].unsqueeze(1).to_broadcast([P, R, P]), ALU.mult).then_inc(mixed, 1)
                if n + 1 < U:
                    v.wait_ge(mixed, n + 1)
                    prepare(n + 1)
                v.wait_ge(s_ok, 2 * n + 2)
                v.wait_ge(diag_mm, n + 1)
                advance(n, 1)
                v.wait_ge(off_mm, n + 1)
                at = t * SSD_H + g * R
                out = xdt[:, t, g * W:(g + 1) * W]
                link(nc.vector.tensor_tensor(heads(out), heads(k.ps[:, 3, :]),
                                             exps[:, t, g * R:(g + 1) * R].unsqueeze(2).to_broadcast([P, R, SSD_P]), ALU.mult))
                nc.vector.tensor_tensor(out, out, k.ps[:, 6, :], ALU.add).then_inc(y_ok, 1)


def odd_layer(k):
    nc, a = k.nc, k.a
    w_in = a["odd_w_in_2"][0]
    nw = a["norm_w_2"][1]
    with ExitStack() as st:
        def sb(stack, name, shape):
            return stack.enter_context(nc.sbuf_tensor(f"odd_{name}", shape, F32))

        y = sb(st, "y", [P, NT, SSD_IN])
        xx = y[:].rearrange("p t (j n) -> p (t j) n", n=SEQ)
        group_ss = sb(st, "group_ss", [P, NT * SSD_G])
        with ExitStack() as s1:
            z = sb(s1, "z", [P, NT, SSD_IN])
            cols = sb(s1, "cols", [P, 24 * 4 + 24])
            dt = sb(s1, "dt", [P, NT, SSD_H])
            bc_t = sb(s1, "bc_t", [P, 8, SEQ])
            head = sb(s1, "head_rows", [P, 2, SSD_H])
            with ExitStack() as s2:
                u_t = split_sb(s2, nc, "odd_u_t", [P, KD, SEQ])
                raw = sb(s2, "w_in_chunk", [P, KD, CHUNK_COLS])
                normed_input(k, "odd_pre", k.norm_gain(1, 2), u_t, first_chunk(raw, w_in))
                column_tables(k, "odd_cols", [(a["odd_conv_w_2"][0].rearrange("k (c p) -> (k c) p", p=P), cols[:, 0:96]),
                                              (a["odd_conv_b_2"].rearrange("o (c p) -> (o c) p", p=P), cols[:, 96:120])])
                taps, shifts = cols[:, 0:96], cols[:, 96:120]
                whole = feature_units([(0, SEQ)])
                project(k, "odd_in", u_t, w_in, [
                    (0, SSD_IN, token_units(NT), by_tokens(z)),
                    (SSD_IN, SSD_IN, whole, by_features(xx), Conv(taps, shifts, 0, 24)),
                    (2 * SSD_IN, D, whole, by_features(bc_t), Conv(taps, shifts, 16, 24))], raw)
                with ExitStack() as s3:
                    w_dt, b_dt = sb(s3, "w_dt", [P, KD, P]), sb(s3, "b_dt", [SSD_H, 1])
                    vector_steps(k, "odd_clear", [lambda v: v.memset(w_dt[:], 0.0)])
                    load_all(k, "odd_dt_in", [(w_dt[:, :, 0:SSD_H], w_in.rearrange("(k p) n -> p k n", p=P)[:, :, SSD_IN + 3 * D:]),
                                              (b_dt[:], a["odd_dt_bias_2"][0].rearrange("(p o) -> p o", o=1)),
                                              (head[:, 0, :], everywhere(a["odd_a_log_2"])),
                                              (head[:, 1, :], everywhere(a["odd_d_skip_2"]))])
                    narrow_projection(k, "odd_dt", u_t, w_dt, b_dt[:, 0:1], SSD_H, dt[:])
            n = NT * SSD_H
            b_tok = sb(s1, "b_tok", [P, NT, 512])
            la = sb(s1, "log_decay", [P, NT, SSD_H])
            sums = {x: sb(s1, x, [P, NT, SSD_H]) for x in ("cum", "last", "exps", "rest")}
            ends = sb(s1, "ends", [P, 2, NT * SSD_H])
            features_to_tokens(k, "odd_btok", [bc_t[:, i, :] for i in range(4)], b_tok)
            exp_rows(k, "odd_alog", head[:, 0, :])
            dtf = dt[:].rearrange("p t h -> p (t h)")
            soft_plus(k, "odd_softplus", dtf, dtf, n)
            vector_steps(k, "odd_decay", [lambda v: v.scalar_tensor_tensor(
                out=la[:], in0=dt[:], scalar=-1.0, in1=head[:, 0, :].unsqueeze(1).to_broadcast([P, NT, SSD_H]), op0=ALU.mult, op1=ALU.mult)])
            flat = {x: y[:].rearrange("p t h -> p (t h)") for x, y in sums.items()}
            delta_gates(k, "odd_sums", la[:].rearrange("p t h -> p (t h)"), n, flat["cum"], flat["last"], flat["exps"], flat["rest"], ends[:])
            with ExitStack() as s2:
                xs = sb(s2, "xs", [P, NT, SSD_IN])
                features_to_tokens(k, "odd_xtok", [xx[:, i, :] for i in range(16)], xs)
                wide = lambda v: v[:].rearrange("p t (h n) -> p (t h) n", n=SSD_P)
                per = lambda v: v.rearrange("p t h -> p (t h)").unsqueeze(2).to_broadcast([P, n, SSD_P])
                vector_steps(k, "odd_xdt", [lambda v: v.tensor_tensor(wide(y), wide(xs), per(dt[:]), ALU.mult)])
                ssd_scan(k, y, b_tok, bc_t, la, sums["cum"], sums["exps"], sums["rest"], ends,
                         xs, head[:, 1, :], z, group_ss[:])
        groups = [y[:, t, g * 512:(g + 1) * 512] for t in range(NT) for g in range(4)]
        norm_rows(k, "odd_groups", [(v, v) for v in groups], 512, sums=group_ss)
        y_t = split_sb(st, nc, "odd_y_t", [P, 16, SEQ])
        raw = sb(st, "w_out_chunk", [P, 16, CHUNK_COLS])
        gains = sb(st, "out_gain", [P, 16])
        column_tables(k, "odd_gain", [(a["odd_out_norm_w_2"].rearrange("o (c p) -> (o c) p", p=P), gains[:])])
        turn(k, "odd_turn_y", [([y[:, t, i * P:(i + 1) * P] for t in range(NT)], y_t[:, i, :], gains[:, i:i + 1], None)
                               for i in range(16)], NT, first_chunk(raw, a["odd_w_out_2"][0]))
        m = y[:, :, 0:D]
        project(k, "odd_out", y_t, a["odd_w_out_2"][0], [(0, D, token_units(NT), by_tokens(m))], raw, k_tiles=16)
        add_normed(k, "odd_post", m, None, nw[3:4])


def second_block(k):
    column_tables(k, "norm_gains", [(k.a["norm_w_2"].rearrange("l r (k p) -> (l r k) p", p=P), k.gains[:])])
    ffn(k, "f0", 0, 0)
    even_layer(k)
    ffn(k, "f1", 0, 1)
    ffn(k, "f2", 1, 0)
    odd_layer(k)
    ffn(k, "f3", 1, 1)


def build_program(nc, args, out):
    with ExitStack() as es:
        k = Core(nc, args, es)
        mod_rows = k.scratch("mod_rows", [2, 6 * D])
        load_all(k, "start", [(k.table[:], args["const_table"]),
                              (k.x[:], args["x"][0].rearrange("(t p) d -> p t d", p=P))])
        modulation(k, mod_rows)
        first_mixer(k, es, mod_rows)
        first_experts(k, es, mod_rows)
        second_block(k)
        with Stage(nc, "finish") as s:
            stored = s.sem("stored")
            block = s.block()

            @block.sync
            def _(sp):
                sp.dma_start(out[0].rearrange("(t p) d -> p t d", p=P), k.x[:]).then_inc(stored, 16)
                sp.wait_ge(stored, 16)


def kernel(**inputs):
    import concourse.bacc as _bacc
    from concourse.bass_utils import run_bass_kernel_spmd as _run

    nc = _bacc.Bacc("TRN2", target_bir_lowering=False, num_devices=1)
    arrays, args = {}, {}
    for name, value in dict(inputs, const_table=CONST_DATA).items():
        a = np.ascontiguousarray(value)
        arrays[f"in_{name}"] = a
        args[name] = nc.dram_tensor(f"in_{name}", a.shape, mybir.dt.from_np(a.dtype), kind="ExternalInput").ap()
    out = nc.dram_tensor("out_0", (1, SEQ, D), F32, kind="ExternalOutput").ap()
    build_program(nc, args, out)
    r = _run(nc, [arrays], core_ids=[0])
    return r.results[0]["out_0"]
```
